# Optimizing a Trainium2 kernel written in Bass

```python
import jax, jax.numpy as jnp
from jax import lax
import numpy as np
import math
import jax
import jax.numpy as jnp

D_MODEL = 1024
BATCH = 1
SEQ = 512
DEPTH = 2

GRID_W = 64
CTX_LEN = 256
EPS = 1e-6
NEG_INF = -1e30

NA_HEADS = 8
NA_HEAD_DIM = 64
NA_WIDTH = NA_HEADS * NA_HEAD_DIM
NA_KH = 8
NA_KW = 16
SGU_GROUPS = 8
SGU_WIDTH = D_MODEL - NA_WIDTH
SGU_GROUP_DIM = SGU_WIDTH // SGU_GROUPS
SGU_CHUNK = 128
HYB_IN = 3 * NA_WIDTH + 2 * SGU_WIDTH

RET_HEADS = 8
RET_QK_DIM = D_MODEL // RET_HEADS
RET_V_DIM = 2 * RET_QK_DIM
RET_QK_WIDTH = RET_HEADS * RET_QK_DIM
RET_V_WIDTH = RET_HEADS * RET_V_DIM
RET_CHUNK = 128
RET_IN = 2 * RET_QK_WIDTH + 2 * RET_V_WIDTH
ROPE_BASE = 10000.0

D_FF = 2816
CONV_W = 3

N_EVEN = (DEPTH + 1) // 2
N_ODD = DEPTH // 2


def rmsnorm(x, g):
    xf = x.astype(jnp.float32)
    y = xf * lax.rsqrt(jnp.mean(xf * xf, axis=-1, keepdims=True) + EPS)
    return (y * g.astype(jnp.float32)).astype(x.dtype)

def modulate(x, shift, scale):
    return x * (1 + scale) + shift

def axial_rope(n_tokens, head_dim):
    t = jnp.arange(n_tokens)
    row = (t // GRID_W).astype(jnp.float32)
    col = (t % GRID_W).astype(jnp.float32)
    n_freq = head_dim // 4
    inv = ROPE_BASE ** (-jnp.arange(n_freq, dtype=jnp.float32) / n_freq)
    ang = jnp.concatenate([row[:, None] * inv, col[:, None] * inv], axis=-1)
    return jnp.cos(ang), jnp.sin(ang)

def apply_rope(x, cos, sin):
    x1, x2 = jnp.split(x, 2, axis=-1)
    c = cos[None, :, None, :]
    s = sin[None, :, None, :]
    return jnp.concatenate([x1 * c - x2 * s, x1 * s + x2 * c], axis=-1).astype(x.dtype)

def neighbourhood_attention(q, k, v, k_ctx, v_ctx, rpb):
    B, T, H, dh = q.shape
    rows = T // GRID_W
    kh = min(NA_KH, rows)
    kw = NA_KW
    scale = dh ** -0.5
    qg = q.reshape(B, rows, GRID_W, H, dh)
    kg = k.reshape(B, rows, GRID_W, H, dh)
    vg = v.reshape(B, rows, GRID_W, H, dh)
    r = jnp.arange(rows)
    r0 = jnp.clip(r - kh // 2, 0, rows - kh)
    key_rows = r0[:, None] + jnp.arange(kh)[None, :]
    k_blk = kg[:, key_rows].reshape(B, rows, kh * GRID_W, H, dh)
    v_blk = vg[:, key_rows].reshape(B, rows, kh * GRID_W, H, dh)
    s_nb = jnp.einsum('brqhd,brkhd->bhrqk', qg, k_blk,
                      preferred_element_type=jnp.float32) * scale
    cidx = jnp.arange(GRID_W)
    c0 = jnp.clip(cidx - kw // 2, 0, GRID_W - kw)
    in_win = (cidx[None, :] >= c0[:, None]) & (cidx[None, :] < c0[:, None] + kw)
    mask = jnp.broadcast_to(in_win[:, None, :], (GRID_W, kh, GRID_W)).reshape(GRID_W, kh * GRID_W)
    dr = key_rows - r[:, None] + (NA_KH - 1)
    dc = jnp.clip(cidx[None, :] - cidx[:, None], -(kw - 1), kw - 1) + (kw - 1)
    bias = rpb[:, dr[:, None, :, None], dc[None, :, None, :]]
    bias = bias.reshape(H, rows, GRID_W, kh * GRID_W).astype(jnp.float32)
    s_nb = jnp.where(mask, s_nb + bias[None], NEG_INF)
    s_cx = jnp.einsum('brqhd,bchd->bhrqc', qg, k_ctx,
                      preferred_element_type=jnp.float32) * scale
    p = jax.nn.softmax(jnp.concatenate([s_nb, s_cx], axis=-1), axis=-1)
    n_nb = kh * GRID_W
    p_nb = p[..., :n_nb].astype(v.dtype)
    p_cx = p[..., n_nb:].astype(v.dtype)
    o = (jnp.einsum('bhrqk,brkhd->brqhd', p_nb, v_blk)
         + jnp.einsum('bhrqc,bchd->brqhd', p_cx, v_ctx))
    return o.reshape(B, T, H * dh).astype(q.dtype)

def context_attention(q, k, v):
    B, L, H, dh = q.shape
    s = jnp.einsum('bqhd,bkhd->bhqk', q, k, preferred_element_type=jnp.float32) * dh ** -0.5
    p = jax.nn.softmax(s, axis=-1).astype(v.dtype)
    return jnp.einsum('bhqk,bkhd->bqhd', p, v).reshape(B, L, H * dh).astype(q.dtype)

def spatial_gating(u, v, w_s, b_s):
    B, N, _ = v.shape
    vf = v.astype(jnp.float32)
    mu = jnp.mean(vf, axis=-1, keepdims=True)
    var = jnp.mean(jnp.square(vf - mu), axis=-1, keepdims=True)
    vn = ((vf - mu) * lax.rsqrt(var + EPS)).astype(v.dtype)
    vc = vn.reshape(B, N // SGU_CHUNK, SGU_CHUNK, SGU_GROUPS, SGU_GROUP_DIM)
    mixed = jnp.einsum('gpq,bnqgc->bnpgc', w_s, vc) + b_s.T[None, None, :, :, None]
    return u * mixed.reshape(B, N, SGU_WIDTH)

def hybrid_na_sgu(h_ctx, h_lat, w_in, rpb, w_s, b_s, w_out, ctx_out):
    heads = lambda a: a.reshape(a.shape[0], a.shape[1], NA_HEADS, NA_HEAD_DIM)
    splits = [NA_WIDTH, 2 * NA_WIDTH, 3 * NA_WIDTH, 3 * NA_WIDTH + SGU_WIDTH]
    q, k, v, u, g = jnp.split(h_lat @ w_in, splits, axis=-1)
    if ctx_out:
        qc, kc, vc, uc, gc = jnp.split(h_ctx @ w_in, splits, axis=-1)
    else:
        kc, vc = jnp.split(h_ctx @ w_in[:, NA_WIDTH:3 * NA_WIDTH], 2, axis=-1)
    a_lat = neighbourhood_attention(heads(q), heads(k), heads(v), heads(kc), heads(vc), rpb)
    s_lat = spatial_gating(jax.nn.gelu(u), jax.nn.gelu(g), w_s, b_s)
    y_lat = jnp.concatenate([a_lat, s_lat], axis=-1) @ w_out
    y_ctx = None
    if ctx_out:
        a_ctx = context_attention(heads(qc), heads(kc), heads(vc))
        s_ctx = spatial_gating(jax.nn.gelu(uc), jax.nn.gelu(gc), w_s, b_s)
        y_ctx = jnp.concatenate([a_ctx, s_ctx], axis=-1) @ w_out
    return y_ctx, y_lat

def retention_chunked(q, k, v, lg, state0):
    B, N, H, dk = q.shape
    dv = v.shape[-1]
    C = RET_CHUNK
    n = N // C
    to_chunks = lambda a: a.reshape(B, n, C, H, a.shape[-1]).transpose(1, 0, 3, 2, 4)
    pos = jnp.arange(C, dtype=jnp.float32)
    diff = pos[:, None] - pos[None, :]
    lower = diff >= 0
    decay_intra = jnp.where(lower[None], jnp.exp(lg[:, None, None] * jnp.where(lower, diff, 0.0)[None]), 0.0)
    decay_q = jnp.exp(lg[:, None] * (pos + 1.0))[None, :, :, None]
    decay_k = jnp.exp(lg[:, None] * (C - 1.0 - pos))[None, :, :, None]
    decay_chunk = jnp.exp(lg * C)[None, :, None, None]

    def step(S, blk):
        qb, kb, vb = blk
        qf = qb.astype(jnp.float32)
        kf = kb.astype(jnp.float32)
        vf = vb.astype(jnp.float32)
        s = jnp.einsum('bhqd,bhkd->bhqk', qf, kf) * decay_intra
        o = jnp.einsum('bhqk,bhkv->bhqv', s, vf) + jnp.einsum('bhqd,bhdv->bhqv', qf * decay_q, S)
        S = S * decay_chunk + jnp.einsum('bhkd,bhkv->bhdv', kf * decay_k, vf)
        return S, o

    _, o = lax.scan(step, state0, (to_chunks(q), to_chunks(k), to_chunks(v)))
    return o.transpose(1, 0, 3, 2, 4).reshape(B, N, H, dv)

def retention_final_state(k, v, lg):
    L = k.shape[1]
    w = jnp.exp(lg[None, :] * (L - 1.0 - jnp.arange(L, dtype=jnp.float32))[:, None])
    return jnp.einsum('blhd,blhv->bhdv', k.astype(jnp.float32) * w[None, :, :, None], v.astype(jnp.float32))

def retention_output(o, g, gn_g, w_out):
    B, N = o.shape[0], o.shape[1]
    mu = jnp.mean(o, axis=-1, keepdims=True)
    var = jnp.mean(jnp.square(o - mu), axis=-1, keepdims=True)
    on = ((o - mu) * lax.rsqrt(var + EPS)).reshape(B, N, RET_V_WIDTH) * gn_g.astype(jnp.float32)
    return (jax.nn.silu(g) * on.astype(g.dtype)) @ w_out

def retention_mixer(h_ctx, h_lat, w_in, log_decay, gn_g, w_out, ctx_out):
    B, T, _ = h_lat.shape
    L = h_ctx.shape[1]
    H, dk, dv = RET_HEADS, RET_QK_DIM, RET_V_DIM
    splits = [RET_QK_WIDTH, 2 * RET_QK_WIDTH, 2 * RET_QK_WIDTH + RET_V_WIDTH]
    q, k, v, g = jnp.split(h_lat @ w_in, splits, axis=-1)
    cos, sin = axial_rope(T, dk)
    q = apply_rope(q.reshape(B, T, H, dk), cos, sin)
    k = apply_rope(k.reshape(B, T, H, dk) * dk ** -0.5, cos, sin)
    v = v.reshape(B, T, H, dv)
    if ctx_out:
        qc, kc, vc, gc = jnp.split(h_ctx @ w_in, splits, axis=-1)
        qc = qc.reshape(B, L, H, dk)
    else:
        kc, vc = jnp.split(h_ctx @ w_in[:, RET_QK_WIDTH:2 * RET_QK_WIDTH + RET_V_WIDTH], [RET_QK_WIDTH], axis=-1)
    kc = kc.reshape(B, L, H, dk) * dk ** -0.5
    vc = vc.reshape(B, L, H, dv)
    outs_lat = []
    outs_ctx = []
    for d in range(2):
        lg = log_decay[d].astype(jnp.float32)
        rev = (lambda a: a[:, ::-1]) if d == 1 else (lambda a: a)
        s_ctx = retention_final_state(rev(kc), rev(vc), lg)
        outs_lat.append(rev(retention_chunked(rev(q), rev(k), rev(v), lg, s_ctx)))
        if ctx_out:
            outs_ctx.append(rev(retention_chunked(rev(qc), rev(kc), rev(vc), lg, jnp.zeros_like(s_ctx))))
    y_lat = retention_output(outs_lat[0] + outs_lat[1], g, gn_g, w_out)
    y_ctx = None
    if ctx_out:
        y_ctx = retention_output(outs_ctx[0] + outs_ctx[1], gc, gn_g, w_out)
    return y_ctx, y_lat

def dwconv3(x, w, b):
    xp = jnp.pad(x, ((0, 0), (1, 1), (0, 0)))
    return xp[:, :-2] * w[0] + xp[:, 1:-1] * w[1] + xp[:, 2:] * w[2] + b

def conv_ffn(h, w_in, conv_w, conv_b, w_out):
    a = dwconv3(h @ w_in, conv_w, conv_b)
    gate, up = jnp.split(a, 2, axis=-1)
    return (jax.nn.silu(gate) * up) @ w_out

def first_inputs(seed: int = 0) -> dict:
    key = jax.random.key(seed)
    ks = jax.random.split(key, 20)
    nrm = lambda k, shape, s: jax.random.normal(k, shape, jnp.float32) * s
    base_decay = np.log1p(-2.0 ** (-5.0 - np.arange(RET_HEADS))).astype(np.float32)
    return {
        "x": nrm(ks[0], (BATCH, SEQ, D_MODEL), 1.0),
        "c": nrm(ks[1], (BATCH, D_MODEL), 1.0),
        "ctx": nrm(ks[2], (BATCH, CTX_LEN, D_MODEL), 1.0),
        "c_ctx": nrm(ks[3], (D_MODEL,), 1.0),
        "ada_w": nrm(ks[4], (DEPTH, D_MODEL, 6 * D_MODEL), 0.5 * D_MODEL ** -0.5),
        "ada_b": nrm(ks[5], (DEPTH, 6 * D_MODEL), 0.02),
        "norm_g": 1.0 + nrm(ks[6], (DEPTH, 4, D_MODEL), 0.1),
        "hyb_w_in": nrm(ks[7], (N_EVEN, D_MODEL, HYB_IN), D_MODEL ** -0.5),
        "na_rpb": nrm(ks[8], (N_EVEN, NA_HEADS, 2 * NA_KH - 1, 2 * NA_KW - 1), 0.1),
        "sgu_w": nrm(ks[9], (N_EVEN, SGU_GROUPS, SGU_CHUNK, SGU_CHUNK), SGU_CHUNK ** -0.5),
        "sgu_b": 1.0 + nrm(ks[10], (N_EVEN, SGU_GROUPS, SGU_CHUNK), 0.1),
        "hyb_w_out": nrm(ks[11], (N_EVEN, D_MODEL, D_MODEL), D_MODEL ** -0.5),
        "ret_w_in": nrm(ks[12], (N_ODD, D_MODEL, RET_IN), D_MODEL ** -0.5),
        "ret_log_decay": jnp.asarray(base_decay)[None, None, :] * (1.0 + nrm(ks[13], (N_ODD, 2, RET_HEADS), 0.05)),
        "ret_gn_g": 1.0 + nrm(ks[14], (N_ODD, RET_V_WIDTH), 0.1),
        "ret_w_out": nrm(ks[15], (N_ODD, RET_V_WIDTH, D_MODEL), RET_V_WIDTH ** -0.5),
        "ffn_w_in": nrm(ks[16], (DEPTH, D_MODEL, 2 * D_FF), D_MODEL ** -0.5),
        "ffn_conv_w": nrm(ks[17], (DEPTH, CONV_W, 2 * D_FF), CONV_W ** -0.5),
        "ffn_conv_b": nrm(ks[18], (DEPTH, 2 * D_FF), 0.02),
        "ffn_w_out": nrm(ks[19], (DEPTH, D_FF, D_MODEL), D_FF ** -0.5),
    }

def first_block(x, c, ctx, c_ctx, ada_w, ada_b, norm_g, hyb_w_in, na_rpb, sgu_w, sgu_b, hyb_w_out,
              ret_w_in, ret_log_decay, ret_gn_g, ret_w_out, ffn_w_in, ffn_conv_w, ffn_conv_b, ffn_w_out):
    xc = ctx
    silu_c = jax.nn.silu(c)
    silu_cc = jax.nn.silu(c_ctx)
    for i in range(DEPTH):
        ctx_out = i < DEPTH - 1
        j = i // 2
        mod_lat = (silu_c @ ada_w[i] + ada_b[i])[:, None, :]
        mod_ctx = (silu_cc @ ada_w[i] + ada_b[i])[None, None, :]
        sh1, sc1, g1, sh2, sc2, g2 = jnp.split(mod_lat, 6, axis=-1)
        csh1, csc1, cg1, csh2, csc2, cg2 = jnp.split(mod_ctx, 6, axis=-1)
        h_lat = modulate(rmsnorm(x, norm_g[i, 0]), sh1, sc1)
        h_ctx = modulate(rmsnorm(xc, norm_g[i, 0]), csh1, csc1)
        if i % 2 == 0:
            y_ctx, y_lat = hybrid_na_sgu(h_ctx, h_lat, hyb_w_in[j], na_rpb[j], sgu_w[j], sgu_b[j],
                                         hyb_w_out[j], ctx_out)
        else:
            y_ctx, y_lat = retention_mixer(h_ctx, h_lat, ret_w_in[j], ret_log_decay[j], ret_gn_g[j],
                                           ret_w_out[j], ctx_out)
        x = x + g1 * rmsnorm(y_lat, norm_g[i, 1])
        h = modulate(rmsnorm(x, norm_g[i, 2]), sh2, sc2)
        x = x + g2 * rmsnorm(conv_ffn(h, ffn_w_in[i], ffn_conv_w[i], ffn_conv_b[i], ffn_w_out[i]), norm_g[i, 3])
        if ctx_out:
            xc = xc + cg1 * rmsnorm(y_ctx, norm_g[i, 1])
            hc = modulate(rmsnorm(xc, norm_g[i, 2]), csh2, csc2)
            xc = xc + cg2 * rmsnorm(conv_ffn(hc, ffn_w_in[i], ffn_conv_w[i], ffn_conv_b[i], ffn_w_out[i]), norm_g[i, 3])
    return x


DEPTH_2 = 1


N_ATTN_HEADS = 8
ATTN_DH = 64
ATTN_DV = 2 * ATTN_DH
ATTN_QK_DIM = N_ATTN_HEADS * 2 * ATTN_DH
ATTN_V_DIM = N_ATTN_HEADS * ATTN_DV
ATTN_SCALE = ATTN_DH ** -0.5
ATTN_QBLOCK = 128
ROPE_THETA = 10000.0
ROPE_AXIS_DIM = ATTN_DH // 2

D_SSD = D_MODEL
SSD_HEADDIM = 64
SSD_HEADS = D_SSD // SSD_HEADDIM
SSD_GROUPS = 4
SSD_HPG = SSD_HEADS // SSD_GROUPS
SSD_STATE = 128
SSD_CONV_W = 3
SSD_CHUNK = 64
XBC_DIM = D_SSD + 2 * SSD_GROUPS * SSD_STATE

IN_SPLITS = (ATTN_QK_DIM, 2 * ATTN_QK_DIM, 2 * ATTN_QK_DIM + ATTN_V_DIM, 2 * ATTN_QK_DIM + ATTN_V_DIM + D_SSD, 2 * ATTN_QK_DIM + ATTN_V_DIM + D_SSD + XBC_DIM, 2 * ATTN_QK_DIM + ATTN_V_DIM + D_SSD + XBC_DIM + 2 * SSD_HEADS)
IN_COLS = IN_SPLITS[-1] + 2 * D_MODEL

N_EXPERTS = 64
EXPERT_FF = 256
SHARED_FF = 256
TOP_K = 8
N_EXPERT_GROUPS = 8
TOPK_GROUPS = 4
ROUTED_SCALE = 2.5
MOE_BLOCK = 128


def rmsnorm_2(u, g):
    uf = u.astype(jnp.float32)
    y = uf * lax.rsqrt(jnp.mean(uf * uf, axis=-1, keepdims=True) + EPS)
    return (y * g.astype(jnp.float32)).astype(u.dtype)

def modulate_2(u, shift, scale):
    return u * (1 + scale) + shift

def rev(t):
    return jnp.flip(t, axis=1)

def axial_rope_tables(n_tok):
    rows = n_tok // GRID_W
    row = jnp.repeat(jnp.arange(rows, dtype=jnp.float32), GRID_W)
    col = jnp.broadcast_to(jnp.arange(GRID_W, dtype=jnp.float32)[None, :], (rows, GRID_W)).reshape(-1)
    inv_freq = ROPE_THETA ** (-jnp.arange(0, ROPE_AXIS_DIM, 2, dtype=jnp.float32) / ROPE_AXIS_DIM)
    ang = jnp.concatenate([row[:, None] * inv_freq, col[:, None] * inv_freq], axis=-1)
    ang = jnp.concatenate([ang, ang], axis=-1)
    return jnp.cos(ang), jnp.sin(ang)

def apply_rope_2(u, cos, sin):
    half = ATTN_DH // 2
    uf = u.astype(jnp.float32)
    rot = jnp.concatenate([-uf[..., half:], uf[..., :half]], axis=-1)
    return (uf * cos[:, None, None, :] + rot * sin[:, None, None, :]).astype(u.dtype)

def diff_attend(q, k, v, lam, g_subln, lam_init):
    s = jnp.einsum('bqhcd,bkhcd->bchqk', q.astype(jnp.float32), k.astype(jnp.float32)) * ATTN_SCALE
    p = jax.nn.softmax(s, axis=-1)
    w = p[:, 0] - lam * p[:, 1]
    o = jnp.einsum('bhqk,bkhd->bqhd', w, v.astype(jnp.float32))
    o = o * lax.rsqrt(jnp.mean(o * o, axis=-1, keepdims=True) + EPS) * g_subln.astype(jnp.float32)
    return (o * (1.0 - lam_init)).astype(v.dtype)

def centred_dwconv(u, w, b):
    pad = SSD_CONV_W // 2
    n = u.shape[1]
    up = jnp.pad(u, ((0, 0), (pad, pad), (0, 0)))
    out = b
    for i in range(SSD_CONV_W):
        out = out + up[:, i:i + n] * w[i]
    return out

def ssd_inputs(xbc, dt_raw, conv_w, conv_b, dt_bias):
    nb, nl, _ = xbc.shape
    u = jax.nn.silu(centred_dwconv(xbc, conv_w, conv_b)).astype(jnp.float32)
    xs, bm, cm = jnp.split(u, (D_SSD, D_SSD + SSD_GROUPS * SSD_STATE), axis=-1)
    xh = xs.reshape(nb, nl, SSD_GROUPS, SSD_HPG, SSD_HEADDIM)
    bm = bm.reshape(nb, nl, SSD_GROUPS, SSD_STATE)
    cm = cm.reshape(nb, nl, SSD_GROUPS, SSD_STATE)
    dt = jax.nn.softplus(dt_raw.astype(jnp.float32).reshape(nb, nl, 2, SSD_GROUPS, SSD_HPG) + dt_bias.astype(jnp.float32).reshape(2, SSD_GROUPS, SSD_HPG))
    return xh, bm, cm, dt[:, :, 0], dt[:, :, 1]

def ssd_chunked(xh, dt, a, bm, cm, h0, with_output):
    nb, nl, ng, nr, npd = xh.shape
    nn = bm.shape[-1]
    nc = nl // SSD_CHUNK
    xc = xh.reshape(nb, nc, SSD_CHUNK, ng, nr, npd)
    dtc = dt.reshape(nb, nc, SSD_CHUNK, ng, nr)
    bc = bm.reshape(nb, nc, SSD_CHUNK, ng, nn)
    acum = jnp.cumsum(dtc * a, axis=2)
    to_end = jnp.exp(acum[:, :, -1:] - acum)
    states = jnp.einsum('bcqgn,bcqgr,bcqgrp->bcgrpn', bc, to_end * dtc, xc)
    chunk_decay = jnp.exp(acum[:, :, -1])

    def step(h, inp):
        st, dec = inp
        return h * dec[..., None, None] + st, (h if with_output else None)

    h_last, h_prev = lax.scan(step, h0, (jnp.moveaxis(states, 1, 0), jnp.moveaxis(chunk_decay, 1, 0)))
    if not with_output:
        return None, h_last
    cc = cm.reshape(nb, nc, SSD_CHUNK, ng, nn)
    seg = acum[:, :, :, None] - acum[:, :, None]
    lower = (jnp.arange(SSD_CHUNK)[:, None] >= jnp.arange(SSD_CHUNK)[None, :])[:, :, None, None]
    decay = jnp.where(lower, jnp.exp(jnp.where(lower, seg, 0.0)), 0.0)
    cb = jnp.einsum('bcign,bcjgn->bcijg', cc, bc)
    y_diag = jnp.einsum('bcijg,bcijgr,bcjgr,bcjgrp->bcigrp', cb, decay, dtc, xc)
    y_off = jnp.einsum('bcign,cbgrpn,bcigr->bcigrp', cc, h_prev, jnp.exp(acum))
    y = (y_diag + y_off).reshape(nb, nl, ng, nr, npd)
    return y, h_last

def merge_branches(o_attn, y_ssd, z, gates, g_ssd_norm, w_branch_attn, w_branch_ssd, w_out):
    out_dtype = z.dtype
    y = y_ssd * jax.nn.silu(z.astype(jnp.float32))
    shp = y.shape
    yg = y.reshape(shp[:-1] + (SSD_GROUPS, D_SSD // SSD_GROUPS))
    yg = yg * lax.rsqrt(jnp.mean(yg * yg, axis=-1, keepdims=True) + EPS)
    y = (yg.reshape(shp) * g_ssd_norm.astype(jnp.float32)).astype(out_dtype)
    ya = o_attn @ w_branch_attn
    ys = y @ w_branch_ssd
    g_a, g_s = jnp.split(jax.nn.sigmoid(gates), 2, axis=-1)
    return (g_a * ya + g_s * ys) @ w_out

def token_mixer(h, hc, update_ctx, lam_init, w_in, lam_q1, lam_k1, lam_q2, lam_k2, g_attn_subln, conv_w, conv_b, dt_bias, a_log, d_skip, g_ssd_norm, w_branch_attn, w_branch_ssd, w_out):
    nb, ns, _ = h.shape
    nl = hc.shape[1]
    w_q, w_k, w_v, w_z, w_xbc, w_dt, w_g = jnp.split(w_in, IN_SPLITS, axis=1)
    q, k, v, z, xbc, dt_raw, gates = jnp.split(h @ w_in, IN_SPLITS, axis=-1)

    lam = (jnp.exp(jnp.sum(lam_q1.astype(jnp.float32) * lam_k1.astype(jnp.float32)))
           - jnp.exp(jnp.sum(lam_q2.astype(jnp.float32) * lam_k2.astype(jnp.float32))) + lam_init)
    cos, sin = axial_rope_tables(ns)
    q = apply_rope_2(q.reshape(nb, ns, N_ATTN_HEADS, 2, ATTN_DH), cos, sin)
    k = apply_rope_2(k.reshape(nb, ns, N_ATTN_HEADS, 2, ATTN_DH), cos, sin)
    v = v.reshape(nb, ns, N_ATTN_HEADS, ATTN_DV)
    kc = (hc @ w_k).reshape(nb, nl, N_ATTN_HEADS, 2, ATTN_DH)
    vc = (hc @ w_v).reshape(nb, nl, N_ATTN_HEADS, ATTN_DV)
    k_all = jnp.concatenate([kc, k], axis=1)
    v_all = jnp.concatenate([vc, v], axis=1)
    n_qb = ns // ATTN_QBLOCK
    q_blocks = jnp.swapaxes(q.reshape(nb, n_qb, ATTN_QBLOCK, N_ATTN_HEADS, 2, ATTN_DH), 0, 1)
    o = lax.map(lambda qb: diff_attend(qb, k_all, v_all, lam, g_attn_subln, lam_init), q_blocks)
    o_lat = jnp.swapaxes(o, 0, 1).reshape(nb, ns, ATTN_V_DIM)

    a = -jnp.exp(a_log.astype(jnp.float32)).reshape(2, SSD_GROUPS, SSD_HPG)
    d = d_skip.astype(jnp.float32).reshape(SSD_GROUPS, SSD_HPG, 1)
    xh_c, bm_c, cm_c, dtf_c, dtb_c = ssd_inputs(hc @ w_xbc, hc @ w_dt, conv_w, conv_b, dt_bias)
    h0 = jnp.zeros((nb, SSD_GROUPS, SSD_HPG, SSD_HEADDIM, SSD_STATE), jnp.float32)
    yf_c, hf = ssd_chunked(xh_c, dtf_c, a[0], bm_c, cm_c, h0, update_ctx)
    yb_c, hb = ssd_chunked(rev(xh_c), rev(dtb_c), a[1], rev(bm_c), rev(cm_c), h0, update_ctx)
    xh, bm, cm, dtf, dtb = ssd_inputs(xbc, dt_raw, conv_w, conv_b, dt_bias)
    yf, _ = ssd_chunked(xh, dtf, a[0], bm, cm, hf, True)
    yb, _ = ssd_chunked(rev(xh), rev(dtb), a[1], rev(bm), rev(cm), hb, True)
    y_lat = (yf + rev(yb) + d * xh).reshape(nb, ns, D_SSD)

    out_lat = merge_branches(o_lat, y_lat, z, gates, g_ssd_norm, w_branch_attn, w_branch_ssd, w_out)
    if not update_ctx:
        return out_lat, None
    qc = (hc @ w_q).reshape(nb, nl, N_ATTN_HEADS, 2, ATTN_DH)
    o_ctx = diff_attend(qc, kc, vc, lam, g_attn_subln, lam_init).reshape(nb, nl, ATTN_V_DIM)
    y_ctx = (yf_c + rev(yb_c) + d * xh_c).reshape(nb, nl, D_SSD)
    out_ctx = merge_branches(o_ctx, y_ctx, hc @ w_z, hc @ w_g, g_ssd_norm, w_branch_attn, w_branch_ssd, w_out)
    return out_lat, out_ctx

def moe_ffn(h, w_router, router_bias, w_e_gate, w_e_up, w_e_down, w_sh_gate, w_sh_up, w_sh_down):
    n_tok, d = h.shape
    scores = jax.nn.sigmoid((h @ w_router).astype(jnp.float32))
    sel = scores + router_bias.astype(jnp.float32)
    grp = sel.reshape(n_tok, N_EXPERT_GROUPS, N_EXPERTS // N_EXPERT_GROUPS)
    grp_score = lax.top_k(grp, 2)[0].sum(-1)
    top_g = lax.top_k(grp_score, TOPK_GROUPS)[1]
    gmask = jax.nn.one_hot(top_g, N_EXPERT_GROUPS, dtype=jnp.float32).sum(1) > 0
    emask = jnp.repeat(gmask, N_EXPERTS // N_EXPERT_GROUPS, axis=1)
    top_e = lax.top_k(jnp.where(emask, sel, -jnp.inf), TOP_K)[1]
    wts = jnp.take_along_axis(scores, top_e, axis=1)
    wts = wts / jnp.sum(wts, axis=-1, keepdims=True) * ROUTED_SCALE

    n_assign = n_tok * TOP_K
    n_blocks = -(-n_assign // MOE_BLOCK) + N_EXPERTS
    n_pad = n_blocks * MOE_BLOCK
    e_flat = top_e.reshape(-1)
    order = jnp.argsort(e_flat)
    e_sorted = e_flat[order]
    tok_sorted = (jnp.arange(n_assign, dtype=jnp.int32) // TOP_K)[order]
    w_sorted = wts.reshape(-1)[order]
    counts = jnp.bincount(e_flat, length=N_EXPERTS)
    start = jnp.cumsum(counts) - counts
    padded = (counts + MOE_BLOCK - 1) // MOE_BLOCK * MOE_BLOCK
    pend = jnp.cumsum(padded)
    pstart = pend - padded
    dest = pstart[e_sorted] + jnp.arange(n_assign, dtype=jnp.int32) - start[e_sorted]
    buf_tok = jnp.zeros((n_pad,), jnp.int32).at[dest].set(tok_sorted)
    buf_w = jnp.zeros((n_pad,), jnp.float32).at[dest].set(w_sorted)
    block_e = jnp.minimum(jnp.searchsorted(pend, jnp.arange(n_blocks, dtype=jnp.int32) * MOE_BLOCK, side='right'), N_EXPERTS - 1)

    def expert_block(args):
        tok_b, w_b, e = args
        xb = h[tok_b]
        hid = jax.nn.silu(xb @ w_e_gate[e]) * (xb @ w_e_up[e])
        return (hid @ w_e_down[e]) * w_b[:, None].astype(h.dtype)

    out = lax.map(expert_block, (buf_tok.reshape(n_blocks, MOE_BLOCK), buf_w.reshape(n_blocks, MOE_BLOCK), block_e))
    routed = jax.ops.segment_sum(out.reshape(n_pad, d), buf_tok, num_segments=n_tok)
    shared = (jax.nn.silu(h @ w_sh_gate) * (h @ w_sh_up)) @ w_sh_down
    return routed + shared

def second_inputs(seed: int = 0) -> dict:
    key = jax.random.key(seed)
    ks = jax.random.split(key, 40)
    f32 = jnp.float32

    def nrm(k, shape, scale):
        return jax.random.normal(k, shape, f32) * scale

    def gain(k, shape):
        return 1.0 + 0.05 * jax.random.normal(k, shape, f32)

    u_dt = jax.random.uniform(ks[18], (DEPTH_2, 2, SSD_HEADS), f32)
    dt0 = jnp.exp(u_dt * (math.log(0.1) - math.log(0.001)) + math.log(0.001))
    return {
        'x': nrm(ks[0], (BATCH, SEQ, D_MODEL), 1.0),
        'c': nrm(ks[1], (BATCH, D_MODEL), 1.0),
        'ctx': nrm(ks[2], (BATCH, CTX_LEN, D_MODEL), 1.0),
        'c_ctx': nrm(ks[3], (D_MODEL,), 1.0),
        'w_ada': nrm(ks[4], (DEPTH_2, D_MODEL, 6 * D_MODEL), 0.5 * D_MODEL ** -0.5),
        'b_ada': nrm(ks[5], (DEPTH_2, 6 * D_MODEL), 0.02),
        'g_pre_mix': gain(ks[6], (DEPTH_2, D_MODEL)),
        'g_post_mix': gain(ks[7], (DEPTH_2, D_MODEL)),
        'g_pre_ffn': gain(ks[8], (DEPTH_2, D_MODEL)),
        'g_post_ffn': gain(ks[9], (DEPTH_2, D_MODEL)),
        'w_in': nrm(ks[10], (DEPTH_2, D_MODEL, IN_COLS), D_MODEL ** -0.5),
        'lam_q1': nrm(ks[11], (DEPTH_2, ATTN_DH), 0.1),
        'lam_k1': nrm(ks[12], (DEPTH_2, ATTN_DH), 0.1),
        'lam_q2': nrm(ks[13], (DEPTH_2, ATTN_DH), 0.1),
        'lam_k2': nrm(ks[14], (DEPTH_2, ATTN_DH), 0.1),
        'g_attn_subln': gain(ks[15], (DEPTH_2, ATTN_DV)),
        'conv_w': nrm(ks[16], (DEPTH_2, SSD_CONV_W, XBC_DIM), SSD_CONV_W ** -0.5),
        'conv_b': nrm(ks[17], (DEPTH_2, XBC_DIM), 0.02),
        'dt_bias': dt0 + jnp.log(-jnp.expm1(-dt0)),
        'a_log': jnp.log(jax.random.uniform(ks[19], (DEPTH_2, 2, SSD_HEADS), f32, 1.0, 16.0)),
        'd_skip': gain(ks[20], (DEPTH_2, SSD_HEADS)),
        'g_ssd_norm': gain(ks[21], (DEPTH_2, D_SSD)),
        'w_branch_attn': nrm(ks[22], (DEPTH_2, ATTN_V_DIM, D_MODEL), ATTN_V_DIM ** -0.5),
        'w_branch_ssd': nrm(ks[23], (DEPTH_2, D_SSD, D_MODEL), D_SSD ** -0.5),
        'w_out': nrm(ks[24], (DEPTH_2, D_MODEL, D_MODEL), D_MODEL ** -0.5),
        'w_router': nrm(ks[25], (DEPTH_2, D_MODEL, N_EXPERTS), D_MODEL ** -0.5),
        'router_bias': nrm(ks[26], (DEPTH_2, N_EXPERTS), 0.01),
        'w_e_gate': nrm(ks[27], (DEPTH_2, N_EXPERTS, D_MODEL, EXPERT_FF), D_MODEL ** -0.5),
        'w_e_up': nrm(ks[28], (DEPTH_2, N_EXPERTS, D_MODEL, EXPERT_FF), D_MODEL ** -0.5),
        'w_e_down': nrm(ks[29], (DEPTH_2, N_EXPERTS, EXPERT_FF, D_MODEL), EXPERT_FF ** -0.5),
        'w_sh_gate': nrm(ks[30], (DEPTH_2, D_MODEL, SHARED_FF), D_MODEL ** -0.5),
        'w_sh_up': nrm(ks[31], (DEPTH_2, D_MODEL, SHARED_FF), D_MODEL ** -0.5),
        'w_sh_down': nrm(ks[32], (DEPTH_2, SHARED_FF, D_MODEL), SHARED_FF ** -0.5),
    }

def second_block(x, c, ctx, c_ctx, w_ada, b_ada, g_pre_mix, g_post_mix, g_pre_ffn, g_post_ffn, w_in, lam_q1, lam_k1, lam_q2, lam_k2, g_attn_subln, conv_w, conv_b, dt_bias, a_log, d_skip, g_ssd_norm, w_branch_attn, w_branch_ssd, w_out, w_router, router_bias, w_e_gate, w_e_up, w_e_down, w_sh_gate, w_sh_up, w_sh_down):
    nb, ns, d = x.shape
    for li in range(DEPTH_2):
        update_ctx = li < DEPTH_2 - 1
        lam_init = 0.8 - 0.6 * math.exp(-0.3 * li)
        mod = jax.nn.silu(c) @ w_ada[li] + b_ada[li]
        sh1, sc1, gt1, sh2, sc2, gt2 = jnp.split(mod[:, None, :], 6, axis=-1)
        mod_c = jax.nn.silu(c_ctx) @ w_ada[li] + b_ada[li]
        sh1c, sc1c, gt1c, sh2c, sc2c, gt2c = jnp.split(mod_c, 6)

        h = modulate_2(rmsnorm_2(x, g_pre_mix[li]), sh1, sc1)
        hc = modulate_2(rmsnorm_2(ctx, g_pre_mix[li]), sh1c, sc1c)
        mix, mix_c = token_mixer(h, hc, update_ctx, lam_init, w_in[li], lam_q1[li], lam_k1[li], lam_q2[li], lam_k2[li], g_attn_subln[li], conv_w[li], conv_b[li], dt_bias[li], a_log[li], d_skip[li], g_ssd_norm[li], w_branch_attn[li], w_branch_ssd[li], w_out[li])
        x = x + gt1 * rmsnorm_2(mix, g_post_mix[li])

        h = modulate_2(rmsnorm_2(x, g_pre_ffn[li]), sh2, sc2)
        moe_w = (w_router[li], router_bias[li], w_e_gate[li], w_e_up[li], w_e_down[li], w_sh_gate[li], w_sh_up[li], w_sh_down[li])
        if update_ctx:
            ctx = ctx + gt1c * rmsnorm_2(mix_c, g_post_mix[li])
            hc = modulate_2(rmsnorm_2(ctx, g_pre_ffn[li]), sh2c, sc2c)
            f = moe_ffn(jnp.concatenate([h.reshape(-1, d), hc.reshape(-1, d)], axis=0), *moe_w)
            f_lat = f[: nb * ns]
            ctx = ctx + gt2c * rmsnorm_2(f[nb * ns:].reshape(ctx.shape), g_post_ffn[li])
        else:
            f_lat = moe_ffn(h.reshape(-1, d), *moe_w)
        x = x + gt2 * rmsnorm_2(f_lat.reshape(x.shape), g_post_ffn[li])
    return x


def setup_inputs(seed=0):
    out = dict(first_inputs(seed))
    for name, value in second_inputs(seed + 1).items():
        if name != "x":
            out[name + "_2"] = value
    return out


def reference(
    x, c, ctx, c_ctx, ada_w, ada_b, norm_g, hyb_w_in, na_rpb, sgu_w, sgu_b, hyb_w_out, ret_w_in,
    ret_log_decay, ret_gn_g, ret_w_out, ffn_w_in, ffn_conv_w, ffn_conv_b, ffn_w_out, c_2, ctx_2,
    c_ctx_2, w_ada_2, b_ada_2, g_pre_mix_2, g_post_mix_2, g_pre_ffn_2, g_post_ffn_2, w_in_2,
    lam_q1_2, lam_k1_2, lam_q2_2, lam_k2_2, g_attn_subln_2, conv_w_2, conv_b_2, dt_bias_2,
    a_log_2, d_skip_2, g_ssd_norm_2, w_branch_attn_2, w_branch_ssd_2, w_out_2, w_router_2,
    router_bias_2, w_e_gate_2, w_e_up_2, w_e_down_2, w_sh_gate_2, w_sh_up_2, w_sh_down_2,
):
    x = first_block(
        x, c, ctx, c_ctx, ada_w, ada_b, norm_g, hyb_w_in, na_rpb, sgu_w, sgu_b, hyb_w_out,
        ret_w_in, ret_log_decay, ret_gn_g, ret_w_out, ffn_w_in, ffn_conv_w, ffn_conv_b,
        ffn_w_out,
    )
    return second_block(
        x, c_2, ctx_2, c_ctx_2, w_ada_2, b_ada_2, g_pre_mix_2, g_post_mix_2, g_pre_ffn_2,
        g_post_ffn_2, w_in_2, lam_q1_2, lam_k1_2, lam_q2_2, lam_k2_2, g_attn_subln_2, conv_w_2,
        conv_b_2, dt_bias_2, a_log_2, d_skip_2, g_ssd_norm_2, w_branch_attn_2, w_branch_ssd_2,
        w_out_2, w_router_2, router_bias_2, w_e_gate_2, w_e_up_2, w_e_down_2, w_sh_gate_2,
        w_sh_up_2, w_sh_down_2,
    )


_drawn_inputs = setup_inputs


def setup_inputs(seed=0):
    import zlib

    import numpy as np

    out = dict(_drawn_inputs(seed))
    spreads = {}
    factors = {'na_rpb': 5.572,
     'g_post_mix_2': 2.786,
     'g_post_ffn_2': 4.614,
     'g_attn_subln_2': 3.767,
     'conv_b_2': 4.01,
     'd_skip_2': 4.199,
     'g_ssd_norm_2': 2.773}
    for name, (base, spread) in spreads.items():
        noise = np.random.default_rng([zlib.crc32(name.encode()), seed]).standard_normal(out[name].shape)
        drawn = base * np.exp(spread * noise) if base else spread * noise
        out[name] = jnp.asarray(drawn.astype(out[name].dtype))
    for name, factor in factors.items():
        out[name] = (out[name] * factor).astype(out[name].dtype)
    return out
```

```python
from contextlib import ExitStack

import numpy as np

import concourse.bass as bass
from concourse import mybir

F32 = mybir.dt.float32
ALU = mybir.AluOpType
ACT = mybir.ActivationFunctionType
AX = mybir.AxisListType

P = 128
D = 1024
KD = D // P
T = 512
L = 256
N = T + L
NTT = N // P
LTT = T // P
GRID_W = 64
EPS = 1e-6
NEG = -1e30
DFF = 2816
FT = DFF // P
NE = 64
TOPK = 8
SLOTS = 8
UC = 1024
LAM_INIT = 0.2
LAT, CTX = (0, T), (T, L)
BIG = 3e38


VEC = {}
_n = 0
for _name, _w in (
    ("c0", 16), ("c2", 16), ("ada_b0", 48), ("ada_b1", 48), ("ada_b2", 48),
    ("norm0", 32), ("norm1", 32), ("norm2", 32),
    ("cw0", 3 * 2 * FT), ("cb0", 2 * FT), ("cw1", 3 * 2 * FT), ("cb1", 2 * FT),
    ("gn_g", 16), ("subln", 1), ("ssd_norm", 8), ("d_skip", 8), ("scw", 48), ("scb", 16),
    ("lgd", 16), ("dt_bias", 32), ("a_log", 32), ("rbias", 64), ("lam", 4), ("before", 64),
):
    VEC[_name] = (_n, _w)
    _n += _w
NVEC = _n

CON = {}
_n = 0
for _name, _w in (("ident", P), ("ones", P), ("ge", P), ("le", P), ("lt", P), ("gt", P), ("negf", P), ("negb", P),
                  ("rot64", P), ("rot32", P), ("namask", 64)):
    CON[_name] = (_n, _w)
    _n += _w
NCON = _n
BCON = {}
for _name, _w in (("absd", 1408), ("cos_r", T), ("sin_r", T), ("cos_d", T), ("sin_d", T)):
    BCON[_name] = (_n, _w)
    _n += _w
NCONALL = _n


PRIMED = ("out_taken", "conv_done", "silu_done", "gate_silu", "up_taken", "hidden_ready", "acc_taken")
PRIME = 4


class Signal:

    def __init__(self, sem, n):
        self.sem, self.n = sem, n

    def take(self, k):
        base = self.n
        self.n += k
        return base


class Chain:

    def __init__(self, sem):
        self.sem, self.n, self.i, self.per, self.n0 = sem, 0, None, 0, 0

    def count(self):
        self.n += 1
        return self.sem

    def value(self):
        return self.n if self.i is None else self.i * self.per + self.n

    def enter(self, i, per):
        self.i, self.per, self.n0 = i, per, self.n

    def leave(self, turns):
        assert self.n - self.n0 == self.per, (self.n - self.n0, self.per)
        self.n = self.n0 + self.per * turns
        self.i = None


class Core:

    def __init__(self, nc, ctx):
        self.nc = nc
        self.words = 53208
        self.sb = ctx.enter_context(nc.sbuf_tensor("arena", [P, self.words], F32))
        self.ps = ctx.enter_context(nc.psum_tensor("ps", [P, 8, 512], F32))
        self.ctx = ctx
        self.signals = {}
        self.unit = 0
        o = 0
        self.X, o = self.at(o, KD, N), o + KD * N
        self.H, o = self.at(o, KD, N), o + KD * N
        self.ring, o = self.at(o, SLOTS, UC), o + SLOTS * UC
        self.vecs, o = self.at(o, NVEC), o + NVEC
        self.con, o = self.at(o, NCON), o + NCON
        self.mods, o = self.at(o, 3, 2, 6, 8), o + 288
        self.csil, o = self.at(o, 8, 2), o + 16
        self.small, o = self.at(o, 64), o + 64
        self.free = o
        self.slot = [ctx.enter_context(nc.semaphore(f"slot_loaded{i}")) for i in range(SLOTS)]

    def at(self, off, *dims):
        n = int(np.prod(dims))
        assert off + n <= self.words, (off, n)
        v = self.sb[:, off:off + n]
        names = "abcd"[:len(dims)]
        if len(dims) > 1:
            v = v.rearrange(f"p ({' '.join(names)}) -> p {' '.join(names)}", **dict(zip(names[1:], dims[1:])))
        return v

    def place(self, *shapes):
        out, o = [], self.free
        for s in shapes:
            out.append(self.at(o, *s))
            o += int(np.prod(s))
        return out

    def sig(self, name):
        if name not in self.signals:
            self.signals[name] = Signal(self.ctx.enter_context(self.nc.semaphore(name)), PRIME if name in PRIMED else 0)
        return self.signals[name]

    def vec(self, name, a=0, b=None):
        o, w = VEC[name]
        return self.vecs[:, o + a:o + (w if b is None else b)]

    def c(self, name):
        o, w = CON[name]
        return self.con[:, o:o + w]

    def units(self, n):
        u = self.unit
        self.unit += n
        return u


class Stage:
    def sync(self, sp): pass
    def tensor(self, pe): pass
    def vector(self, dve): pass
    def scalar(self, act): pass
    def gpsimd(self, pool): pass


def turns(n, body, peel=False):
    first = body if peel and n >= body else 0
    t = (n - first) // body
    return first, t, n - first - t * body


def ring_loads(k, sp, w, u0, n, cols=lambda j: UC, period=8):
    used = k.sig("unit_used")

    def load(i, j):
        u = u0 + j
        if not (isinstance(i, int) and u + i - SLOTS < 0):
            sp.wait_ge(used.sem, u + i - SLOTS + 1)
        c = cols(j)
        sp.dma_start(k.ring[:, u % SLOTS, 0:c], w(i, j, c)).then_inc(k.slot[u % SLOTS], 16)

    first, t, tail = turns(n, period, peel=u0 < SLOTS)
    for j in range(first):
        load(0, j)
    if t > 1:
        with sp.Fori(0, t) as i:
            for j in range(period):
                load(i * period + first, j)
    elif t == 1:
        for j in range(period):
            load(first, j)
    for j in range(tail):
        load(first + t * period, j)


def slot_count(u, i=0):
    return (u // SLOTS + 1) * 16 + i * 16



class Load(Stage):

    def __init__(self, k, dram):
        self.k, self.dram = k, dram
        self.got = k.sig("inputs_loaded")
        self.got.take(64)

    def sync(self, sp):
        k, d = self.k, self.dram
        sp.dma_start(k.vecs, d["vecs"]).then_inc(self.got.sem, 16)
        sp.dma_start(k.con, d["consts"][:, 0:NCON]).then_inc(self.got.sem, 16)
        sp.dma_start(k.X[:, :, 0:T], d["xT"]).then_inc(self.got.sem, 16)
        sp.dma_start(k.X[:, :, T:N], d["ctxT"]).then_inc(self.got.sem, 16)

    def tensor(self, pe):
        pe.wait_ge(self.got.sem, 64)

    def vector(self, dve):
        k = self.k
        for n, name in enumerate(PRIMED):
            dve.memset(k.small[:, n:n + 1], 0.0).then_inc(k.sig(name).sem, PRIME)
        dve.wait_ge(self.got.sem, 64)

    def scalar(self, act):
        act.wait_ge(self.got.sem, 64)

    def gpsimd(self, pool):
        pool.wait_ge(self.got.sem, 64)


class Mods(Stage):

    def __init__(self, k, layer, w, cvec):
        self.k, self.layer, self.w, self.cvec = k, layer, w, cvec
        self.u0 = k.units(48)
        k.sig("unit_used").take(48)
        self.silu = k.sig("silu_c").take(1)

    def sync(self, sp):
        ring_loads(self.k, sp, lambda i, j, c: self.w[i + j, :, 0:c], self.u0, 48)

    def scalar(self, act):
        k = self.k
        act.activation(k.csil.rearrange("p a b -> p (a b)"), k.vec(self.cvec), ACT.Silu)\
            .then_inc(k.sig("silu_c").sem, 1)

    def tensor(self, pe):
        k = self.k
        pe.wait_ge(k.sig("silu_c").sem, self.silu + 1)

        def unit(i, j):
            u = self.u0 + j
            pe.wait_ge(k.slot[u % SLOTS], slot_count(u, i))
            for c in range(KD):
                at = (i * 8 + j) * 2
                mm = pe.matmul(k.ps[:, 0, bass.ds(at, 2)], lhsT=k.ring[:, u % SLOTS, c * P:(c + 1) * P],
                               rhs=k.csil[:, c, :], start=c == 0, stop=c == KD - 1)
            mm.then_inc(k.sig("unit_used").sem, 1)

        with pe.Fori(0, 6) as i:
            for j in range(8):
                unit(i, j)

    def vector(self, dve):
        k, l = self.k, self.layer
        dve.wait_ge(k.sig("unit_used").sem, self.u0 + 48)
        m = k.mods[:, l].rearrange("p w a b -> p w (a b)")
        for w in range(2):
            dve.tensor_tensor(m[:, w, :], k.ps[:, 0, w:96:2], k.vec(f"ada_b{l}"), ALU.add).then_inc(k.dve.count(), 1)
        dve.wait_ge(k.dve.sem, k.dve.value())
        g = k.vec(f"norm{l}").rearrange("p (a b) -> p a b", b=8)
        for w in range(2):
            mm = k.mods[:, l, w]
            for at, gain in ((1, 0), (4, 2)):
                dve.scalar_tensor_tensor(out=mm[:, at, :], in0=mm[:, at, :], scalar=1.0, in1=g[:, gain, :],
                                         op0=ALU.add, op1=ALU.mult)
            for at, gain in ((2, 1), (5, 3)):
                dve.tensor_tensor(mm[:, at, :], mm[:, at, :], g[:, gain, :], ALU.mult)


class Norm(Stage):

    def __init__(self, k, src, layer, gain, shift=None, into=None, spans=(LAT, CTX), which=(0, 1), scratch=None):
        self.k, self.src, self.into, self.spans = k, src, into, spans
        self.gain = [k.mods[:, layer, w, gain, :] for w in which]
        self.shift = None if shift is None else [k.mods[:, layer, w, shift, :] for w in which]
        n = len(spans)
        self.sq_base = k.sig("square_ready").take(KD * n)
        self.ss_base = k.sig("sum_ready").take(n)
        self.sd_base = k.sig("root_ready").take(n)
        self.t_base = k.sig("scaled_ready").take(KD * n)
        self.off = k.free if scratch is None else scratch

    def buffers(self):
        k = self.k
        return k.at(self.off, KD, N), k.at(self.off + KD * N, N), k.at(self.off + KD * N + N, N)

    def scalar(self, act):
        k = self.k
        sq, sd, _ = self.buffers()
        for n, (o, w) in enumerate(self.spans):
            for c in range(KD):
                act.activation(sq[:, c, o:o + w], self.src[:, c, o:o + w], ACT.Square)\
                    .then_inc(k.sig("square_ready").sem, 1)
        for n, (o, w) in enumerate(self.spans):
            act.wait_ge(k.sig("sum_ready").sem, self.ss_base + n + 1)
            act.activation(sd[:, o:o + w], k.ps[:, n, 0:w], ACT.Sqrt, bias=EPS, scale=1.0 / D)\
                .then_inc(k.sig("root_ready").sem, 1)
        if self.into is not None:
            for n, (o, w) in enumerate(self.spans):
                for c in range(KD):
                    act.wait_ge(k.sig("scaled_ready").sem, self.t_base + n * KD + c + 1)
                    act.activation(self.into[:, c, o:o + w], sq[:, c, o:o + w], ACT.Identity,
                                   bias=self.shift[n][:, c:c + 1], scale=self.gain[n][:, c:c + 1])

    def tensor(self, pe):
        k = self.k
        sq, _, _ = self.buffers()
        for n, (o, w) in enumerate(self.spans):
            for c in range(KD):
                pe.wait_ge(k.sig("square_ready").sem, self.sq_base + n * KD + c + 1)
                mm = pe.matmul(k.ps[:, n, 0:w], lhsT=k.c("ones"), rhs=sq[:, c, o:o + w], start=c == 0, stop=c == KD - 1)
            mm.then_inc(k.sig("sum_ready").sem, 1)

    def vector(self, dve):
        k = self.k
        sq, sd, rs = self.buffers()
        for n, (o, w) in enumerate(self.spans):
            dve.wait_ge(k.sig("root_ready").sem, self.sd_base + n + 1)
            dve.reciprocal(rs[:, o:o + w], sd[:, o:o + w]).then_inc(k.dve.count(), 1)
            dve.wait_ge(k.dve.sem, k.dve.value())
            for c in range(KD):
                if self.into is not None:
                    dve.tensor_tensor(sq[:, c, o:o + w], self.src[:, c, o:o + w], rs[:, o:o + w], ALU.mult)\
                        .then_inc(k.sig("scaled_ready").sem, 1)
                else:
                    dve.scalar_tensor_tensor(out=sq[:, c, o:o + w], in0=self.src[:, c, o:o + w],
                                             scalar=self.gain[n][:, c:c + 1], in1=rs[:, o:o + w],
                                             op0=ALU.mult, op1=ALU.mult).then_inc(k.sig("scaled_ready").sem, 1)

    def gpsimd(self, pool):
        k = self.k
        if self.into is not None:
            return
        sq, _, _ = self.buffers()
        for n, (o, w) in enumerate(self.spans):
            for c in range(KD):
                pool.wait_ge(k.sig("scaled_ready").sem, self.t_base + n * KD + c + 1)
                pool.tensor_tensor(k.X[:, c, o:o + w], k.X[:, c, o:o + w], sq[:, c, o:o + w], ALU.add)


class Linear(Stage):

    def __init__(self, k, w, n_tiles, rhs, dst, kt=KD, spans=(LAT, CTX), func=ACT.Copy, t0=0, d0=0):
        self.k, self.w, self.n_tiles, self.rhs, self.dst, self.kt = k, w, n_tiles, rhs, dst, kt
        self.spans, self.func, self.t0, self.d0 = spans, func, t0, d0
        self.upt = -(-kt // 8)
        self.n_units = n_tiles * self.upt
        self.u0 = k.units(self.n_units)
        k.sig("unit_used").take(self.n_units)
        self.body = 24 if self.upt == 3 else 8
        self.taken = k.sig("out_taken").take(n_tiles)

    def cols(self, j):
        return min(8, self.kt - 8 * (j % self.upt)) * P

    def sync(self, sp):
        upt = self.upt
        if upt == 1:
            src = lambda i, j, c: self.w[i + j + self.t0, :, 0:c]
        elif upt == 2:
            src = lambda i, j, c: self.w[i + j, :, 0:c]
        else:
            src = lambda i, j, c: self.w[j // upt, :, (j % upt) * UC:(j % upt) * UC + c]
        ring_loads(self.k, sp, src, self.u0, self.n_units, self.cols, self.body)

    def tensor(self, pe):
        k, upt = self.k, self.upt

        def unit(i, j):
            u = self.u0 + j
            t = j // upt
            pe.wait_ge(k.slot[u % SLOTS], slot_count(u, i * (self.body // 8)))
            part = j % upt
            ks = range(part * 8, min(part * 8 + 8, self.kt))
            if part == 0:
                pe.wait_ge(k.sig("out_taken").sem, self.taken + t - 1 + i * (self.body // upt))
            for s, (o, w) in enumerate(self.spans):
                for c in ks:
                    mm = pe.matmul(k.ps[:, 2 * s + t % 2, 0:w],
                                   lhsT=k.ring[:, u % SLOTS, (c % 8) * P:(c % 8 + 1) * P],
                                   rhs=self.rhs[:, c, o:o + w], start=c == 0, stop=c == self.kt - 1)
            mm.then_inc(k.sig("unit_used").sem, 1)

        run_body(pe, self.n_units, self.body, unit)

    def scalar(self, act):
        k, upt = self.k, self.upt

        def unit(i, j):
            if j % upt != upt - 1:
                return
            t = j // upt
            act.wait_ge(k.sig("unit_used").sem, self.u0 + j + 1 + i * self.body)
            for s, (o, w) in enumerate(self.spans):
                a = act.activation(self.dst[:, i * (self.body // upt) + t + self.d0, o:o + w],
                                   k.ps[:, 2 * s + t % 2, 0:w], self.func)
            a.then_inc(k.sig("out_taken").sem, 1)

        run_body(act, self.n_units, self.body, unit)


def run_body(eng, n, body, unit, chain=None, per=0):
    t = n // body
    if t > 1:
        with eng.Fori(0, t) as i:
            if chain:
                chain.enter(i, per)
            for j in range(body):
                unit(i, j)
            if chain:
                chain.leave(t)
    elif t == 1:
        for j in range(body):
            unit(0, j)
    for j in range(n - t * body):
        unit(t, j)


class TokLinear(Stage):

    def __init__(self, k, w, groups, dst, func=ACT.Copy, t0=0):
        self.k, self.w, self.groups, self.dst, self.func, self.t0 = k, w, groups, dst, func, t0
        self.u0 = k.units(4 * groups)
        k.sig("unit_used").take(4 * groups)
        self.taken = k.sig("tok_taken").take(NTT * groups)
        self.ready = k.sig("tok_ready").take((NTT - 1) * groups)

    def sync(self, sp):
        ring_loads(self.k, sp, lambda i, j, c: self.w[i + j + self.t0, :, 0:c], self.u0, 4 * self.groups)

    def tensor(self, pe):
        k = self.k
        for g in range(self.groups):
            s0 = (self.u0 + 4 * g) % SLOTS
            for j in range(4):
                pe.wait_ge(k.slot[(self.u0 + 4 * g + j) % SLOTS], slot_count(self.u0 + 4 * g + j))
            for t in range(NTT):
                n = g * NTT + t
                if n >= 4:
                    pe.wait_ge(k.sig("tok_taken").sem, self.taken + n - 3)
                for c in range(KD):
                    mm = pe.matmul(k.ps[:, 4 + n % 4, :].rearrange("p (a b) -> p a b", a=4),
                                   lhsT=k.H[:, c, t * P:(t + 1) * P],
                                   rhs=k.ring[:, s0:s0 + 4, c * P:(c + 1) * P], start=c == 0, stop=c == KD - 1)
                if t < NTT - 1:
                    mm.then_inc(k.sig("tok_ready").sem, 1)
                else:
                    mm.then_inc(k.sig("unit_used").sem, 4)

    def scalar(self, act):
        k = self.k
        for g in range(self.groups):
            for t in range(NTT):
                n = g * NTT + t
                if t < NTT - 1:
                    act.wait_ge(k.sig("tok_ready").sem, self.ready + g * (NTT - 1) + t + 1)
                else:
                    act.wait_ge(k.sig("unit_used").sem, self.u0 + 4 * g + 4)
                act.activation(self.dst[:, t, g * 512:(g + 1) * 512], k.ps[:, 4 + n % 4, :], self.func)\
                    .then_inc(k.sig("tok_taken").sem, 1)


class ConvLinear(Stage):

    def __init__(self, k, w, n_tiles, dst, cw, cb, off, spans=(LAT, CTX), pair=True, t0=0):
        self.k, self.w, self.n, self.dst, self.cw, self.cb = k, w, n_tiles, dst, cw, cb
        self.spans, self.pair, self.t0 = spans, pair, t0
        self.u0 = k.units(n_tiles)
        k.sig("unit_used").take(n_tiles)
        self.taken = k.sig("out_taken").take(n_tiles)
        self.conv = k.sig("conv_done").take(n_tiles)
        self.gated = k.sig("silu_done").take(n_tiles // 2 if pair else n_tiles)
        self.raw = k.at(off, 2, N)
        self.cv = k.at(off + 2 * N, 4, N)
        self.end = spans[-1][0] + spans[-1][1]

    def sync(self, sp):
        ring_loads(self.k, sp, lambda i, j, c: self.w[i + j + self.t0, :, 0:c], self.u0, self.n)

    def tensor(self, pe):
        k = self.k

        def unit(i, j):
            u = self.u0 + j
            pe.wait_ge(k.slot[u % SLOTS], slot_count(u, i))
            pe.wait_ge(k.sig("out_taken").sem, self.taken + j - 1 + i * 8)
            for s, (o, w) in enumerate(self.spans):
                for c in range(KD):
                    mm = pe.matmul(k.ps[:, 2 * s + j % 2, 0:w], lhsT=k.ring[:, u % SLOTS, c * P:(c + 1) * P],
                                   rhs=k.H[:, c, o:o + w], start=c == 0, stop=c == KD - 1)
            mm.then_inc(k.sig("unit_used").sem, 1)

        run_body(pe, self.n, 8, unit)

    def scalar(self, act):
        k = self.k

        def silu(i, j):
            if self.pair and j % 2 == 1:
                return
            act.wait_ge(k.sig("conv_done").sem, self.conv + j + 1 + i * 8)
            src = self.cv[:, j % 4, 0:self.end]
            out = src if self.pair else self.dst[j][:, 0:self.end]
            act.activation(out, src, ACT.Silu).then_inc(k.sig("silu_done").sem, 1)

        def unit(i, j):
            act.wait_ge(k.sig("unit_used").sem, self.u0 + j + 1 + i * 8)
            act.wait_ge(k.sig("conv_done").sem, self.conv + j - 1 + i * 8)
            for s, (o, w) in enumerate(self.spans):
                a = act.activation(self.raw[:, j % 2, o:o + w], k.ps[:, 2 * s + j % 2, 0:w], ACT.Copy)
            a.then_inc(k.sig("out_taken").sem, 1)
            silu(i, j)

        run_body(act, self.n, 8, unit)

    def vector(self, dve):
        k = self.k
        n_cols = 2 * FT if self.pair else 16

        def unit(i, j):
            dve.wait_ge(k.sig("out_taken").sem, self.taken + j + 1 + i * 8)
            ci = i * 8 + j + self.t0
            cw = [k.vec(self.cw)[:, bass.ds(ci + t * n_cols, 1)] for t in range(3)]
            cb = k.vec(self.cb)[:, bass.ds(ci, 1)]
            raw, cv = self.raw[:, j % 2, :], self.cv[:, j % 4, :]
            if not self.pair:
                dve.wait_ge(k.sig("silu_done").sem, self.gated + j - 3 + i * 8)
            dve.tensor_scalar(cv[:, 0:self.end], raw[:, 0:self.end], cw[1], cb, ALU.mult, ALU.add).then_inc(k.dve.count(), 1)
            dve.wait_ge(k.dve.sem, k.dve.value())
            for o, w in self.spans:
                a = dve.scalar_tensor_tensor(out=cv[:, o + 1:o + w], in0=raw[:, o:o + w - 1], scalar=cw[0],
                                             in1=cv[:, o + 1:o + w], op0=ALU.mult, op1=ALU.add)
            a.then_inc(k.dve.count(), 1)
            dve.wait_ge(k.dve.sem, k.dve.value())
            for o, w in self.spans:
                a = dve.scalar_tensor_tensor(out=cv[:, o:o + w - 1], in0=raw[:, o + 1:o + w], scalar=cw[2],
                                             in1=cv[:, o:o + w - 1], op0=ALU.mult, op1=ALU.add)
            a.then_inc(k.sig("conv_done").sem, 1)
            if self.pair and j % 2 == 1:
                dve.wait_ge(k.sig("conv_done").sem, self.conv + j + 1 + i * 8)
                dve.wait_ge(k.sig("silu_done").sem, self.gated + j // 2 + 1 + i * 4)
                dve.tensor_tensor(self.dst[:, i * 4 + j // 2, 0:self.end], self.cv[:, (j - 1) % 4, 0:self.end],
                                  self.cv[:, j % 4, 0:self.end], ALU.mult)

        run_body(dve, self.n, 8, unit, k.dve, 16)


class SpatialGate(Stage):

    def __init__(self, k, dram, G, U, off):
        self.k, self.dram, self.G, self.U = k, dram, G, U
        self.ws, self.bs = k.at(off, 8, P), k.at(off + 1024, 4, P)
        self.tmp = k.at(off + 1536, 2, 4, P)
        self.st = k.at(off + 2560, NTT, 6)
        self.mv = k.at(off + 2600, NTT, 2)
        self.sd = k.at(off + 2620, NTT)
        self.data = k.sig("stage_data").take(32)
        self.var = k.sig("variance_ready").take(1)
        self.root = k.sig("root_ready").take(1)
        self.vn = k.sig("gate_normed").take(NTT)
        self.mix = k.sig("mixed_ready").take(NTT)
        self.used = k.sig("mixed_taken").take(NTT)

    def gpsimd(self, pool):
        k = self.k
        pool.dma_start(self.ws, self.dram["sgu_w"]).then_inc(k.sig("stage_data").sem, 16)
        pool.dma_start(self.bs, self.dram["sgu_b"]).then_inc(k.sig("stage_data").sem, 16)

    def vector(self, dve):
        k, G = self.k, self.G
        for t in range(NTT):
            dve.bn_stats(self.st[:, t, :], G[:, t, :]).then_inc(k.dve.count(), 1)
        dve.wait_ge(k.dve.sem, k.dve.value())
        for t in range(NTT):
            a = dve.bn_aggr(self.mv[:, t, :], self.st[:, t, :])
        a.then_inc(k.sig("variance_ready").sem, 1)
        dve.wait_ge(k.sig("root_ready").sem, self.root + 1)
        dve.reciprocal(self.sd, self.sd).then_inc(k.dve.count(), 1)
        dve.wait_ge(k.dve.sem, k.dve.value())
        for t in range(NTT):
            dve.tensor_scalar(G[:, t, :], G[:, t, :], self.mv[:, t, 0:1], self.sd[:, t:t + 1],
                              ALU.subtract, ALU.mult).then_inc(k.sig("gate_normed").sem, 1)
        dve.wait_ge(k.sig("stage_data").sem, self.data + 32)
        for t in range(NTT):
            dve.wait_ge(k.sig("mixed_ready").sem, self.mix + t + 1)
            a = dve.tensor_tensor(self.tmp[:, t % 2], k.ps[:, t % 4, :].rearrange("p (a b) -> p a b", a=4),
                                  self.bs, ALU.add)
            a.then_inc(k.sig("mixed_taken").sem, 1)
            dve.wait_ge(k.sig("mixed_taken").sem, self.used + t + 1)
            dve.tensor_tensor(k.H[:, 4:8, t * P:(t + 1) * P], self.tmp[:, t % 2],
                              self.U[:, 0:4, t * P:(t + 1) * P], ALU.mult)

    def scalar(self, act):
        k = self.k
        act.wait_ge(k.sig("variance_ready").sem, self.var + 1)
        act.activation(self.sd, self.mv[:, :, 1], ACT.Sqrt, bias=EPS).then_inc(k.sig("root_ready").sem, 1)

    def tensor(self, pe):
        k = self.k
        pe.wait_ge(k.sig("stage_data").sem, self.data + 32)
        for t in range(NTT):
            pe.wait_ge(k.sig("gate_normed").sem, self.vn + t + 1)
            if t >= 4:
                pe.wait_ge(k.sig("mixed_taken").sem, self.used + t - 3)
            for g in range(8):
                half = (g % 2) * 64
                mm = pe.matmul(k.ps[half:half + 64, t % 4, (g // 2) * P:(g // 2 + 1) * P],
                               lhsT=self.G[:, t, g * 64:(g + 1) * 64], rhs=self.ws[:, g, :], start=True, stop=True)
            mm.then_inc(k.sig("mixed_ready").sem, 1)


class Neighbourhood(Stage):

    def __init__(self, k, dram, QK, V, off):
        self.k, self.dram, self.QK, self.V = k, dram, QK, V
        self.bt = k.at(off, 2, 16, 64)
        self.s = k.at(off + 2048, 2, N)
        self.p = k.at(off + 2048 + 2 * N, 2, N)
        self.pt = k.at(off + 2048 + 4 * N, 2, N)
        self.st = k.at(off + 2048 + 6 * N, 8, 4)
        self.its = [(h, q) for h in range(8) for q in range(NTT)]
        n = len(self.its)
        self.bias = k.sig("bias_loaded").take(32 * 8)
        self.masked = k.sig("bias_masked").take(8)
        self.s_rdy = k.sig("scores_ready").take(n)
        self.m_rdy = k.sig("max_ready").take(n)
        self.e_rdy = k.sig("exp_ready").take(n)
        self.p_rdy = k.sig("probs_ready").take(n)
        self.t_rdy = k.sig("turned_ready").take(n)
        self.t_tak = k.sig("turned_taken").take(n)
        self.o_rdy = k.sig("heads_ready").take(n)
        self.o_tak = k.sig("heads_taken").take(n)
        self.r_rdy = k.sig("recip_ready").take(n)

    def gpsimd(self, pool):
        k = self.k
        for h in range(8):
            if h >= 2:
                pool.wait_ge(k.sig("max_ready").sem, self.m_rdy + (h - 2) * NTT + LTT)
            for half in range(2):
                pool.dma_start(self.bt[half * 64:half * 64 + 64, h % 2, 1:15, :],
                               self.dram["rpb"][h, :, 1 - half:15 - half, :])\
                    .then_inc(k.sig("bias_loaded").sem, 16)
            pool.wait_ge(k.sig("bias_loaded").sem, self.bias + 32 * (h + 1))
            b = self.bt[:, h % 2, 1:15, :]
            pool.tensor_tensor(b, b, k.c("namask").unsqueeze(1).to_broadcast([P, 14, 64]), ALU.add)\
                .then_inc(k.sig("bias_masked").sem, 1)

    def stages(self, n, eng_scores, eng_turn, eng_out):
        for i in range(n + 2):
            if i < n:
                eng_scores(i)
            if 1 <= i <= n:
                eng_turn(i - 1)
            if i >= 2:
                eng_out(i - 2)

    def tensor(self, pe):
        k = self.k

        def scores(i):
            h, q = self.its[i]
            b, hp = (i % 2) * 2, (h % 2) * 64
            if i >= 2:
                pe.wait_ge(k.sig("max_ready").sem, self.m_rdy + i - 1)
            lhsT = self.QK[hp:hp + 64, h // 2, q * P:(q + 1) * P]
            if q < LTT:
                pe.matmul(k.ps[:, b, 0:T], lhsT=lhsT, rhs=self.QK[hp:hp + 64, 4 + h // 2, 0:T], start=True, stop=True)
            pe.matmul(k.ps[:, b + 1, 0:L], lhsT=lhsT, rhs=self.QK[hp:hp + 64, 4 + h // 2, T:N], start=True, stop=True)\
                .then_inc(k.sig("scores_ready").sem, 1)

        def turn(i):
            h, q = self.its[i]
            pe.wait_ge(k.sig("probs_ready").sem, self.p_rdy + i + 1)
            if i >= 1:
                pe.wait_ge(k.sig("turned_taken").sem, self.t_tak + i)
            for t in range(0 if q < LTT else LTT, NTT):
                mm = pe.transpose(k.ps[:, 4 + t // 4, (t % 4) * P:(t % 4 + 1) * P], self.p[:, i % 2, t * P:(t + 1) * P],
                                  k.c("ident"))
            mm.then_inc(k.sig("turned_ready").sem, 1)

        def out(i):
            h, q = self.its[i]
            hp = (h % 2) * 64
            pe.wait_ge(k.sig("turned_taken").sem, self.t_tak + i + 1)
            if i >= 2:
                pe.wait_ge(k.sig("heads_taken").sem, self.o_tak + i - 1)
            t0 = 0 if q < LTT else LTT
            for t in range(t0, NTT):
                mm = pe.matmul(k.ps[hp:hp + 64, 6 + i % 2, 0:P], lhsT=self.V[:, t, h * 64:(h + 1) * 64],
                               rhs=self.pt[:, i % 2, t * P:(t + 1) * P], start=t == t0, stop=t == NTT - 1)
            mm.then_inc(k.sig("heads_ready").sem, 1)

        self.stages(len(self.its), scores, turn, out)

    def vector(self, dve):
        k = self.k

        def scores(i):
            h, q = self.its[i]
            b = (i % 2) * 2
            s, st = self.s[:, i % 2, :], self.st[:, i % 8, :]
            dve.wait_ge(k.sig("scores_ready").sem, self.s_rdy + i + 1)
            if i >= 2:
                dve.wait_ge(k.sig("exp_ready").sem, self.e_rdy + i - 1)
            if q == 0:
                dve.wait_ge(k.sig("bias_masked").sem, self.masked + h + 1)
            if q < LTT:
                j0 = 7 - 2 * q
                dve.scalar_tensor_tensor(out=s[:, 0:T], in0=k.ps[:, b, 0:T], scalar=0.125,
                                         in1=self.bt[:, h % 2, j0:j0 + 8, :].rearrange("p a b -> p (a b)"),
                                         op0=ALU.mult, op1=ALU.add)
            lo = 0 if q < LTT else T
            dve.tensor_scalar(s[:, T:N], k.ps[:, b + 1, 0:L], 0.125, None, ALU.mult).then_inc(k.dve.count(), 1)
            dve.wait_ge(k.dve.sem, k.dve.value())
            dve.tensor_reduce(st[:, 0:1], s[:, lo:N], AX.X, ALU.max, negate=True).then_inc(k.sig("max_ready").sem, 1)

        def turn(i):
            st = self.st[:, i % 8, :]
            dve.wait_ge(k.sig("exp_ready").sem, self.e_rdy + i + 1)
            dve.reciprocal(st[:, 2:3], st[:, 1:2]).then_inc(k.sig("recip_ready").sem, 1)
            h, q = self.its[i]
            lo = 0 if q < LTT else T
            dve.wait_ge(k.sig("recip_ready").sem, self.r_rdy + i + 1)
            p = self.p[:, i % 2, lo:N]
            a = dve.tensor_scalar(p, p, st[:, 2:3], None, ALU.mult)
            a.then_inc(k.sig("probs_ready").sem, 1)

        def out(i):
            h, q = self.its[i]
            hp = (h % 2) * 64
            dve.wait_ge(k.sig("heads_ready").sem, self.o_rdy + i + 1)
            dve.tensor_copy(k.H[hp:hp + 64, h // 2, q * P:(q + 1) * P], k.ps[hp:hp + 64, 6 + i % 2, 0:P])\
                .then_inc(k.sig("heads_taken").sem, 1)

        n = len(self.its)
        for i in range(n + 2):
            if i < n:
                scores(i)
            if 1 <= i <= n:
                turn(i - 1)
            if i >= 2:
                out(i - 2)

    def scalar(self, act):
        k = self.k

        def scores(i):
            h, q = self.its[i]
            lo = 0 if q < LTT else T
            st = self.st[:, i % 8, :]
            act.wait_ge(k.sig("max_ready").sem, self.m_rdy + i + 1)
            if i >= 2:
                act.wait_ge(k.sig("turned_ready").sem, self.t_rdy + i - 1)
            act.activation(self.p[:, i % 2, lo:N], self.s[:, i % 2, lo:N], ACT.Exp, bias=st[:, 0:1],
                           accum_out=st[:, 1:2]).then_inc(k.sig("exp_ready").sem, 1)

        def turn(i):
            h, q = self.its[i]
            act.wait_ge(k.sig("turned_ready").sem, self.t_rdy + i + 1)
            if i >= 2:
                act.wait_ge(k.sig("heads_ready").sem, self.o_rdy + i - 1)
            if q < LTT:
                act.copy(self.pt[:, i % 2, 0:T], k.ps[:, 4, :])
            act.copy(self.pt[:, i % 2, T:N], k.ps[:, 5, 0:L]).then_inc(k.sig("turned_taken").sem, 1)

        self.stages(len(self.its), scores, turn, lambda i: None)


class Rope(Stage):

    def __init__(self, k, dram, view, tiles, rot, cos, off, load=True):
        self.k, self.dram, self.view, self.tiles, self.rot, self.cos = k, dram, view, tiles, rot, cos
        self.load = load
        self.cs = k.at(off, 2, T)
        self.tmp = k.at(off + 2 * T, 2, T)
        n = len(tiles)
        self.data = k.sig("stage_data").take(16)
        self.rdy = k.sig("rotated_ready").take(n)
        self.tak = k.sig("rotated_taken").take(n)

    def gpsimd(self, pool):
        k, o = self.k, BCON[self.cos][0]
        pool.dma_start(self.cs.rearrange("p a b -> p (a b)"), self.dram["consts"][:, o:o + 2 * T])\
            .then_inc(k.sig("stage_data").sem, 16)

    def tensor(self, pe):
        k = self.k
        for n, t in enumerate(self.tiles):
            if n >= 2:
                pe.wait_ge(k.sig("rotated_taken").sem, self.tak + n - 1)
            pe.matmul(k.ps[:, n % 2, :], lhsT=k.c(self.rot), rhs=self.view[:, t, 0:T], start=True, stop=True)\
                .then_inc(k.sig("rotated_ready").sem, 1)

    def vector(self, dve):
        k = self.k
        dve.wait_ge(k.sig("stage_data").sem, self.data + 16)
        for n, t in enumerate(self.tiles):
            x, tmp = self.view[:, t, 0:T], self.tmp[:, n % 2, :]
            dve.wait_ge(k.sig("rotated_ready").sem, self.rdy + n + 1)
            dve.tensor_tensor(x, x, self.cs[:, 0, :], ALU.mult)
            dve.tensor_tensor(tmp, k.ps[:, n % 2, :], self.cs[:, 1, :], ALU.mult).then_inc(k.sig("rotated_taken").sem, 1)
            dve.wait_ge(k.sig("rotated_taken").sem, self.tak + n + 1)
            dve.tensor_tensor(x, x, tmp, ALU.add)


class Retention(Stage):

    def __init__(self, k, dram, QK, V, O, head0, off):
        self.k, self.dram, self.QK, self.V, self.O, self.head0 = k, dram, QK, V, O, head0
        self.absd = k.at(off, 1408)
        self.F = k.at(off + 1408, 1408)
        self.tmp = k.at(off + 2816, P)
        self.dc = k.at(off + 2944, 1, T)
        self.s = k.at(off + 2944 + T, 2, NTT, T)
        self.data = k.sig("stage_data").take(16)
        self.strip = k.sig("strip_exp").take(4)
        self.s_rdy = k.sig("scores_ready").take(4 * NTT)
        self.s_tak = k.sig("decayed_ready").take(4 * NTT)
        self.o_rdy = k.sig("heads_ready").take(8)
        self.o_tak = k.sig("heads_taken").take(8)

    def gpsimd(self, pool):
        o = BCON["absd"][0]
        pool.dma_start(self.absd, self.dram["consts"][:, o:o + 1408]).then_inc(self.k.sig("stage_data").sem, 16)

    def scalar(self, act):
        k = self.k
        act.wait_ge(k.sig("stage_data").sem, self.data + 16)

        def strip(h):
            if h >= 1:
                act.wait_ge(k.sig("decayed_ready").sem, self.s_tak + h * NTT)
            lf = k.vec("lgd", self.head0 + h, self.head0 + h + 1)
            lb = k.vec("lgd", 8 + self.head0 + h, 8 + self.head0 + h + 1)
            act.activation(self.F[:, 0:768], self.absd[:, 0:768], ACT.Exp, scale=lb)
            act.activation(self.F[:, 768:1408], self.absd[:, 768:1408], ACT.Exp, scale=lf)
            act.activation(self.tmp, self.absd[:, 640:768], ACT.Exp, scale=lf).then_inc(k.sig("strip_exp").sem, 1)

        def out(h):
            for v in range(2):
                act.wait_ge(k.sig("heads_ready").sem, self.o_rdy + 2 * h + v + 1)
                act.copy(self.O[:, 2 * (self.head0 + h) + v, :], k.ps[:, 4 + (2 * h + v) % 4, :])\
                    .then_inc(k.sig("heads_taken").sem, 1)

        for h in range(5):
            if h < 4:
                strip(h)
            if h >= 1:
                out(h - 1)

    def vector(self, dve):
        k = self.k
        diag = self.F[:, 640:768]
        for h in range(4):
            dve.wait_ge(k.sig("strip_exp").sem, self.strip + h + 1)
            dve.tensor_tensor(diag, diag, k.c("le"), ALU.mult)
            dve.tensor_tensor(self.tmp, self.tmp, k.c("ge"), ALU.mult).then_inc(k.dve.count(), 1)
            dve.wait_ge(k.dve.sem, k.dve.value())
            dve.tensor_tensor(diag, diag, self.tmp, ALU.add).then_inc(k.dve.count(), 1)
            dve.wait_ge(k.dve.sem, k.dve.value())
            for t in range(NTT):
                n = h * NTT + t
                if t < LTT:
                    decay = self.F[:, 640 - P * t:640 - P * t + T]
                else:
                    c = t - LTT
                    decay = self.dc[:, 0, :]
                    dve.wait_ge(k.sig("decayed_ready").sem, self.s_tak + n)
                    dve.tensor_tensor(decay, self.F[:, 896 - P * c:896 - P * c + T],
                                      self.F[:, P - P * c:P - P * c + T], ALU.add).then_inc(k.dve.count(), 1)
                    dve.wait_ge(k.dve.sem, k.dve.value())
                dve.wait_ge(k.sig("scores_ready").sem, self.s_rdy + n + 1)
                if h >= 2:
                    dve.wait_ge(k.sig("heads_ready").sem, self.o_rdy + 2 * (h - 1))
                dve.scalar_tensor_tensor(out=self.s[:, h % 2, t, :], in0=k.ps[:, n % 4, :], scalar=float(P) ** -0.5,
                                         in1=decay, op0=ALU.mult, op1=ALU.mult).then_inc(k.sig("decayed_ready").sem, 1)

    def tensor(self, pe):
        k = self.k

        def scores(h):
            for t in range(NTT):
                n = h * NTT + t
                if n >= 4:
                    pe.wait_ge(k.sig("decayed_ready").sem, self.s_tak + n - 3)
                pe.matmul(k.ps[:, n % 4, :], lhsT=self.QK[:, 4 + h, t * P:(t + 1) * P], rhs=self.QK[:, h, 0:T],
                          start=True, stop=True).then_inc(k.sig("scores_ready").sem, 1)

        def out(h):
            for v in range(2):
                if h >= 2:
                    pe.wait_ge(k.sig("heads_taken").sem, self.o_tak + 2 * (h - 2) + v + 1)
                for t in range(NTT):
                    pe.wait_ge(k.sig("decayed_ready").sem, self.s_tak + h * NTT + t + 1)
                    mm = pe.matmul(k.ps[:, 4 + (2 * h + v) % 4, :],
                                   lhsT=self.V[:, t, h * 256 + v * P:h * 256 + (v + 1) * P],
                                   rhs=self.s[:, h % 2, t, :], start=t == 0, stop=t == NTT - 1)
                mm.then_inc(k.sig("heads_ready").sem, 1)

        scores(0)
        for h in range(4):
            if h < 3:
                scores(h + 1)
            out(h)


class GroupNorm(Stage):

    def __init__(self, k, view, groups, per, gain, off, center=False, after=1.0):
        self.k, self.view, self.groups, self.per, self.gain = k, view, groups, per, gain
        self.center, self.after = center, after
        self.sq = k.at(off, 2, per, T)
        self.sd = k.at(off + 2 * per * T, 2, T)
        self.rs = k.at(off + 2 * per * T + 2 * T, 2, T)
        n = groups
        self.mean = k.sig("mean_ready").take(n if center else 0)
        self.cent = k.sig("centred").take(n if center else 0)
        self.sq_b = k.sig("square_ready").take(n)
        self.ss_b = k.sig("sum_ready").take(n)
        self.sd_b = k.sig("root_ready").take(n)
        self.nrm = k.sig("normed").take(n)

    def tensor(self, pe):
        k, per = self.k, self.per

        def mean(g):
            if g >= 2:
                pe.wait_ge(k.sig("centred").sem, self.cent + g - 1)
            for t in range(per):
                mm = pe.matmul(k.ps[:, g % 2, :], lhsT=k.c("ones"), rhs=self.view[:, g * per + t, 0:T],
                               start=t == 0, stop=t == per - 1)
            mm.then_inc(k.sig("mean_ready").sem, 1)

        def square(g):
            pe.wait_ge(k.sig("square_ready").sem, self.sq_b + g + 1)
            if g >= 2:
                pe.wait_ge(k.sig("root_ready").sem, self.sd_b + g - 1)
            for t in range(per):
                mm = pe.matmul(k.ps[:, 2 + g % 2, :], lhsT=k.c("ones"), rhs=self.sq[:, g % 2, t, :],
                               start=t == 0, stop=t == per - 1)
            mm.then_inc(k.sig("sum_ready").sem, 1)

        for g in range(self.groups + 1):
            if g < self.groups and self.center:
                mean(g)
            if g >= 1:
                square(g - 1)

    def scalar(self, act):
        k, per = self.k, self.per
        for g in range(self.groups + 1):
            if g < self.groups:
                if self.center:
                    act.wait_ge(k.sig("centred").sem, self.cent + g + 1)
                if g >= 2:
                    act.wait_ge(k.sig("sum_ready").sem, self.ss_b + g - 1)
                for t in range(per):
                    a = act.activation(self.sq[:, g % 2, t, :], self.view[:, g * per + t, 0:T], ACT.Square)
                a.then_inc(k.sig("square_ready").sem, 1)
            if g >= 1:
                act.wait_ge(k.sig("sum_ready").sem, self.ss_b + g)
                if g >= 3:
                    act.wait_ge(k.sig("normed").sem, self.nrm + g - 2)
                act.activation(self.sd[:, (g - 1) % 2, :], k.ps[:, 2 + (g - 1) % 2, :], ACT.Sqrt, bias=EPS,
                               scale=1.0 / (per * P)).then_inc(k.sig("root_ready").sem, 1)

    def vector(self, dve):
        k, per = self.k, self.per
        for g in range(self.groups + 1):
            if g < self.groups and self.center:
                dve.wait_ge(k.sig("mean_ready").sem, self.mean + g + 1)
                for t in range(per):
                    x = self.view[:, g * per + t, 0:T]
                    a = dve.scalar_tensor_tensor(out=x, in0=k.ps[:, g % 2, :], scalar=-1.0 / (per * P), in1=x,
                                                 op0=ALU.mult, op1=ALU.add)
                a.then_inc(k.sig("centred").sem, 1)
            if g >= 1:
                b = (g - 1) % 2
                dve.wait_ge(k.sig("root_ready").sem, self.sd_b + g)
                dve.reciprocal(self.rs[:, b, :], self.sd[:, b, :]).then_inc(k.dve.count(), 1)
                dve.wait_ge(k.dve.sem, k.dve.value())
                if self.after != 1.0:
                    dve.tensor_scalar(self.rs[:, b, :], self.rs[:, b, :], self.after, None, ALU.mult).then_inc(k.dve.count(), 1)
                    dve.wait_ge(k.dve.sem, k.dve.value())
                for t in range(per):
                    x = self.view[:, (g - 1) * per + t, 0:T]
                    a = dve.scalar_tensor_tensor(out=x, in0=x, scalar=self.gain((g - 1) * per + t),
                                                 in1=self.rs[:, b, :], op0=ALU.mult, op1=ALU.mult)
                a.then_inc(k.sig("normed").sem, 1)


class GatedLinear(Stage):

    def __init__(self, k, w, n_tiles, x, dst, func, off, add=None, t0=0):
        self.k, self.w, self.n, self.x, self.dst, self.func, self.t0, self.add = k, w, n_tiles, x, dst, func, t0, add
        self.u0 = k.units(n_tiles)
        k.sig("unit_used").take(n_tiles)
        self.taken = k.sig("out_taken").take(n_tiles)
        self.conv = k.sig("conv_done").take(n_tiles)
        self.buf = k.at(off, 2, T)

    def sync(self, sp):
        ring_loads(self.k, sp, lambda i, j, c: self.w[i + j + self.t0, :, 0:c], self.u0, self.n)

    def tensor(self, pe):
        k = self.k

        def unit(i, j):
            u = self.u0 + j
            pe.wait_ge(k.slot[u % SLOTS], slot_count(u, i))
            pe.wait_ge(k.sig("out_taken").sem, self.taken + j - 1 + i * 8)
            for c in range(KD):
                mm = pe.matmul(k.ps[:, j % 2, :], lhsT=k.ring[:, u % SLOTS, c * P:(c + 1) * P],
                               rhs=k.H[:, c, 0:T], start=c == 0, stop=c == KD - 1)
            mm.then_inc(k.sig("unit_used").sem, 1)

        run_body(pe, self.n, 8, unit)

    def scalar(self, act):
        k = self.k

        def unit(i, j):
            act.wait_ge(k.sig("unit_used").sem, self.u0 + j + 1 + i * 8)
            act.wait_ge(k.sig("conv_done").sem, self.conv + j - 1 + i * 8)
            act.activation(self.buf[:, j % 2, :], k.ps[:, j % 2, :], self.func).then_inc(k.sig("out_taken").sem, 1)

        run_body(act, self.n, 8, unit)

    def vector(self, dve):
        k = self.k

        def unit(i, j):
            dve.wait_ge(k.sig("out_taken").sem, self.taken + j + 1 + i * 8)
            a = dve.tensor_tensor(self.dst[:, i * 8 + j, :], self.buf[:, j % 2, :], self.x[:, i * 8 + j, :], ALU.mult)
            if self.add is not None:
                a.then_inc(k.dve.count(), 1)
                dve.wait_ge(k.dve.sem, k.dve.value())
                a = dve.tensor_tensor(self.dst[:, i * 8 + j, :], self.dst[:, i * 8 + j, :],
                                      self.add[:, i * 8 + j, :], ALU.add)
            a.then_inc(k.sig("conv_done").sem, 1)

        run_body(dve, self.n, 8, unit, k.dve, 8 if self.add is not None else 0)


class DiffAttention(Stage):

    def __init__(self, k, Q, K, V, O, off):
        self.k, self.Q, self.K, self.V, self.O = k, Q, K, V, O
        self.p = k.at(off, 2, 2, N)
        self.pt = k.at(off + 4 * N, 2, N)
        self.st = k.at(off + 6 * N, 8, 8)
        self.lam = k.at(off + 6 * N + 64, 8)
        self.its = [(h, q) for h in range(8) for q in range(LTT)]
        n = len(self.its)
        self.lam_b = k.sig("lambda_steps").take(3)
        self.s_rdy = k.sig("scores_ready").take(2 * n)
        self.m_rdy = k.sig("max_ready").take(2 * n)
        self.e_rdy = k.sig("exp_ready").take(2 * n)
        self.p_rdy = k.sig("probs_ready").take(n)
        self.t_rdy = k.sig("turned_ready").take(n)
        self.t_tak = k.sig("turned_taken").take(n)
        self.o_rdy = k.sig("heads_ready").take(n)
        self.o_tak = k.sig("heads_taken").take(n)

    def tensor(self, pe):
        k, n = self.k, len(self.its)
        pe.wait_ge(k.sig("lambda_steps").sem, self.lam_b + 1)
        pe.matmul(k.ps[:, 7, 0:2], lhsT=k.c("ones"), rhs=self.lam[:, 0:2], start=True, stop=True)\
            .then_inc(k.sig("lambda_steps").sem, 1)

        def scores(i):
            h, q = self.its[i]
            for c in range(2):
                if i >= 1:
                    pe.wait_ge(k.sig("exp_ready").sem, self.e_rdy + 2 * (i - 1) + c + 1)
                for half in range(2):
                    mm = pe.matmul(k.ps[:, 2 * c + half, 0:384], lhsT=self.Q[c * 64:c * 64 + 64, h, q * P:(q + 1) * P],
                                   rhs=self.K[c * 64:c * 64 + 64, h, half * 384:(half + 1) * 384],
                                   start=True, stop=True)
                mm.then_inc(k.sig("scores_ready").sem, 1)

        def turn(i):
            pe.wait_ge(k.sig("probs_ready").sem, self.p_rdy + i + 1)
            if i >= 1:
                pe.wait_ge(k.sig("turned_taken").sem, self.t_tak + i)
            for t in range(NTT):
                mm = pe.transpose(k.ps[:, 4 + t // 4, (t % 4) * P:(t % 4 + 1) * P],
                                  self.p[:, i % 2, 0, t * P:(t + 1) * P], k.c("ident"))
            mm.then_inc(k.sig("turned_ready").sem, 1)

        def out(i):
            h, q = self.its[i]
            pe.wait_ge(k.sig("turned_taken").sem, self.t_tak + i + 1)
            if i >= 2:
                pe.wait_ge(k.sig("heads_taken").sem, self.o_tak + i - 1)
            elif i == 1:
                pe.wait_ge(k.sig("lambda_steps").sem, self.lam_b + 3)
            for t in range(NTT):
                mm = pe.matmul(k.ps[:, 6 + i % 2, 0:P], lhsT=self.V[:, t, h * P:(h + 1) * P],
                               rhs=self.pt[:, i % 2, t * P:(t + 1) * P], start=t == 0, stop=t == NTT - 1)
            mm.then_inc(k.sig("heads_ready").sem, 1)

        for i in range(n + 2):
            if i < n:
                scores(i)
            if 1 <= i <= n:
                turn(i - 1)
            if i >= 2:
                out(i - 2)

    def vector(self, dve):
        k, n = self.k, len(self.its)
        lam = self.lam
        v = k.vec("lam")
        dve.tensor_tensor(lam[:, 0:2], v[:, 0:4:2], v[:, 1:4:2], ALU.mult).then_inc(k.sig("lambda_steps").sem, 1)
        dve.wait_ge(k.sig("lambda_steps").sem, self.lam_b + 3)
        dve.tensor_tensor(lam[:, 4:5], lam[:, 3:4], lam[:, 2:3], ALU.subtract).then_inc(k.dve.count(), 1)
        dve.wait_ge(k.dve.sem, k.dve.value())
        dve.tensor_scalar(lam[:, 5:6], lam[:, 4:5], -LAM_INIT, None, ALU.add).then_inc(k.dve.count(), 1)
        dve.wait_ge(k.dve.sem, k.dve.value())

        def scores(i):
            for c in range(2):
                st = self.st[:, i % 8, :]
                dve.wait_ge(k.sig("scores_ready").sem, self.s_rdy + 2 * i + c + 1)
                dve.tensor_reduce(st[:, 6 + c:7 + c], k.ps[:, 2 * c:2 * c + 2, 0:384], AX.XY, ALU.max,
                                  negate=True).then_inc(k.dve.count(), 1)
                dve.wait_ge(k.dve.sem, k.dve.value())
                dve.tensor_scalar(st[:, c:c + 1], st[:, 6 + c:7 + c], 0.125, None, ALU.mult)\
                    .then_inc(k.sig("max_ready").sem, 1)

        def turn(i):
            st, p = self.st[:, i % 8, :], self.p[:, i % 2]
            dve.wait_ge(k.sig("exp_ready").sem, self.e_rdy + 2 * i + 2)
            dve.reciprocal(st[:, 4:6], st[:, 2:4]).then_inc(k.dve.count(), 1)
            dve.wait_ge(k.dve.sem, k.dve.value())
            dve.tensor_scalar(p[:, 1, :], p[:, 1, :], st[:, 5:6], lam[:, 5:6], ALU.mult, ALU.mult).then_inc(k.dve.count(), 1)
            dve.wait_ge(k.dve.sem, k.dve.value())
            dve.scalar_tensor_tensor(out=p[:, 0, :], in0=p[:, 0, :], scalar=st[:, 4:5], in1=p[:, 1, :],
                                     op0=ALU.mult, op1=ALU.add).then_inc(k.sig("probs_ready").sem, 1)

        for i in range(n + 1):
            if i < n:
                scores(i)
            if i >= 1:
                turn(i - 1)

    def scalar(self, act):
        k, n = self.k, len(self.its)
        act.wait_ge(k.sig("lambda_steps").sem, self.lam_b + 2)
        act.activation(self.lam[:, 2:4], k.ps[:, 7, 0:2], ACT.Exp).then_inc(k.sig("lambda_steps").sem, 1)

        def scores(i):
            st = self.st[:, i % 8, :]
            for c in range(2):
                act.wait_ge(k.sig("max_ready").sem, self.m_rdy + 2 * i + c + 1)
                if i >= 2:
                    act.wait_ge(k.sig("turned_ready").sem, self.t_rdy + i - 1)
                act.activation(self.p[:, i % 2, c, :].rearrange("p (a b) -> p a b", a=2),
                               k.ps[:, 2 * c:2 * c + 2, 0:384], ACT.Exp, bias=st[:, c:c + 1], scale=0.125,
                               accum_out=st[:, 2 + c:3 + c]).then_inc(k.sig("exp_ready").sem, 1)

        def turn(i):
            act.wait_ge(k.sig("turned_ready").sem, self.t_rdy + i + 1)
            if i >= 2:
                act.wait_ge(k.sig("heads_ready").sem, self.o_rdy + i - 1)
            act.copy(self.pt[:, i % 2, 0:T], k.ps[:, 4, :])
            act.copy(self.pt[:, i % 2, T:N], k.ps[:, 5, 0:L]).then_inc(k.sig("turned_taken").sem, 1)

        def out(i):
            h, q = self.its[i]
            act.wait_ge(k.sig("heads_ready").sem, self.o_rdy + i + 1)
            act.copy(self.O[:, h, q * P:(q + 1) * P], k.ps[:, 6 + i % 2, 0:P]).then_inc(k.sig("heads_taken").sem, 1)

        for i in range(n + 2):
            if i < n:
                scores(i)
            if 1 <= i <= n:
                turn(i - 1)
            if i >= 2:
                out(i - 2)


class StepSizes(Stage):

    def __init__(self, k, w, dt, A, nA, AT, off):
        self.k, self.w, self.dt, self.A, self.nA, self.AT = k, w, dt, A, nA, AT
        self.u0 = k.units(8)
        k.sig("unit_used").take(8)
        self.x, self.e, self.s, self.s2, self.r, self.dta, self.ndta = (
            k.at(off + 192 * j, NTT, 32) for j in range(7))
        self.ea = k.at(off + 192 * 7, 32)
        self.steps = k.sig("dt_steps").take(8)

    def sync(self, sp):
        ring_loads(self.k, sp, lambda i, j, c: self.w[0, :, 0:c], self.u0, 8, lambda j: 256)

    def tensor(self, pe):
        k = self.k
        u, st = self.u0, k.sig("dt_steps")
        for j in range(8):
            pe.wait_ge(k.slot[(u + j) % SLOTS], slot_count(u + j))
        for t in range(NTT):
            for c in range(KD):
                mm = pe.matmul(k.ps[:, 0, t * 32:(t + 1) * 32], lhsT=k.H[:, c, t * P:(t + 1) * P],
                               rhs=k.ring[:, u % SLOTS, c * 32:(c + 1) * 32], start=c == 0, stop=c == KD - 1)
        mm.then_inc(k.sig("unit_used").sem, 8)
        pe.wait_ge(st.sem, self.steps + 3)

        def total(t, d, parts):
            o = k.ps[:, 1, t * 32 + d * 16:t * 32 + (d + 1) * 16]
            for n, (m, x, tt) in enumerate(parts):
                mm = pe.matmul(o, lhsT=k.c(m), rhs=x[:, tt, d * 16:(d + 1) * 16], start=n == 0, stop=n == len(parts) - 1)
            return mm

        for t in range(LTT):
            total(t, 0, [("ge", self.dta, t)] + [("ones", self.dta, a) for a in range(t)])
            total(t, 1, [("lt", self.ndta, t)] + [("ones", self.ndta, a) for a in range(t)])
        for t in range(LTT, NTT):
            total(t, 0, [("gt", self.ndta, t)] + [("ones", self.ndta, a) for a in range(t + 1, NTT)])
            mm = total(t, 1, [("lt", self.ndta, t)] + [("ones", self.ndta, a) for a in range(t)])
        mm.then_inc(st.sem, 1)
        pe.wait_ge(st.sem, self.steps + 5)
        for t in range(LTT):
            mm = pe.transpose(k.ps[0:32, 2, t * P:(t + 1) * P], self.A[:, t, :], k.c("ident"))
        mm.then_inc(st.sem, 1)

    def scalar(self, act):
        k, st = self.k, self.k.sig("dt_steps")
        act.wait_ge(st.sem, self.steps + 1)
        act.activation(self.ea, k.vec("a_log"), ACT.Exp)
        act.activation(self.e, self.e, ACT.Exp, scale=-1.0).then_inc(st.sem, 1)

    def vector(self, dve):
        k, st = self.k, self.k.sig("dt_steps")
        x, e, s, s2, r = self.x, self.e, self.s, self.s2, self.r
        over = lambda v: v.unsqueeze(1).to_broadcast([P, NTT, 32])
        dve.wait_ge(k.sig("unit_used").sem, self.u0 + 8)
        dve.tensor_tensor(x, k.ps[:, 0, 0:192].rearrange("p (a b) -> p a b", a=NTT),
                          over(k.vec("dt_bias")), ALU.add).then_inc(k.dve.count(), 1)
        dve.wait_ge(k.dve.sem, k.dve.value())
        dve.tensor_scalar(r, x, -1.0, None, ALU.mult).then_inc(k.dve.count(), 1)
        dve.wait_ge(k.dve.sem, k.dve.value())
        dve.tensor_tensor(e, x, r, ALU.max).then_inc(st.sem, 1)
        dve.wait_ge(st.sem, self.steps + 2)
        dve.tensor_scalar(r, e, 2.0, None, ALU.add).then_inc(k.dve.count(), 1)
        dve.wait_ge(k.dve.sem, k.dve.value())
        dve.reciprocal(r, r).then_inc(k.dve.count(), 1)
        dve.wait_ge(k.dve.sem, k.dve.value())
        dve.tensor_tensor(s, e, r, ALU.mult).then_inc(k.dve.count(), 1)
        dve.wait_ge(k.dve.sem, k.dve.value())
        dve.tensor_tensor(s2, s, s, ALU.mult).then_inc(k.dve.count(), 1)
        dve.wait_ge(k.dve.sem, k.dve.value())
        dve.tensor_scalar(r, s2, 1.0 / 15, 1.0 / 13, ALU.mult, ALU.add).then_inc(k.dve.count(), 1)
        dve.wait_ge(k.dve.sem, k.dve.value())
        for n in (11, 9, 7, 5, 3, 1):
            dve.tensor_tensor(r, r, s2, ALU.mult).then_inc(k.dve.count(), 1)
            dve.wait_ge(k.dve.sem, k.dve.value())
            dve.tensor_scalar(r, r, 1.0 / n, None, ALU.add).then_inc(k.dve.count(), 1)
            dve.wait_ge(k.dve.sem, k.dve.value())
        dve.tensor_tensor(r, r, s, ALU.mult).then_inc(k.dve.count(), 1)
        dve.wait_ge(k.dve.sem, k.dve.value())
        dve.tensor_scalar(r, r, 2.0, None, ALU.mult).then_inc(k.dve.count(), 1)
        dve.wait_ge(k.dve.sem, k.dve.value())
        dve.scalar_tensor_tensor(out=self.dt, in0=x, scalar=0.0, in1=r, op0=ALU.max, op1=ALU.add).then_inc(k.dve.count(), 1)
        dve.wait_ge(k.dve.sem, k.dve.value())
        dve.tensor_tensor(self.ndta, self.dt, over(self.ea), ALU.mult).then_inc(k.dve.count(), 1)
        dve.wait_ge(k.dve.sem, k.dve.value())
        dve.tensor_scalar(self.dta, self.ndta, -1.0, None, ALU.mult).then_inc(st.sem, 1)
        dve.wait_ge(st.sem, self.steps + 4)
        a = k.ps[:, 1, 0:192].rearrange("p (a b) -> p a b", a=NTT)
        dve.tensor_scalar(self.nA, a, -1.0, None, ALU.mult)
        dve.tensor_copy(self.A, a).then_inc(st.sem, 1)
        dve.wait_ge(st.sem, self.steps + 6)
        dve.tensor_copy(self.AT[0:32, :], k.ps[0:32, 2, :])


class Scan(Stage):

    def __init__(self, k, g, bufs, Y, dt, nA, AT, off):
        self.k, self.g, self.Y, self.dt, self.nA, self.AT = k, g, Y, dt, nA, AT
        self.B, self.C, self.xs = bufs[0], bufs[1], bufs[2:4]
        self.xt = k.at(off, NTT, 256)
        self.cb = k.at(off + 1536, NTT, T)
        self.M = k.at(off + 4608, NTT, T)
        self.E = k.at(off + 7680, 4, 1024)
        self.dg = k.at(off + 11776, 2, LTT, 2 * P)
        n = 4 * NTT
        self.pre = k.sig("turned_ready").take(3 + NTT)
        self.pre_t = k.sig("turned_taken").take(3 + NTT)
        self.abc = k.sig("sums_spread").take(4)
        self.cap = k.sig("capped").take(4)
        self.e_rdy = k.sig("exp_ready").take(n)
        self.m_rdy = k.sig("decayed_ready").take(n)
        self.y_tak = k.sig("heads_taken").take(2)
        self.y_rdy = k.sig("heads_ready").take(n)

    def tensor(self, pe):
        k = self.k
        for b in range(3):
            for t in (2 * b, 2 * b + 1):
                for c in range(2):
                    mm = pe.transpose(k.ps[:, b, (t % 2) * 256 + c * P:(t % 2) * 256 + (c + 1) * P],
                                      self.xs[c][:, t * P:(t + 1) * P], k.c("ident"))
            mm.then_inc(k.sig("turned_ready").sem, 1)
        for t in range(NTT):
            if t >= 1:
                pe.wait_ge(k.sig("turned_taken").sem, self.pre_t + (t if t < 4 else t))
            pe.matmul(k.ps[:, (3 + t) % 4, :], lhsT=self.B[:, t * P:(t + 1) * P], rhs=self.C[:, 0:T],
                      start=True, stop=True).then_inc(k.sig("turned_ready").sem, 1)

        def spread(r):
            if r >= 1:
                pe.wait_ge(k.sig("exp_ready").sem, self.e_rdy + r * NTT)
            for d in range(2):
                col = d * 16 + self.g * 4 + r
                mm = pe.matmul(k.ps[:, 4 + d, :], lhsT=k.c("ident")[0:32, col:col + 1].to_broadcast([32, P]),
                               rhs=self.AT[0:32, :], start=True, stop=True)
            mm.then_inc(k.sig("sums_spread").sem, 1)

        def out(r):
            half = (r % 2) * 64
            for t in range(NTT):
                n = r * NTT + t
                pe.wait_ge(k.sig("decayed_ready").sem, self.m_rdy + n + 1)
                pe.matmul(k.ps[half:half + 64, 6 + r // 2, :], lhsT=self.xt[:, t, r * 64:(r + 1) * 64],
                          rhs=self.M[:, t, :], start=t == 0, stop=t == NTT - 1)\
                    .then_inc(k.sig("heads_ready").sem, 1)
                if t == 3 and r < 3:
                    spread(r + 1)

        spread(0)
        for r in range(4):
            out(r)

    def scalar(self, act):
        k = self.k
        for b in range(3):
            act.wait_ge(k.sig("turned_ready").sem, self.pre + b + 1)
            act.copy(self.xt[:, 2 * b:2 * b + 2, :], k.ps[:, b, :].rearrange("p (a b) -> p a b", a=2))\
                .then_inc(k.sig("turned_taken").sem, 1)
        for t in range(NTT):
            act.wait_ge(k.sig("turned_ready").sem, self.pre + 3 + t + 1)
            act.copy(self.cb[:, t, :], k.ps[:, (3 + t) % 4, :]).then_inc(k.sig("turned_taken").sem, 1)
        for r in range(4):
            f, b = self.g * 4 + r, 16 + self.g * 4 + r
            act.wait_ge(k.sig("capped").sem, self.cap + r + 1)
            act.activation(self.dg[:, r % 2], self.dg[:, r % 2], ACT.Exp)
            for t in range(NTT):
                n = r * NTT + t
                E = self.E[:, n % 4, :]
                if n >= 4:
                    act.wait_ge(k.sig("decayed_ready").sem, self.m_rdy + n - 3)
                bf, bb = self.nA[:, t, f:f + 1], self.nA[:, t, b:b + 1]
                if t < LTT:
                    if t < LTT - 1:
                        a = act.activation(E[:, (t + 1) * P:T], k.ps[:, 4, (t + 1) * P:T], ACT.Exp, bias=bf)
                    if t > 0:
                        a = act.activation(E[:, 0:t * P], k.ps[:, 5, 0:t * P], ACT.Exp, bias=bb)
                else:
                    act.activation(E[:, 0:T], k.ps[:, 4, :], ACT.Exp, bias=bf)
                    a = act.activation(E[:, T:2 * T], k.ps[:, 5, :], ACT.Exp, bias=bb)
                a.then_inc(k.sig("exp_ready").sem, 1)

    def vector(self, dve):
        k = self.k

        def cap(r):
            dve.wait_ge(k.sig("sums_spread").sem, self.abc + r + 1)
            for t in range(LTT):
                for d, m in ((0, "negf"), (1, "negb")):
                    col = d * 16 + self.g * 4 + r
                    a = dve.scalar_tensor_tensor(out=self.dg[:, r % 2, t, d * P:(d + 1) * P],
                                                 in0=k.ps[:, 4 + d, t * P:(t + 1) * P], scalar=self.nA[:, t, col:col + 1],
                                                 in1=k.c(m), op0=ALU.add, op1=ALU.min)
            a.then_inc(k.sig("capped").sem, 1)

        cap(0)
        dve.wait_ge(k.sig("turned_taken").sem, self.pre_t + 3 + NTT)
        for r in range(4):
            f, b = self.g * 4 + r, 16 + self.g * 4 + r
            for t in range(NTT):
                if t == 5 and r < 3:
                    cap(r + 1)
                n = r * NTT + t
                E, M, cb = self.E[:, n % 4, :], self.M[:, t, :], self.cb[:, t, :]
                df, db = self.dt[:, t, f:f + 1], self.dt[:, t, b:b + 1]
                dve.wait_ge(k.sig("exp_ready").sem, self.e_rdy + n + 1)
                if r >= 1:
                    dve.wait_ge(k.sig("heads_ready").sem, self.y_rdy + n - NTT + 1)
                if t < LTT:
                    o = t * P
                    dg = self.dg[:, r % 2, t]
                    e0, e1, span = dg[:, 0:P], dg[:, P:2 * P], slice(o, o + P)
                    if t < LTT - 1:
                        dve.scalar_tensor_tensor(out=M[:, o + P:T], in0=E[:, o + P:T], scalar=df, in1=cb[:, o + P:T],
                                                 op0=ALU.mult, op1=ALU.mult)
                else:
                    e0, e1, span = E[:, 0:T], E[:, T:2 * T], slice(0, T)
                dve.tensor_scalar(e0, e0, df, None, ALU.mult).then_inc(k.dve.count(), 1)
                if 0 < t < LTT:
                    dve.scalar_tensor_tensor(out=M[:, 0:o], in0=E[:, 0:o], scalar=db, in1=cb[:, 0:o],
                                             op0=ALU.mult, op1=ALU.mult)
                dve.wait_ge(k.dve.sem, k.dve.value())
                dve.scalar_tensor_tensor(out=e0, in0=e1, scalar=db, in1=e0, op0=ALU.mult, op1=ALU.add).then_inc(k.dve.count(), 1)
                dve.wait_ge(k.dve.sem, k.dve.value())
                dve.tensor_tensor(M[:, span], e0, cb[:, span], ALU.mult).then_inc(k.sig("decayed_ready").sem, 1)
            if r % 2 == 1:
                dve.wait_ge(k.sig("heads_ready").sem, self.y_rdy + (r + 1) * NTT)
                c = 2 * self.g + r // 2
                dve.scalar_tensor_tensor(out=self.Y[:, c, :], in0=self.xs[r // 2][:, 0:T],
                                         scalar=k.vec("d_skip", c, c + 1), in1=k.ps[:, 6 + r // 2, :],
                                         op0=ALU.mult, op1=ALU.add)


class Router(Stage):

    def __init__(self, k, w, rows, off):
        self.k, self.w, self.rows = k, w, rows
        self.u0 = k.units(8)
        k.sig("unit_used").take(8)
        self.sc, self.sel, self.ms, self.mr, self.wt = (k.at(off + 256 * j, LTT, NE) for j in range(5))
        self.cmp, self.cm2 = k.at(off + 1280, LTT, 8, 8), k.at(off + 1536, LTT, 8, 8)
        self.m8 = k.at(off + 1792, LTT, 8, 8)
        self.gs, self.gm, self.v8 = (k.at(off + 2048 + 32 * j, LTT, 8) for j in range(3))
        self.sm, self.rs = k.at(off + 2144, LTT), k.at(off + 2148, LTT)
        self.wT = k.at(off + 2152, T)
        self.steps = k.sig("router_steps").take(4)
        self.stored = k.sig("weights_stored").take(16)

    def sync(self, sp):
        k = self.k
        ring_loads(k, sp, lambda i, j, c: self.w[0, :, 0:c], self.u0, 8, lambda j: 512)

    def tensor(self, pe):
        k, st = self.k, self.k.sig("router_steps")
        for j in range(8):
            pe.wait_ge(k.slot[(self.u0 + j) % SLOTS], slot_count(self.u0 + j))
        for t in range(LTT):
            for c in range(KD):
                mm = pe.matmul(k.ps[:, 0, t * NE:(t + 1) * NE], lhsT=k.H[:, c, t * P:(t + 1) * P],
                               rhs=k.ring[:, self.u0 % SLOTS, c * NE:(c + 1) * NE], start=c == 0, stop=c == KD - 1)
        mm.then_inc(k.sig("unit_used").sem, 8)
        pe.wait_ge(st.sem, self.steps + 2)
        for t in range(LTT):
            mm = pe.transpose(k.ps[0:NE, 1, t * P:(t + 1) * P], self.wt[:, t, :], k.c("ident"))
        mm.then_inc(st.sem, 1)

    def scalar(self, act):
        k = self.k
        act.wait_ge(k.sig("unit_used").sem, self.u0 + 8)
        act.activation(self.sc, k.ps[:, 0, 0:256].rearrange("p (a b) -> p a b", a=LTT), ACT.Sigmoid)\
            .then_inc(k.sig("router_steps").sem, 1)

    def vector(self, dve):
        k, st = self.k, self.k.sig("router_steps")
        dve.wait_ge(st.sem, self.steps + 1)
        dve.tensor_tensor(self.sel, self.sc, k.vec("rbias").unsqueeze(1).to_broadcast([P, LTT, NE]), ALU.add).then_inc(k.dve.count(), 1)
        dve.wait_ge(k.dve.sem, k.dve.value())
        for t in range(LTT):
            for g in range(8):
                dve.max(self.m8[:, t, g, :], self.sel[:, t, g * 8:(g + 1) * 8]).then_inc(k.dve.count(), 1)
        dve.wait_ge(k.dve.sem, k.dve.value())
        dve.tensor_tensor(self.gs, self.m8[:, :, :, 0], self.m8[:, :, :, 1], ALU.add).then_inc(k.dve.count(), 1)
        dve.wait_ge(k.dve.sem, k.dve.value())
        for t in range(LTT):
            mine = self.gs[:, t, :].unsqueeze(2).to_broadcast([P, 8, 8])
            other = self.gs[:, t, :].unsqueeze(1).to_broadcast([P, 8, 8])
            dve.tensor_tensor(self.cmp[:, t], other, mine, ALU.is_gt)
            dve.tensor_tensor(self.cm2[:, t], other, mine, ALU.is_equal).then_inc(k.dve.count(), 1)
        dve.wait_ge(k.dve.sem, k.dve.value())
        bef = k.vec("before").rearrange("p (a b) -> p a b", a=8)
        for t in range(LTT):
            dve.tensor_tensor(self.cm2[:, t], self.cm2[:, t], bef, ALU.mult).then_inc(k.dve.count(), 1)
        dve.wait_ge(k.dve.sem, k.dve.value())
        dve.tensor_tensor(self.cmp, self.cmp, self.cm2, ALU.add).then_inc(k.dve.count(), 1)
        dve.wait_ge(k.dve.sem, k.dve.value())
        dve.tensor_reduce(self.gm, self.cmp, AX.X, ALU.add).then_inc(k.dve.count(), 1)
        dve.wait_ge(k.dve.sem, k.dve.value())
        dve.tensor_scalar(self.gm, self.gm, 3.5, NEG, ALU.is_gt, ALU.mult).then_inc(k.dve.count(), 1)
        dve.wait_ge(k.dve.sem, k.dve.value())
        for t in range(LTT):
            dve.tensor_tensor(self.ms[:, t].rearrange("p (a b) -> p a b", a=8),
                                         self.sel[:, t].rearrange("p (a b) -> p a b", a=8),
                                         self.gm[:, t].unsqueeze(2).to_broadcast([P, 8, 8]), ALU.add).then_inc(k.dve.count(), 1)
        dve.wait_ge(k.dve.sem, k.dve.value())
        for t in range(LTT):
            dve.max(self.v8[:, t], self.ms[:, t]).then_inc(k.dve.count(), 1)
        dve.wait_ge(k.dve.sem, k.dve.value())
        for t in range(LTT):
            dve.match_replace(out=self.mr[:, t], in_to_replace=self.v8[:, t], in_values=self.ms[:, t],
                                         imm_value=-BIG).then_inc(k.dve.count(), 1)
        dve.wait_ge(k.dve.sem, k.dve.value())
        dve.scalar_tensor_tensor(out=self.wt, in0=self.mr, scalar=-2e38, in1=self.sc, op0=ALU.is_lt,
                                 op1=ALU.mult).then_inc(k.dve.count(), 1)
        dve.wait_ge(k.dve.sem, k.dve.value())
        dve.tensor_reduce(self.sm, self.wt, AX.X, ALU.add).then_inc(k.dve.count(), 1)
        dve.wait_ge(k.dve.sem, k.dve.value())
        dve.reciprocal(self.rs, self.sm).then_inc(k.dve.count(), 1)
        dve.wait_ge(k.dve.sem, k.dve.value())
        for t in range(LTT):
            a = dve.tensor_scalar(self.wt[:, t], self.wt[:, t], self.rs[:, t:t + 1], 2.5, ALU.mult, ALU.mult)
        a.then_inc(st.sem, 1)
        dve.memset(self.wT[64:65, :], 1.0)
        dve.wait_ge(st.sem, self.steps + 3)
        dve.tensor_copy(self.wT[0:NE, :], k.ps[0:NE, 1, :]).then_inc(st.sem, 1)

    def gpsimd(self, pool):
        k = self.k
        pool.wait_ge(k.sig("router_steps").sem, self.steps + 4)
        pool.dma_start(self.rows, self.wT[0:NE + 1, :]).then_inc(k.sig("weights_stored").sem, 16)
        pool.wait_ge(k.sig("weights_stored").sem, self.stored + 16)


class Experts(Stage):

    TURN = 24

    def __init__(self, k, w, rows, acc, off):
        self.k, self.w, self.rows, self.acc = k, w, rows, acc
        self.n = NE + 1
        self.u0 = k.units(6 * self.n)
        k.sig("unit_used").take(6 * self.n)
        self.hid = k.at(off, 2, 2, T)
        self.sg = k.at(off + 2048, 2, T)
        self.tm = k.at(off + 3072, 2, T)
        self.wb = k.at(off + 4096, 2, T)
        n = self.n
        self.silu = k.sig("gate_silu").take(2 * n)
        self.up = k.sig("up_taken").take(2 * n)
        self.hr = k.sig("hidden_ready").take(n)
        self.at = k.sig("acc_taken").take(8 * n)
        self.dr = k.sig("down_ready").take(6 * n)
        self.wl = [k.sig(f"row_loaded{b}").take(16 * (n // 2 + 1)) for b in range(2)]

    def steps(self, eng, gate, down):
        gate(0, 0, 0, self.u0)
        with eng.Fori(0, (self.n - 1) // 4) as i:
            for j in range(4):
                u = self.u0 + 4 + 6 * j
                gate(j + 1, i, (j + 1) % 2, u)
                down(j, i, j % 2, u + 4)
        down(self.n - 1, 0, (self.n - 1) % 2, self.u0 + 6 * self.n - 2)

    def sync(self, sp):
        k = self.k
        ring_loads(k, sp, lambda i, j, c: self.w[i + j, :, 0:c], self.u0, 6 * self.n)

    def gpsimd(self, pool):
        k = self.k

        def load(e, i, b, u):
            pool.wait_ge(k.sig("hidden_ready").sem, self.hr + e - 1 + i * 4)
            pool.dma_start(self.wb[:, b, :], self.rows[bass.ds(e + i * 4, 1), :].to_broadcast([P, T]))\
                .then_inc(k.sig(f"row_loaded{b}").sem, 16)

        self.steps(pool, load, lambda e, i, b, u: None)

    def tensor(self, pe):
        k = self.k

        def gate(e, i, b, u):
            for f in range(2):
                pe.wait_ge(k.sig("up_taken").sem, self.up + 2 * (e - 1) + f + 1 + i * 8)
                for h in range(2):
                    un = u + 2 * f + h
                    pe.wait_ge(k.slot[un % SLOTS], slot_count(un, i * 3))
                    for c in range(KD):
                        mm = pe.matmul(k.ps[:, 2 * f + h, :], lhsT=k.ring[:, un % SLOTS, c * P:(c + 1) * P],
                                       rhs=k.H[:, c, 0:T], start=c == 0, stop=c == KD - 1)
                    mm.then_inc(k.sig("unit_used").sem, 1)

        def down(e, i, b, u):
            pe.wait_ge(k.sig("hidden_ready").sem, self.hr + e + 1 + i * 4)
            for half in range(2):
                pe.wait_ge(k.slot[(u + half) % SLOTS], slot_count(u + half, i * 3))
                for t in range(4):
                    n = 8 * e + 4 * half + t
                    pe.wait_ge(k.sig("acc_taken").sem, self.at + n - 3 + i * 32)
                    for f in range(2):
                        o = (t * 2 + f) * P
                        mm = pe.matmul(k.ps[:, 4 + t, :], lhsT=k.ring[:, (u + half) % SLOTS, o:o + P],
                                       rhs=self.hid[:, b, f, :], start=f == 0, stop=f == 1)
                    mm.then_inc(k.sig("down_ready" if t < 3 else "unit_used").sem, 1)

        self.steps(pe, gate, down)

    def scalar(self, act):
        k = self.k

        def gate(e, i, b, u):
            for f in range(2):
                act.wait_ge(k.sig("unit_used").sem, u + 2 * f + 2 + i * 24)
                act.wait_ge(k.sig("up_taken").sem, self.up + 2 * (e - 1) + f + 1 + i * 8)
                act.activation(self.sg[:, f, :], k.ps[:, 2 * f, :], ACT.Silu).then_inc(k.sig("gate_silu").sem, 1)

        self.steps(act, gate, lambda e, i, b, u: None)

    def vector(self, dve):
        k = self.k
        dve.memset(self.acc, 0.0).then_inc(k.dve.count(), 1)
        dve.wait_ge(k.dve.sem, k.dve.value())

        def gate(e, i, b, u):
            dve.wait_ge(k.sig("hidden_ready").sem, self.hr + e + i * 4)
            for f in range(2):
                dve.wait_ge(k.sig("gate_silu").sem, self.silu + 2 * e + f + 1 + i * 8)
                dve.tensor_tensor(self.tm[:, f, :], k.ps[:, 2 * f + 1, :], self.sg[:, f, :], ALU.mult)\
                    .then_inc(k.sig("up_taken").sem, 1)
            dve.wait_ge(k.sig("up_taken").sem, self.up + 2 * e + 2 + i * 8)
            dve.wait_ge(k.sig(f"row_loaded{b}").sem, self.wl[b] + 16 * (e // 2 + 1) + i * 32)
            for f in range(2):
                a = dve.tensor_tensor(self.hid[:, b, f, :], self.tm[:, f, :], self.wb[:, b, :], ALU.mult)
            a.then_inc(k.sig("hidden_ready").sem, 1)

        def down(e, i, b, u):
            dve.wait_ge(k.sig("acc_taken").sem, self.at + 8 * e + i * 32)
            for half in range(2):
                for t in range(4):
                    if t < 3:
                        dve.wait_ge(k.sig("down_ready").sem, self.dr + 6 * e + 3 * half + t + 1 + i * 24)
                    else:
                        dve.wait_ge(k.sig("unit_used").sem, u + half + 1 + i * 24)
                    c = 4 * half + t
                    dve.tensor_tensor(self.acc[:, c, :], k.ps[:, 4 + t, :], self.acc[:, c, :], ALU.add)\
                        .then_inc(k.sig("acc_taken").sem, 1)

        self.steps(dve, gate, down)


class LoadContext(Stage):

    def __init__(self, k, dram):
        self.k, self.dram = k, dram
        self.got = k.sig("context_loaded").take(16)

    def gpsimd(self, pool):
        k = self.k
        pool.dma_start(k.X[:, :, T:N], self.dram["ctx2T"]).then_inc(k.sig("context_loaded").sem, 16)
        pool.wait_ge(k.sig("context_loaded").sem, self.got + 16)


def plan(k, d):
    F = k.free
    st = [Load(k, d)]
    add = st.append
    add(Mods(k, 0, d["ada0"], "c0"))
    add(Norm(k, k.X, 0, 1, 0, k.H))
    QK, V, U, G = k.at(F, 8, N), k.at(F + 6144, NTT, 512), k.at(F + 9216, 4, N), k.at(F + 12288, NTT, 512)
    add(Linear(k, d["hyb_qku"], 8, k.H, QK))
    add(Linear(k, d["hyb_qku"], 4, k.H, U, func=ACT.Gelu_apprx_tanh, t0=8))
    add(TokLinear(k, d["hyb_vg"], 1, V))
    add(TokLinear(k, d["hyb_vg"], 1, G, func=ACT.Gelu_apprx_tanh, t0=4))
    add(SpatialGate(k, d, G, U, F + 15360))
    add(Neighbourhood(k, d, QK, V, F + 15360))
    Yo = k.at(F, KD, N)
    add(Linear(k, d["hyb_out"], 8, k.H, Yo))
    add(Norm(k, Yo, 0, 2, scratch=F + 6144))
    add(Norm(k, k.X, 0, 4, 3, k.H))
    hid = k.at(F, FT, N)
    add(ConvLinear(k, d["ffn_in0"], 2 * FT, hid, "cw0", "cb0", F + FT * N))
    add(Linear(k, d["ffn_out0"], 8, hid, k.H, kt=FT))
    add(Norm(k, k.H, 0, 5))
    add(Mods(k, 1, d["ada1"], "c0"))
    add(Norm(k, k.X, 1, 1, 0, k.H))
    O = k.at(F, 16, T)
    for half in range(2):
        q, QK, V = F + 8192, k.at(F + 8192, 8, N), k.at(F + 8192 + 6144, NTT, 1024)
        add(Linear(k, d["ret_qk"], 8, k.H, QK, t0=8 * half))
        add(Rope(k, d, QK, range(8), "rot64", "cos_r", F + 20480))
        add(TokLinear(k, d["ret_v"], 2, V, t0=8 * half))
        add(Retention(k, d, QK, V, O, 4 * half, F + 20480))
    add(GroupNorm(k, O, 8, 2, lambda t: k.vec("gn_g", t, t + 1), F + 8192, center=True))
    add(GatedLinear(k, d["ret_g"], 16, O, O, ACT.Silu, F + 8192))
    Yo = k.at(F + 8192, KD, N)
    add(Linear(k, d["ret_out"], 8, O, Yo, kt=16, spans=(LAT,)))
    add(Norm(k, Yo, 1, 2, spans=(LAT,), scratch=F + 8192 + 6144))
    add(Norm(k, k.X, 1, 4, 3, k.H, spans=(LAT,)))
    add(ConvLinear(k, d["ffn_in1"], 2 * FT, hid, "cw1", "cb1", F + FT * N, spans=(LAT,)))
    add(Linear(k, d["ffn_out1"], 8, hid, k.H, kt=FT, spans=(LAT,)))
    add(Norm(k, k.H, 1, 5, spans=(LAT,)))
    add(LoadContext(k, d))
    add(Mods(k, 2, d["ada2"], "c2"))
    add(Norm(k, k.X, 2, 1, 0, k.H))
    O, Y = k.at(F, KD, T), k.at(F + 4096, KD, T)
    Q, K, V = k.at(F + 4096, KD, T), k.at(F + 8192, KD, N), k.at(F + 14336, NTT, 1024)
    add(Linear(k, d["dif_qk"], 8, k.H, Q, spans=(LAT,)))
    add(Linear(k, d["dif_qk"], 8, k.H, K, t0=8))
    add(Rope(k, d, Q, range(8), "rot32", "cos_d", F + 20480))
    add(Rope(k, d, K, range(8), "rot32", "cos_d", F + 20480))
    add(TokLinear(k, d["dif_v"], 2, V))
    add(DiffAttention(k, Q, K, V, O, F + 20480))
    add(GroupNorm(k, O, 8, 1, lambda t: k.vec("subln"), F + 8192, after=1.0 - LAM_INIT))
    dt, A, nA, AT = k.at(F + 8192, NTT, 32), k.at(F + 8384, NTT, 32), k.at(F + 8576, NTT, 32), k.at(F + 8768, T)
    add(StepSizes(k, d["w_dt"], dt, A, nA, AT, F + 9280))
    bufs = [k.at(F + 9280 + N * j, N) for j in range(4)]
    for g in range(4):
        add(ConvLinear(k, d["xbc"], 4, bufs, "scw", "scb", F + 9280 + 4 * N, pair=False, t0=4 * g))
        add(Scan(k, g, bufs, Y, dt, nA, AT, F + 9280 + 4 * N))
    add(GatedLinear(k, d["z"], 8, Y, Y, ACT.Silu, F + 8192))
    add(GroupNorm(k, Y, 4, 2, lambda t: k.vec("ssd_norm", t, t + 1), F + 8192))
    YA, YS = k.at(F + 8192, KD, T), k.at(F + 12288, KD, T)
    add(Linear(k, d["w_ba"], 8, O, YA, spans=(LAT,)))
    add(GatedLinear(k, d["gates"], 8, YA, YA, ACT.Sigmoid, F + 16384))
    add(Linear(k, d["w_bs"], 8, Y, YS, spans=(LAT,)))
    add(GatedLinear(k, d["gates"], 8, YS, YS, ACT.Sigmoid, F + 16384, add=YA, t0=8))
    Yo = k.at(F, KD, T)
    add(Linear(k, d["w_out2"], 8, YS, Yo, spans=(LAT,)))
    add(Norm(k, Yo, 2, 2, spans=(LAT,), scratch=F + 16384))
    add(Norm(k, k.X, 2, 4, 3, k.H, spans=(LAT,)))
    add(Router(k, d["w_router"], d["rows"], F))
    acc = k.at(F, KD, T)
    add(Experts(k, d["w_exp"], d["rows"], acc, F + 4096))
    add(Norm(k, acc, 2, 5, spans=(LAT,), scratch=F + 4096))
    return st


def build(nc, d, out, upto=None, dump=None):
    with ExitStack() as ctx:
        k = Core(nc, ctx)
        stages = plan(k, d)
        if upto is not None:
            stages = stages[:upto]
        met = ctx.enter_context(nc.semaphore("stage_met"))
        stored = ctx.enter_context(nc.semaphore("output_stored"))
        own = ctx.enter_context(nc.semaphore("vector_own"))
        block = ctx.enter_context(nc.Block(no_gpsimd_drain=True))

        def run(eng, part):
            for n, s in enumerate(stages):
                part(s, eng)
                eng.drain().then_inc(met, 1)
                eng.wait_ge(met, 4 * (n + 1))

        @block.sync
        def _(sp):
            for s in stages:
                s.sync(sp)
            sp.wait_ge(met, 4 * len(stages))
            src = k.X[:, :, 0:T] if dump is None else dump(k)
            sp.dma_start(out, src).then_inc(stored, 16)
            sp.wait_ge(stored, 16)

        @block.tensor
        def _(pe):
            run(pe, lambda s, e: s.tensor(e))

        @block.vector
        def _(dve):
            k.dve = Chain(own)
            run(dve, lambda s, e: s.vector(e))

        @block.scalar
        def _(act):
            run(act, lambda s, e: s.scalar(e))

        @block.gpsimd
        def _(pool):
            run(pool, lambda s, e: s.gpsimd(e))



def cols(v):
    v = np.asarray(v).reshape(-1, P)
    return v.T


def tiles(w):
    K, n = w.shape
    return np.ascontiguousarray(w.reshape(K // P, P, n // P, P).transpose(2, 1, 0, 3)).reshape(n // P, P, K)


def feature_major(x):
    return np.ascontiguousarray(x.T.reshape(KD, P, -1).transpose(1, 0, 2))


def constants():
    c = np.zeros((P, NCONALL), np.float32)
    r, j = np.arange(P)[:, None], np.arange(P)[None, :]

    def put(name, v):
        o, w = (CON.get(name) or BCON.get(name))
        c[:, o:o + w] = v

    put("ident", r == j)
    put("ones", 1.0)
    put("ge", j >= r)
    put("le", j <= r)
    put("lt", r < j)
    put("gt", r > j)
    put("negf", np.where(j >= r, 0.0, NEG))
    put("negb", np.where(j <= r, 0.0, NEG))
    for name, half in (("rot64", 64), ("rot32", 32)):
        m = np.zeros((P, P), np.float32)
        for o in range(P):
            if o % (2 * half) < half:
                m[o + half, o] = -1.0
            else:
                m[o - half, o] = 1.0
        put(name, m)
    q = np.arange(P) % GRID_W
    c0 = np.clip(q - 8, 0, GRID_W - 16)
    kc = np.arange(GRID_W)
    put("namask", np.where((kc[None] >= c0[:, None]) & (kc[None] < c0[:, None] + 16), 0.0, NEG))
    put("absd", np.abs(np.arange(1408)[None, :] - 640 - r))
    t = np.arange(T)
    row, col = (t // GRID_W).astype(np.float32), (t % GRID_W).astype(np.float32)
    for tag, nf, base, dim in (("r", 32, 10000.0, 128), ("d", 16, 10000.0, 64)):
        inv = (np.float32(base) ** (-np.arange(nf, dtype=np.float32) / np.float32(nf))).astype(np.float32)
        ang = np.concatenate([row[:, None] * inv, col[:, None] * inv], -1).astype(np.float32)
        full = np.tile(ang, (1, P // (dim // 2))).T
        put(f"cos_{tag}", np.cos(full))
        put(f"sin_{tag}", np.sin(full))
    return c


def lay_out(a):
    f = np.float32
    a = {n: np.asarray(v) for n, v in a.items()}
    rep = lambda v: np.broadcast_to(np.asarray(v).reshape(1, -1), (P, np.asarray(v).size))
    vecs = np.zeros((P, NVEC), f)

    def put(name, v):
        o, w = VEC[name]
        vecs[:, o:o + w] = v

    pair = lambda x, y: np.stack([cols(x), cols(y)], -1).reshape(P, 16)
    put("c0", pair(a["c"][0], a["c_ctx"]))
    put("c2", pair(a["c_2"][0], a["c_ctx_2"]))
    put("ada_b0", cols(a["ada_b"][0]))
    put("ada_b1", cols(a["ada_b"][1]))
    put("ada_b2", cols(a["b_ada_2"][0]))
    put("norm0", cols(a["norm_g"][0].reshape(-1)))
    put("norm1", cols(a["norm_g"][1].reshape(-1)))
    put("norm2", np.concatenate([cols(a[n + "_2"][0]) for n in ("g_pre_mix", "g_post_mix", "g_pre_ffn", "g_post_ffn")], 1))
    gu = np.arange(2 * FT).reshape(2, FT).T.reshape(-1)
    for l in range(2):
        put(f"cw{l}", np.concatenate([cols(a["ffn_conv_w"][l][t])[:, gu] for t in range(3)], 1))
        put(f"cb{l}", cols(a["ffn_conv_b"][l])[:, gu])
    put("gn_g", cols(a["ret_gn_g"][0]))
    put("subln", cols(a["g_attn_subln_2"][0]))
    put("ssd_norm", cols(a["g_ssd_norm_2"][0]))
    put("d_skip", cols(np.repeat(a["d_skip_2"][0], 64)))
    order = np.array([[8 + g, 12 + g, 2 * g, 2 * g + 1] for g in range(4)]).reshape(-1)
    put("scw", np.concatenate([cols(a["conv_w_2"][0][t])[:, order] for t in range(3)], 1))
    put("scb", cols(a["conv_b_2"][0])[:, order])
    put("lgd", rep(a["ret_log_decay"][0]))
    put("dt_bias", rep(a["dt_bias_2"][0]))
    put("a_log", rep(a["a_log_2"][0]))
    put("rbias", rep(a["router_bias_2"][0]))
    for n, name in enumerate(("lam_q1_2", "lam_k1_2", "lam_q2_2", "lam_k2_2")):
        vecs[0:64, VEC["lam"][0] + n] = a[name][0]
    put("before", rep((np.arange(8)[None, :] < np.arange(8)[:, None]).astype(f)))

    d = {"vecs": vecs, "consts": constants(), "xT": feature_major(a["x"][0]), "ctxT": feature_major(a["ctx"][0]),
         "ctx2T": feature_major(a["ctx_2"][0])}
    d["ada0"], d["ada1"], d["ada2"] = tiles(a["ada_w"][0]), tiles(a["ada_w"][1]), tiles(a["w_ada_2"][0])
    w = a["hyb_w_in"][0]
    d["hyb_qku"] = tiles(np.concatenate([w[:, 0:1024], w[:, 1536:2048]], 1))
    d["hyb_vg"] = tiles(np.concatenate([w[:, 1024:1536], w[:, 2048:2560]], 1))
    rpb = np.zeros((8, 15, 127), f)
    rpb[:, :, 48:79] = a["na_rpb"][0]
    col = np.arange(GRID_W)
    d["rpb"] = np.ascontiguousarray(rpb[:, :, 63 - col[:, None] + col[None, :]].transpose(0, 2, 1, 3))
    d["sgu_w"] = np.ascontiguousarray(a["sgu_w"][0].transpose(2, 0, 1))
    b = a["sgu_b"][0].reshape(4, 2, P).transpose(1, 0, 2)
    d["sgu_b"] = np.ascontiguousarray(np.repeat(b, 64, axis=0))
    d["hyb_out"] = tiles(a["hyb_w_out"][0])
    for l in range(2):
        d[f"ffn_in{l}"] = tiles(a["ffn_w_in"][l])[gu]
        d[f"ffn_out{l}"] = tiles(a["ffn_w_out"][l])
    w = a["ret_w_in"][0]
    q, kk = tiles(w[:, 0:1024]), tiles(w[:, 1024:2048])
    d["ret_qk"] = np.concatenate([q[0:4], kk[0:4], q[4:8], kk[4:8]])
    d["ret_v"], d["ret_g"] = tiles(w[:, 2048:4096]), tiles(w[:, 4096:6144])
    halves = lambda t: np.ascontiguousarray(t.reshape(t.shape[0], P, 2, UC).transpose(0, 2, 1, 3)).reshape(-1, P, UC)
    d["ret_out"] = halves(tiles(a["ret_w_out"][0]))
    w = a["w_in_2"][0]
    d["dif_qk"], d["dif_v"], d["z"] = tiles(w[:, 0:2048]), tiles(w[:, 2048:3072]), tiles(w[:, 3072:4096])
    d["xbc"] = tiles(w[:, 4096:6144])[order]
    d["w_dt"] = np.ascontiguousarray(w[:, 6144:6176].reshape(KD, P, 32).transpose(1, 0, 2)).reshape(1, P, 256)
    d["gates"] = tiles(w[:, 6176:8224])
    d["w_ba"], d["w_bs"], d["w_out2"] = (tiles(a[n + "_2"][0]) for n in ("w_branch_attn", "w_branch_ssd", "w_out"))
    d["w_router"] = np.ascontiguousarray(a["w_router_2"][0].reshape(KD, P, NE).transpose(1, 0, 2)).reshape(1, P, 512)
    wg = np.concatenate([a["w_e_gate_2"][0], a["w_sh_gate_2"]])
    wu = np.concatenate([a["w_e_up_2"][0], a["w_sh_up_2"]])
    wd = np.concatenate([a["w_e_down_2"][0], a["w_sh_down_2"]])
    n = NE + 1
    up = np.stack([wg, wu], 1).reshape(n, 2, KD, P, 2, P).transpose(0, 4, 1, 3, 2, 5).reshape(n, 4, P, UC)
    down = wd.reshape(n, 2, P, 2, 4, P).transpose(0, 3, 2, 4, 1, 5).reshape(n, 2, P, UC)
    e = np.empty((6 * n, P, UC), f)
    e[0:4] = up[0]
    mid = e[4:6 * n - 2].reshape(n - 1, 6, P, UC)
    mid[:, 0:4], mid[:, 4:6] = up[1:], down[:-1]
    e[6 * n - 2:] = down[-1]
    d["w_exp"] = e
    return d


def kernel(**inputs):
    import concourse.bacc as bacc
    from concourse.bass_utils import run_bass_kernel_spmd

    nc = bacc.Bacc("TRN2", target_bir_lowering=False, num_devices=1)
    d = lay_out(inputs)
    dram = {n: nc.dram_tensor(n, v.shape, F32, kind="ExternalInput").ap() for n, v in d.items()}
    dram["rows"] = nc.dram_tensor("expert_rows", [NE + 1, T], F32, kind="Internal").ap()
    out = nc.dram_tensor("out", [P, KD, T], F32, kind="ExternalOutput").ap()
    build(nc, dram, out)
    r = run_bass_kernel_spmd(nc, [d], core_ids=[0])
    y = np.asarray(r.results[0]["out"])
    return np.ascontiguousarray(y.transpose(2, 1, 0)).reshape(1, T, D)
```

```python
from contextlib import ExitStack

import numpy as np

import concourse.bass as bass
from concourse import mybir

F32 = mybir.dt.float32
I32 = mybir.dt.int32
U32 = mybir.dt.uint32
ALU = mybir.AluOpType
ACT = mybir.ActivationFunctionType
AX = mybir.AxisListType

P = 128
D = 1024
KD = D // P
T = 512
L = 256
N = T + L
NTT = N // P
LTT = T // P
GRID_W = 64
EPS = 1e-6
NEG = -1e30
DFF = 2816
FT = DFF // P
NE = 64
MINB = T * 8 // P
MAXB = MINB + NE
SLOTS = 8
UC = 1024
LAM_INIT = 0.2
LAT, CTX = (0, T), (T, L)
BIG = 3e38


VEC = {}
_n = 0
for _name, _w in (
    ("c0", 16), ("c2", 16), ("ada_b0", 48), ("ada_b1", 48), ("ada_b2", 48),
    ("norm0", 32), ("norm1", 32), ("norm2", 32),
    ("cw0", 3 * 2 * FT), ("cb0", 2 * FT), ("cw1", 3 * 2 * FT), ("cb1", 2 * FT),
    ("gn_g", 16), ("subln", 1), ("ssd_norm", 8), ("d_skip", 8), ("scw", 48), ("scb", 16),
    ("lgd", 16), ("dt_bias", 32), ("a_log", 32), ("rbias", 64), ("lam", 4), ("before", 64),
):
    VEC[_name] = (_n, _w)
    _n += _w
NVEC = _n

CON = {}
_n = 0
for _name, _w in (("ident", P), ("ones", P), ("ge", P), ("le", P), ("lt", P), ("gt", P), ("negf", P), ("negb", P),
                  ("rot64", P), ("rot32", P), ("namask", 64)):
    CON[_name] = (_n, _w)
    _n += _w
NCON = _n
BCON = {}
for _name, _w in (("absd", 1408), ("cos_r", T), ("sin_r", T), ("cos_d", T), ("sin_d", T), ("iota", P + LTT)):
    BCON[_name] = (_n, _w)
    _n += _w
NCONALL = _n


INTERNAL = {"h_rows": [T, D], "y_rows": [MAXB * P, D]}
MOE_PRIMED = ("gate_up_made", "down_made", "x_turned", "x_taken", "h_made", "hT_taken", "h_turned", "silu_made",
              "y_taken0", "y_taken1")
PRIMED = ("out_taken", "conv_done", "silu_done")
PRIME = 4


class Signal:

    def __init__(self, sem, n):
        self.sem, self.n = sem, n

    def take(self, k):
        base = self.n
        self.n += k
        return base


class Chain:

    def __init__(self, sem):
        self.sem, self.n, self.i, self.per, self.n0 = sem, 0, None, 0, 0

    def count(self):
        self.n += 1
        return self.sem

    def value(self):
        return self.n if self.i is None else self.i * self.per + self.n

    def enter(self, i, per):
        self.i, self.per, self.n0 = i, per, self.n

    def leave(self, turns):
        assert self.n - self.n0 == self.per, (self.n - self.n0, self.per)
        self.n = self.n0 + self.per * turns
        self.i = None


class Core:

    def __init__(self, nc, ctx):
        self.nc = nc
        self.words = 53208
        self.sb = ctx.enter_context(nc.sbuf_tensor("arena", [P, self.words], F32))
        self.ps = ctx.enter_context(nc.psum_tensor("ps", [P, 8, 512], F32))
        self.ctx = ctx
        self.signals = {}
        self.unit = 0
        o = 0
        self.X, o = self.at(o, KD, N), o + KD * N
        self.H, o = self.at(o, KD, N), o + KD * N
        self.ring, o = self.at(o, SLOTS, UC), o + SLOTS * UC
        self.vecs, o = self.at(o, NVEC), o + NVEC
        self.con, o = self.at(o, NCON), o + NCON
        self.mods, o = self.at(o, 3, 2, 6, 8), o + 288
        self.csil, o = self.at(o, 8, 2), o + 16
        self.small, o = self.at(o, 64), o + 64
        self.free = o
        self.slot = [ctx.enter_context(nc.semaphore(f"slot_loaded{i}")) for i in range(SLOTS)]

    def at(self, off, *dims):
        n = int(np.prod(dims))
        assert off + n <= self.words, (off, n)
        v = self.sb[:, off:off + n]
        names = "abcd"[:len(dims)]
        if len(dims) > 1:
            v = v.rearrange(f"p ({' '.join(names)}) -> p {' '.join(names)}", **dict(zip(names[1:], dims[1:])))
        return v

    def place(self, *shapes):
        out, o = [], self.free
        for s in shapes:
            out.append(self.at(o, *s))
            o += int(np.prod(s))
        return out

    def sig(self, name):
        if name not in self.signals:
            self.signals[name] = Signal(self.ctx.enter_context(self.nc.semaphore(name)), PRIME if name in PRIMED else 0)
        return self.signals[name]

    def vec(self, name, a=0, b=None):
        o, w = VEC[name]
        return self.vecs[:, o + a:o + (w if b is None else b)]

    def c(self, name):
        o, w = CON[name]
        return self.con[:, o:o + w]

    def units(self, n):
        u = self.unit
        self.unit += n
        return u


class Stage:
    def sync(self, sp): pass
    def tensor(self, pe): pass
    def vector(self, dve): pass
    def scalar(self, act): pass
    def gpsimd(self, pool): pass


def turns(n, body, peel=False):
    first = body if peel and n >= body else 0
    t = (n - first) // body
    return first, t, n - first - t * body


def ring_loads(k, sp, w, u0, n, cols=lambda j: UC, period=8):
    used = k.sig("unit_used")

    def load(i, j):
        u = u0 + j
        if not (isinstance(i, int) and u + i - SLOTS < 0):
            sp.wait_ge(used.sem, u + i - SLOTS + 1)
        c = cols(j)
        sp.dma_start(k.ring[:, u % SLOTS, 0:c], w(i, j, c)).then_inc(k.slot[u % SLOTS], 16)

    first, t, tail = turns(n, period, peel=u0 < SLOTS)
    for j in range(first):
        load(0, j)
    if t > 1:
        with sp.Fori(0, t) as i:
            for j in range(period):
                load(i * period + first, j)
    elif t == 1:
        for j in range(period):
            load(first, j)
    for j in range(tail):
        load(first + t * period, j)


def slot_count(u, i=0):
    return (u // SLOTS + 1) * 16 + i * 16



class Load(Stage):

    def __init__(self, k, dram):
        self.k, self.dram = k, dram
        self.got = k.sig("inputs_loaded")
        self.got.take(64)

    def sync(self, sp):
        k, d = self.k, self.dram
        sp.dma_start(k.vecs, d["vecs"]).then_inc(self.got.sem, 16)
        sp.dma_start(k.con, d["consts"][:, 0:NCON]).then_inc(self.got.sem, 16)
        sp.dma_start(k.X[:, :, 0:T], d["xT"]).then_inc(self.got.sem, 16)
        sp.dma_start(k.X[:, :, T:N], d["ctxT"]).then_inc(self.got.sem, 16)

    def tensor(self, pe):
        pe.wait_ge(self.got.sem, 64)

    def vector(self, dve):
        k = self.k
        for n, name in enumerate(PRIMED):
            dve.memset(k.small[:, n:n + 1], 0.0).then_inc(k.sig(name).sem, PRIME)
        dve.wait_ge(self.got.sem, 64)

    def scalar(self, act):
        act.wait_ge(self.got.sem, 64)

    def gpsimd(self, pool):
        pool.wait_ge(self.got.sem, 64)


class Mods(Stage):

    def __init__(self, k, layer, w, cvec):
        self.k, self.layer, self.w, self.cvec = k, layer, w, cvec
        self.u0 = k.units(48)
        k.sig("unit_used").take(48)
        self.silu = k.sig("silu_c").take(1)
        self.row = k.at(k.free, 2, T)[0:2]
        self.r_rdy = k.sig("mod_row_ready").take(12)
        self.r_trn = k.sig("mod_row_turned").take(12)

    def sync(self, sp):
        ring_loads(self.k, sp, lambda i, j, c: self.w[i + j, :, 0:c], self.u0, 48)

    def groups(self, eng, product, turn):
        product(0, 0)
        product(0, 1)
        turn(0, 0)
        with eng.Fori(1, 6) as i:
            turn(i, -1)
            product(i, 0)
            product(i, 1)
            turn(i, 0)
        turn(6, -1)

    def tensor(self, pe):
        k = self.k
        pe.wait_ge(k.sig("silu_c").sem, self.silu + 1)

        def product(i, j):
            if not (isinstance(i, int) and i == 0):
                pe.wait_ge(k.sig("mod_row_ready").sem, self.r_rdy + i * 2 + j - 1)
            for n in range(4):
                u = self.u0 + 4 * j + n
                pe.wait_ge(k.slot[u % SLOTS], slot_count(u, i))
                for h in range(2):
                    c = 2 * n + h
                    mm = pe.matmul(k.ps[0:2, j, :], lhsT=k.csil[:, c, :], rhs=k.ring[:, u % SLOTS, h * T:(h + 1) * T],
                                   start=c == 0, stop=c == KD - 1)
                mm.then_inc(k.sig("unit_used").sem, 1)

        def turn(i, j):
            pe.wait_ge(k.sig("mod_row_ready").sem, self.r_rdy + i * 2 + j + 1)
            for n in range(4):
                mm = pe.matmul(k.ps[:, 2, bass.ds((i * 2 + j) * 8 + 2 * n, 2)],
                               lhsT=self.row[:, j % 2, n * P:(n + 1) * P], rhs=k.c("ident")[0:2, 0:2],
                               start=True, stop=True)
            mm.then_inc(k.sig("mod_row_turned").sem, 1)

        self.groups(pe, product, turn)

    def scalar(self, act):
        k = self.k
        act.activation(k.csil.rearrange("p a b -> p (a b)"), k.vec(self.cvec), ACT.Silu)\
            .then_inc(k.sig("silu_c").sem, 1)

        def take(i, j):
            act.wait_ge(k.sig("unit_used").sem, self.u0 + i * 8 + 4 * j + 4)
            if not (isinstance(i, int) and i == 0):
                act.wait_ge(k.sig("mod_row_turned").sem, self.r_trn + i * 2 + j - 1)
            act.copy(self.row[:, j, :], k.ps[0:2, j, :]).then_inc(k.sig("mod_row_ready").sem, 1)

        self.groups(act, take, lambda i, j: None)

    def vector(self, dve):
        k, l = self.k, self.layer
        dve.wait_ge(k.sig("mod_row_turned").sem, self.r_trn + 12)
        m = k.mods[:, l].rearrange("p w a b -> p w (a b)")
        for w in range(2):
            dve.tensor_tensor(m[:, w, :], k.ps[:, 2, w:96:2], k.vec(f"ada_b{l}"), ALU.add).then_inc(k.dve.count(), 1)
        dve.wait_ge(k.dve.sem, k.dve.value())
        g = k.vec(f"norm{l}").rearrange("p (a b) -> p a b", b=8)
        for w in range(2):
            mm = k.mods[:, l, w]
            for at, gain in ((1, 0), (4, 2)):
                dve.scalar_tensor_tensor(out=mm[:, at, :], in0=mm[:, at, :], scalar=1.0, in1=g[:, gain, :],
                                         op0=ALU.add, op1=ALU.mult)
            for at, gain in ((2, 1), (5, 3)):
                dve.tensor_tensor(mm[:, at, :], mm[:, at, :], g[:, gain, :], ALU.mult)


class Norm(Stage):

    def __init__(self, k, src, layer, gain, shift=None, into=None, spans=(LAT, CTX), which=(0, 1), scratch=None):
        self.k, self.src, self.into, self.spans = k, src, into, spans
        self.gain = [k.mods[:, layer, w, gain, :] for w in which]
        self.shift = None if shift is None else [k.mods[:, layer, w, shift, :] for w in which]
        n = len(spans)
        self.sq_base = k.sig("square_ready").take(KD // 2 * n)
        self.sq_odd = k.sig("odd_square_ready").take(KD // 2 * n)
        self.rs_base = k.sig("inverse_ready").take(n)
        self.ss_base = k.sig("sum_ready").take(n)
        self.sd_base = k.sig("root_ready").take(n)
        self.t_base = k.sig("scaled_ready").take(KD * n)
        self.off = k.free if scratch is None else scratch

    def buffers(self):
        k = self.k
        return k.at(self.off, KD, N), k.at(self.off + KD * N, N), k.at(self.off + KD * N + N, N)

    def scalar(self, act):
        k = self.k
        sq, sd, _ = self.buffers()
        for n, (o, w) in enumerate(self.spans):
            for c in range(0, KD, 2):
                act.activation(sq[:, c, o:o + w], self.src[:, c, o:o + w], ACT.Square)\
                    .then_inc(k.sig("square_ready").sem, 1)
        for n, (o, w) in enumerate(self.spans):
            act.wait_ge(k.sig("sum_ready").sem, self.ss_base + n + 1)
            act.activation(sd[:, o:o + w], k.ps[:, n, 0:w], ACT.Sqrt, bias=EPS, scale=1.0 / D)\
                .then_inc(k.sig("root_ready").sem, 1)
        if self.into is not None:
            for n, (o, w) in enumerate(self.spans):
                for c in range(KD):
                    act.wait_ge(k.sig("scaled_ready").sem, self.t_base + n * KD + c + 1)
                    act.activation(self.into[:, c, o:o + w], sq[:, c, o:o + w], ACT.Identity,
                                   bias=self.shift[n][:, c:c + 1], scale=self.gain[n][:, c:c + 1])

    def tensor(self, pe):
        k = self.k
        sq, _, _ = self.buffers()
        for n, (o, w) in enumerate(self.spans):
            for c in range(KD):
                if c % 2 == 0:
                    pe.wait_ge(k.sig("square_ready").sem, self.sq_base + (n * KD + c) // 2 + 1)
                else:
                    pe.wait_ge(k.sig("odd_square_ready").sem, self.sq_odd + (n * KD + c) // 2 + 1)
                mm = pe.matmul(k.ps[:, n, 0:w], lhsT=k.c("ones"), rhs=sq[:, c, o:o + w], start=c == 0, stop=c == KD - 1)
            mm.then_inc(k.sig("sum_ready").sem, 1)

    def vector(self, dve):
        k = self.k
        sq, sd, rs = self.buffers()
        for n, (o, w) in enumerate(self.spans):
            for c in range(1, KD, 2):
                x = self.src[:, c, o:o + w]
                dve.tensor_tensor(sq[:, c, o:o + w], x, x, ALU.mult).then_inc(k.sig("odd_square_ready").sem, 1)
        for n, (o, w) in enumerate(self.spans):
            dve.wait_ge(k.sig("root_ready").sem, self.sd_base + n + 1)
            dve.reciprocal(rs[:, o:o + w], sd[:, o:o + w]).then_inc(k.sig("inverse_ready").sem, 1)
            dve.wait_ge(k.sig("inverse_ready").sem, self.rs_base + n + 1)
            if self.into is not None:
                for c in range(KD):
                    dve.tensor_tensor(sq[:, c, o:o + w], self.src[:, c, o:o + w], rs[:, o:o + w], ALU.mult)\
                        .then_inc(k.sig("scaled_ready").sem, 1)
                continue
            for c in range(KD):
                dve.scalar_tensor_tensor(out=sq[:, c, o:o + w], in0=self.src[:, c, o:o + w],
                                         scalar=self.gain[n][:, c:c + 1], in1=rs[:, o:o + w],
                                         op0=ALU.mult, op1=ALU.mult).then_inc(k.sig("scaled_ready").sem, 1)
            dve.wait_ge(k.sig("scaled_ready").sem, self.t_base + n * KD + KD)
            for c in range(6, KD):
                dve.tensor_tensor(k.X[:, c, o:o + w], k.X[:, c, o:o + w], sq[:, c, o:o + w], ALU.add)

    def gpsimd(self, pool):
        k = self.k
        if self.into is not None:
            return
        sq, _, _ = self.buffers()
        for n, (o, w) in enumerate(self.spans):
            for c in range(6):
                pool.wait_ge(k.sig("scaled_ready").sem, self.t_base + n * KD + c + 1)
                pool.tensor_tensor(k.X[:, c, o:o + w], k.X[:, c, o:o + w], sq[:, c, o:o + w], ALU.add)


class Linear(Stage):

    def __init__(self, k, w, n_tiles, rhs, dst, kt=KD, spans=(LAT, CTX), func=ACT.Copy, t0=0, d0=0):
        self.k, self.w, self.n_tiles, self.rhs, self.dst, self.kt = k, w, n_tiles, rhs, dst, kt
        self.spans, self.func, self.t0, self.d0 = spans, func, t0, d0
        self.upt = -(-kt // 8)
        self.n_units = n_tiles * self.upt
        self.u0 = k.units(self.n_units)
        k.sig("unit_used").take(self.n_units)
        self.body = 24 if self.upt == 3 else 8
        self.taken = k.sig("out_taken").take(n_tiles)

    def cols(self, j):
        return min(8, self.kt - 8 * (j % self.upt)) * P

    def sync(self, sp):
        upt = self.upt
        if upt == 1:
            src = lambda i, j, c: self.w[i + j + self.t0, :, 0:c]
        elif upt == 2:
            src = lambda i, j, c: self.w[i + j, :, 0:c]
        else:
            src = lambda i, j, c: self.w[j // upt, :, (j % upt) * UC:(j % upt) * UC + c]
        ring_loads(self.k, sp, src, self.u0, self.n_units, self.cols, self.body)

    def tensor(self, pe):
        k, upt = self.k, self.upt

        def unit(i, j):
            u = self.u0 + j
            t = j // upt
            pe.wait_ge(k.slot[u % SLOTS], slot_count(u, i * (self.body // 8)))
            part = j % upt
            ks = range(part * 8, min(part * 8 + 8, self.kt))
            if part == 0:
                pe.wait_ge(k.sig("out_taken").sem, self.taken + t - 1 + i * (self.body // upt))
            for s, (o, w) in enumerate(self.spans):
                for c in ks:
                    mm = pe.matmul(k.ps[:, 2 * s + t % 2, 0:w],
                                   lhsT=k.ring[:, u % SLOTS, (c % 8) * P:(c % 8 + 1) * P],
                                   rhs=self.rhs[:, c, o:o + w], start=c == 0, stop=c == self.kt - 1)
            mm.then_inc(k.sig("unit_used").sem, 1)

        run_body(pe, self.n_units, self.body, unit)

    def scalar(self, act):
        k, upt = self.k, self.upt

        def unit(i, j):
            if j % upt != upt - 1:
                return
            t = j // upt
            act.wait_ge(k.sig("unit_used").sem, self.u0 + j + 1 + i * self.body)
            for s, (o, w) in enumerate(self.spans):
                a = act.activation(self.dst[:, i * (self.body // upt) + t + self.d0, o:o + w],
                                   k.ps[:, 2 * s + t % 2, 0:w], self.func)
            a.then_inc(k.sig("out_taken").sem, 1)

        run_body(act, self.n_units, self.body, unit)


def run_body(eng, n, body, unit, chain=None, per=0):
    t = n // body
    if t > 1:
        with eng.Fori(0, t) as i:
            if chain:
                chain.enter(i, per)
            for j in range(body):
                unit(i, j)
            if chain:
                chain.leave(t)
    elif t == 1:
        for j in range(body):
            unit(0, j)
    for j in range(n - t * body):
        unit(t, j)


class TokLinear(Stage):

    def __init__(self, k, w, groups, dst, func=ACT.Copy, t0=0):
        self.k, self.w, self.groups, self.dst, self.func, self.t0 = k, w, groups, dst, func, t0
        self.u0 = k.units(4 * groups)
        k.sig("unit_used").take(4 * groups)
        self.taken = k.sig("tok_taken").take(NTT * groups)
        self.ready = k.sig("tok_ready").take((NTT - 1) * groups)

    def sync(self, sp):
        ring_loads(self.k, sp, lambda i, j, c: self.w[i + j + self.t0, :, 0:c], self.u0, 4 * self.groups)

    def tensor(self, pe):
        k = self.k
        for g in range(self.groups):
            s0 = (self.u0 + 4 * g) % SLOTS
            for j in range(4):
                pe.wait_ge(k.slot[(self.u0 + 4 * g + j) % SLOTS], slot_count(self.u0 + 4 * g + j))
            for t in range(NTT):
                n = g * NTT + t
                if n >= 4:
                    pe.wait_ge(k.sig("tok_taken").sem, self.taken + n - 3)
                for c in range(KD):
                    mm = pe.matmul(k.ps[:, 4 + n % 4, :].rearrange("p (a b) -> p a b", a=4),
                                   lhsT=k.H[:, c, t * P:(t + 1) * P],
                                   rhs=k.ring[:, s0:s0 + 4, c * P:(c + 1) * P], start=c == 0, stop=c == KD - 1)
                if t < NTT - 1:
                    mm.then_inc(k.sig("tok_ready").sem, 1)
                else:
                    mm.then_inc(k.sig("unit_used").sem, 4)

    def scalar(self, act):
        k = self.k
        for g in range(self.groups):
            for t in range(NTT):
                n = g * NTT + t
                if t < NTT - 1:
                    act.wait_ge(k.sig("tok_ready").sem, self.ready + g * (NTT - 1) + t + 1)
                else:
                    act.wait_ge(k.sig("unit_used").sem, self.u0 + 4 * g + 4)
                act.activation(self.dst[:, t, g * 512:(g + 1) * 512], k.ps[:, 4 + n % 4, :], self.func)\
                    .then_inc(k.sig("tok_taken").sem, 1)


class ConvLinear(Stage):

    def __init__(self, k, w, n_tiles, dst, cw, cb, off, spans=(LAT, CTX), pair=True, t0=0):
        self.k, self.w, self.n, self.dst, self.cw, self.cb = k, w, n_tiles, dst, cw, cb
        self.spans, self.pair, self.t0 = spans, pair, t0
        self.u0 = k.units(n_tiles)
        k.sig("unit_used").take(n_tiles)
        self.taken = k.sig("out_taken").take(n_tiles)
        self.conv = k.sig("conv_done").take(n_tiles)
        self.gated = k.sig("silu_done").take(n_tiles // 2 if pair else n_tiles)
        self.raw = k.at(off, 2, N)
        self.cv = k.at(off + 2 * N, 4, N)
        self.end = spans[-1][0] + spans[-1][1]

    def sync(self, sp):
        ring_loads(self.k, sp, lambda i, j, c: self.w[i + j + self.t0, :, 0:c], self.u0, self.n)

    def tensor(self, pe):
        k = self.k

        def unit(i, j):
            u = self.u0 + j
            pe.wait_ge(k.slot[u % SLOTS], slot_count(u, i))
            pe.wait_ge(k.sig("out_taken").sem, self.taken + j - 1 + i * 8)
            for s, (o, w) in enumerate(self.spans):
                for c in range(KD):
                    mm = pe.matmul(k.ps[:, 2 * s + j % 2, 0:w], lhsT=k.ring[:, u % SLOTS, c * P:(c + 1) * P],
                                   rhs=k.H[:, c, o:o + w], start=c == 0, stop=c == KD - 1)
            mm.then_inc(k.sig("unit_used").sem, 1)

        run_body(pe, self.n, 8, unit)

    def scalar(self, act):
        k = self.k

        def silu(i, j):
            if self.pair and j % 2 == 1:
                return
            act.wait_ge(k.sig("conv_done").sem, self.conv + j + 1 + i * 8)
            src = self.cv[:, j % 4, 0:self.end]
            out = src if self.pair else self.dst[j][:, 0:self.end]
            act.activation(out, src, ACT.Silu).then_inc(k.sig("silu_done").sem, 1)

        def unit(i, j):
            act.wait_ge(k.sig("unit_used").sem, self.u0 + j + 1 + i * 8)
            act.wait_ge(k.sig("conv_done").sem, self.conv + j - 1 + i * 8)
            for s, (o, w) in enumerate(self.spans):
                a = act.activation(self.raw[:, j % 2, o:o + w], k.ps[:, 2 * s + j % 2, 0:w], ACT.Copy)
            a.then_inc(k.sig("out_taken").sem, 1)
            silu(i, j)

        run_body(act, self.n, 8, unit)

    def vector(self, dve):
        k = self.k
        n_cols = 2 * FT if self.pair else 16

        def unit(i, j):
            dve.wait_ge(k.sig("out_taken").sem, self.taken + j + 1 + i * 8)
            ci = i * 8 + j + self.t0
            cw = [k.vec(self.cw)[:, bass.ds(ci + t * n_cols, 1)] for t in range(3)]
            cb = k.vec(self.cb)[:, bass.ds(ci, 1)]
            raw, cv = self.raw[:, j % 2, :], self.cv[:, j % 4, :]
            if not self.pair:
                dve.wait_ge(k.sig("silu_done").sem, self.gated + j - 3 + i * 8)
            dve.tensor_scalar(cv[:, 0:self.end], raw[:, 0:self.end], cw[1], cb, ALU.mult, ALU.add).then_inc(k.dve.count(), 1)
            dve.wait_ge(k.dve.sem, k.dve.value())
            for o, w in self.spans:
                a = dve.scalar_tensor_tensor(out=cv[:, o + 1:o + w], in0=raw[:, o:o + w - 1], scalar=cw[0],
                                             in1=cv[:, o + 1:o + w], op0=ALU.mult, op1=ALU.add)
            a.then_inc(k.dve.count(), 1)
            dve.wait_ge(k.dve.sem, k.dve.value())
            for o, w in self.spans:
                a = dve.scalar_tensor_tensor(out=cv[:, o:o + w - 1], in0=raw[:, o + 1:o + w], scalar=cw[2],
                                             in1=cv[:, o:o + w - 1], op0=ALU.mult, op1=ALU.add)
            a.then_inc(k.sig("conv_done").sem, 1)
            if self.pair and j % 2 == 1:
                dve.wait_ge(k.sig("conv_done").sem, self.conv + j + 1 + i * 8)
                dve.wait_ge(k.sig("silu_done").sem, self.gated + j // 2 + 1 + i * 4)
                dve.tensor_tensor(self.dst[:, i * 4 + j // 2, 0:self.end], self.cv[:, (j - 1) % 4, 0:self.end],
                                  self.cv[:, j % 4, 0:self.end], ALU.mult)

        run_body(dve, self.n, 8, unit, k.dve, 16)


class SpatialGate(Stage):

    def __init__(self, k, dram, G, U, off):
        self.k, self.dram, self.G, self.U = k, dram, G, U
        self.ws, self.bs = k.at(off, 8, P), k.at(off + 1024, 4, P)
        self.tmp = k.at(off + 1536, 2, 4, P)
        self.st = k.at(off + 2560, NTT, 6)
        self.mv = k.at(off + 2600, NTT, 2)
        self.sd = k.at(off + 2620, NTT)
        self.data = k.sig("stage_data").take(32)
        self.var = k.sig("variance_ready").take(1)
        self.root = k.sig("root_ready").take(1)
        self.vn = k.sig("gate_normed").take(NTT)
        self.mix = k.sig("mixed_ready").take(NTT)
        self.used = k.sig("mixed_taken").take(NTT)

    def gpsimd(self, pool):
        k = self.k
        pool.dma_start(self.ws, self.dram["sgu_w"]).then_inc(k.sig("stage_data").sem, 16)
        pool.dma_start(self.bs, self.dram["sgu_b"]).then_inc(k.sig("stage_data").sem, 16)

    def vector(self, dve):
        k, G = self.k, self.G
        for t in range(NTT):
            dve.bn_stats(self.st[:, t, :], G[:, t, :]).then_inc(k.dve.count(), 1)
        dve.wait_ge(k.dve.sem, k.dve.value())
        for t in range(NTT):
            a = dve.bn_aggr(self.mv[:, t, :], self.st[:, t, :])
        a.then_inc(k.sig("variance_ready").sem, 1)
        dve.wait_ge(k.sig("root_ready").sem, self.root + 1)
        dve.reciprocal(self.sd, self.sd).then_inc(k.dve.count(), 1)
        dve.wait_ge(k.dve.sem, k.dve.value())
        for t in range(NTT):
            dve.tensor_scalar(G[:, t, :], G[:, t, :], self.mv[:, t, 0:1], self.sd[:, t:t + 1],
                              ALU.subtract, ALU.mult).then_inc(k.sig("gate_normed").sem, 1)
        dve.wait_ge(k.sig("stage_data").sem, self.data + 32)
        for t in range(NTT):
            dve.wait_ge(k.sig("mixed_ready").sem, self.mix + t + 1)
            a = dve.tensor_tensor(self.tmp[:, t % 2], k.ps[:, t % 4, :].rearrange("p (a b) -> p a b", a=4),
                                  self.bs, ALU.add)
            a.then_inc(k.sig("mixed_taken").sem, 1)
            dve.wait_ge(k.sig("mixed_taken").sem, self.used + t + 1)
            dve.tensor_tensor(k.H[:, 4:8, t * P:(t + 1) * P], self.tmp[:, t % 2],
                              self.U[:, 0:4, t * P:(t + 1) * P], ALU.mult)

    def scalar(self, act):
        k = self.k
        act.wait_ge(k.sig("variance_ready").sem, self.var + 1)
        act.activation(self.sd, self.mv[:, :, 1], ACT.Sqrt, bias=EPS).then_inc(k.sig("root_ready").sem, 1)

    def tensor(self, pe):
        k = self.k
        pe.wait_ge(k.sig("stage_data").sem, self.data + 32)
        for t in range(NTT):
            pe.wait_ge(k.sig("gate_normed").sem, self.vn + t + 1)
            if t >= 4:
                pe.wait_ge(k.sig("mixed_taken").sem, self.used + t - 3)
            for g in range(8):
                half = (g % 2) * 64
                mm = pe.matmul(k.ps[half:half + 64, t % 4, (g // 2) * P:(g // 2 + 1) * P],
                               lhsT=self.G[:, t, g * 64:(g + 1) * 64], rhs=self.ws[:, g, :], start=True, stop=True)
            mm.then_inc(k.sig("mixed_ready").sem, 1)


class Neighbourhood(Stage):

    def __init__(self, k, dram, QK, V, off):
        self.k, self.dram, self.QK, self.V = k, dram, QK, V
        self.bt = k.at(off, 2, 16, 64)
        self.s = k.at(off + 2048, 2, N)
        self.p = k.at(off + 2048 + 2 * N, 2, N)
        self.pt = k.at(off + 2048 + 4 * N, 2, N)
        self.st = k.at(off + 2048 + 6 * N, 8, 4)
        self.its = [(h, q) for h in range(8) for q in range(NTT)]
        n = len(self.its)
        self.bias = k.sig("bias_loaded").take(32 * 8)
        self.masked = k.sig("bias_masked").take(8)
        self.s_rdy = k.sig("scores_ready").take(n)
        self.m_rdy = k.sig("max_ready").take(n)
        self.e_rdy = k.sig("exp_ready").take(n)
        self.p_rdy = k.sig("probs_ready").take(n)
        self.t_rdy = k.sig("turned_ready").take(n)
        self.t_tak = k.sig("turned_taken").take(n)
        self.o_rdy = k.sig("heads_ready").take(n)
        self.o_tak = k.sig("heads_taken").take(n)
        self.r_rdy = k.sig("recip_ready").take(n)

    def gpsimd(self, pool):
        k = self.k
        for h in range(8):
            if h >= 2:
                pool.wait_ge(k.sig("max_ready").sem, self.m_rdy + (h - 2) * NTT + LTT)
            for half in range(2):
                pool.dma_start(self.bt[half * 64:half * 64 + 64, h % 2, 1:15, :],
                               self.dram["rpb"][h, :, 1 - half:15 - half, :])\
                    .then_inc(k.sig("bias_loaded").sem, 16)
            pool.wait_ge(k.sig("bias_loaded").sem, self.bias + 32 * (h + 1))
            b = self.bt[:, h % 2, 1:15, :]
            pool.tensor_tensor(b, b, k.c("namask").unsqueeze(1).to_broadcast([P, 14, 64]), ALU.add)\
                .then_inc(k.sig("bias_masked").sem, 1)

    def stages(self, n, eng_scores, eng_turn, eng_out):
        for i in range(n + 2):
            if i < n:
                eng_scores(i)
            if 1 <= i <= n:
                eng_turn(i - 1)
            if i >= 2:
                eng_out(i - 2)

    def tensor(self, pe):
        k = self.k

        def scores(i):
            h, q = self.its[i]
            b, hp = (i % 2) * 2, (h % 2) * 64
            if i >= 2:
                pe.wait_ge(k.sig("max_ready").sem, self.m_rdy + i - 1)
            lhsT = self.QK[hp:hp + 64, h // 2, q * P:(q + 1) * P]
            if q < LTT:
                pe.matmul(k.ps[:, b, 0:T], lhsT=lhsT, rhs=self.QK[hp:hp + 64, 4 + h // 2, 0:T], start=True, stop=True)
            pe.matmul(k.ps[:, b + 1, 0:L], lhsT=lhsT, rhs=self.QK[hp:hp + 64, 4 + h // 2, T:N], start=True, stop=True)\
                .then_inc(k.sig("scores_ready").sem, 1)

        def turn(i):
            h, q = self.its[i]
            pe.wait_ge(k.sig("probs_ready").sem, self.p_rdy + i + 1)
            if i >= 1:
                pe.wait_ge(k.sig("turned_taken").sem, self.t_tak + i)
            for t in range(0 if q < LTT else LTT, NTT):
                mm = pe.transpose(k.ps[:, 4 + t // 4, (t % 4) * P:(t % 4 + 1) * P], self.p[:, i % 2, t * P:(t + 1) * P],
                                  k.c("ident"))
            mm.then_inc(k.sig("turned_ready").sem, 1)

        def out(i):
            h, q = self.its[i]
            hp = (h % 2) * 64
            pe.wait_ge(k.sig("turned_taken").sem, self.t_tak + i + 1)
            if i >= 2:
                pe.wait_ge(k.sig("heads_taken").sem, self.o_tak + i - 1)
            t0 = 0 if q < LTT else LTT
            for t in range(t0, NTT):
                mm = pe.matmul(k.ps[hp:hp + 64, 6 + i % 2, 0:P], lhsT=self.V[:, t, h * 64:(h + 1) * 64],
                               rhs=self.pt[:, i % 2, t * P:(t + 1) * P], start=t == t0, stop=t == NTT - 1)
            mm.then_inc(k.sig("heads_ready").sem, 1)

        n = len(self.its)
        scores(0)
        for i in range(n + 2):
            if i + 1 < n:
                scores(i + 1)
            if i >= 2:
                out(i - 2)
            if 1 <= i <= n:
                turn(i - 1)

    def vector(self, dve):
        k = self.k

        def scores(i):
            h, q = self.its[i]
            b = (i % 2) * 2
            s, st = self.s[:, i % 2, :], self.st[:, i % 8, :]
            dve.wait_ge(k.sig("scores_ready").sem, self.s_rdy + i + 1)
            if i >= 2:
                dve.wait_ge(k.sig("exp_ready").sem, self.e_rdy + i - 1)
            if q == 0:
                dve.wait_ge(k.sig("bias_masked").sem, self.masked + h + 1)
            if q < LTT:
                j0 = 7 - 2 * q
                dve.scalar_tensor_tensor(out=s[:, 0:T], in0=k.ps[:, b, 0:T], scalar=0.125,
                                         in1=self.bt[:, h % 2, j0:j0 + 8, :].rearrange("p a b -> p (a b)"),
                                         op0=ALU.mult, op1=ALU.add)
            lo = 0 if q < LTT else T
            dve.tensor_scalar(s[:, T:N], k.ps[:, b + 1, 0:L], 0.125, None, ALU.mult).then_inc(k.dve.count(), 1)
            dve.wait_ge(k.dve.sem, k.dve.value())
            dve.tensor_reduce(st[:, 0:1], s[:, lo:N], AX.X, ALU.max, negate=True).then_inc(k.sig("max_ready").sem, 1)

        def turn(i):
            st = self.st[:, i % 8, :]
            dve.wait_ge(k.sig("exp_ready").sem, self.e_rdy + i + 1)
            dve.reciprocal(st[:, 2:3], st[:, 1:2]).then_inc(k.sig("recip_ready").sem, 1)
            h, q = self.its[i]
            lo = 0 if q < LTT else T
            dve.wait_ge(k.sig("recip_ready").sem, self.r_rdy + i + 1)
            p = self.p[:, i % 2, lo:N]
            a = dve.tensor_scalar(p, p, st[:, 2:3], None, ALU.mult)
            a.then_inc(k.sig("probs_ready").sem, 1)

        def out(i):
            h, q = self.its[i]
            hp = (h % 2) * 64
            dve.wait_ge(k.sig("heads_ready").sem, self.o_rdy + i + 1)
            dve.tensor_copy(k.H[hp:hp + 64, h // 2, q * P:(q + 1) * P], k.ps[hp:hp + 64, 6 + i % 2, 0:P])\
                .then_inc(k.sig("heads_taken").sem, 1)

        n = len(self.its)
        for i in range(n + 2):
            if i < n:
                scores(i)
            if 1 <= i <= n:
                turn(i - 1)
            if i >= 2:
                out(i - 2)

    def scalar(self, act):
        k = self.k

        def scores(i):
            h, q = self.its[i]
            lo = 0 if q < LTT else T
            st = self.st[:, i % 8, :]
            act.wait_ge(k.sig("max_ready").sem, self.m_rdy + i + 1)
            if i >= 2:
                act.wait_ge(k.sig("turned_ready").sem, self.t_rdy + i - 1)
            act.activation(self.p[:, i % 2, lo:N], self.s[:, i % 2, lo:N], ACT.Exp, bias=st[:, 0:1],
                           accum_out=st[:, 1:2]).then_inc(k.sig("exp_ready").sem, 1)

        def turn(i):
            h, q = self.its[i]
            act.wait_ge(k.sig("turned_ready").sem, self.t_rdy + i + 1)
            if i >= 2:
                act.wait_ge(k.sig("heads_ready").sem, self.o_rdy + i - 1)
            if q < LTT:
                act.copy(self.pt[:, i % 2, 0:T], k.ps[:, 4, :])
            act.copy(self.pt[:, i % 2, T:N], k.ps[:, 5, 0:L]).then_inc(k.sig("turned_taken").sem, 1)

        self.stages(len(self.its), scores, turn, lambda i: None)


class Rope(Stage):

    def __init__(self, k, dram, view, tiles, rot, cos, off, load=True):
        self.k, self.dram, self.view, self.tiles, self.rot, self.cos = k, dram, view, tiles, rot, cos
        self.load = load
        self.cs = k.at(off, 2, T)
        self.tmp = k.at(off + 2 * T, 2, T)
        n = len(tiles)
        self.data = k.sig("stage_data").take(16)
        self.rdy = k.sig("rotated_ready").take(n)
        self.tak = k.sig("rotated_taken").take(n)

    def gpsimd(self, pool):
        k, o = self.k, BCON[self.cos][0]
        pool.dma_start(self.cs.rearrange("p a b -> p (a b)"), self.dram["consts"][:, o:o + 2 * T])\
            .then_inc(k.sig("stage_data").sem, 16)

    def tensor(self, pe):
        k = self.k
        for n, t in enumerate(self.tiles):
            if n >= 2:
                pe.wait_ge(k.sig("rotated_taken").sem, self.tak + n - 1)
            pe.matmul(k.ps[:, n % 2, :], lhsT=k.c(self.rot), rhs=self.view[:, t, 0:T], start=True, stop=True)\
                .then_inc(k.sig("rotated_ready").sem, 1)

    def vector(self, dve):
        k = self.k
        dve.wait_ge(k.sig("stage_data").sem, self.data + 16)
        for n, t in enumerate(self.tiles):
            x, tmp = self.view[:, t, 0:T], self.tmp[:, n % 2, :]
            dve.wait_ge(k.sig("rotated_ready").sem, self.rdy + n + 1)
            dve.tensor_tensor(x, x, self.cs[:, 0, :], ALU.mult)
            dve.tensor_tensor(tmp, k.ps[:, n % 2, :], self.cs[:, 1, :], ALU.mult).then_inc(k.sig("rotated_taken").sem, 1)
            dve.wait_ge(k.sig("rotated_taken").sem, self.tak + n + 1)
            dve.tensor_tensor(x, x, tmp, ALU.add)


class Retention(Stage):

    def __init__(self, k, dram, QK, V, O, head0, off):
        self.k, self.dram, self.QK, self.V, self.O, self.head0 = k, dram, QK, V, O, head0
        self.absd = k.at(off, 1408)
        self.F = k.at(off + 1408, 1408)
        self.tmp = k.at(off + 2816, P)
        self.dc = k.at(off + 2944, 1, T)
        self.s = k.at(off + 2944 + T, 2, NTT, T)
        self.data = k.sig("stage_data").take(16)
        self.strip = k.sig("strip_exp").take(4)
        self.s_rdy = k.sig("scores_ready").take(4 * NTT)
        self.s_tak = k.sig("decayed_ready").take(4 * NTT)
        self.o_rdy = k.sig("heads_ready").take(8)
        self.o_tak = k.sig("heads_taken").take(8)

    def gpsimd(self, pool):
        o = BCON["absd"][0]
        pool.dma_start(self.absd, self.dram["consts"][:, o:o + 1408]).then_inc(self.k.sig("stage_data").sem, 16)

    def scalar(self, act):
        k = self.k
        act.wait_ge(k.sig("stage_data").sem, self.data + 16)

        def strip(h):
            if h >= 1:
                act.wait_ge(k.sig("decayed_ready").sem, self.s_tak + h * NTT)
            lf = k.vec("lgd", self.head0 + h, self.head0 + h + 1)
            lb = k.vec("lgd", 8 + self.head0 + h, 8 + self.head0 + h + 1)
            act.activation(self.F[:, 0:768], self.absd[:, 0:768], ACT.Exp, scale=lb)
            act.activation(self.F[:, 768:1408], self.absd[:, 768:1408], ACT.Exp, scale=lf)
            act.activation(self.tmp, self.absd[:, 640:768], ACT.Exp, scale=lf).then_inc(k.sig("strip_exp").sem, 1)

        def out(h):
            for v in range(2):
                act.wait_ge(k.sig("heads_ready").sem, self.o_rdy + 2 * h + v + 1)
                act.copy(self.O[:, 2 * (self.head0 + h) + v, :], k.ps[:, 4 + (2 * h + v) % 4, :])\
                    .then_inc(k.sig("heads_taken").sem, 1)

        for h in range(5):
            if h < 4:
                strip(h)
            if h >= 1:
                out(h - 1)

    def vector(self, dve):
        k = self.k
        diag = self.F[:, 640:768]
        for h in range(4):
            dve.wait_ge(k.sig("strip_exp").sem, self.strip + h + 1)
            dve.tensor_tensor(diag, diag, k.c("le"), ALU.mult)
            dve.tensor_tensor(self.tmp, self.tmp, k.c("ge"), ALU.mult).then_inc(k.dve.count(), 1)
            dve.wait_ge(k.dve.sem, k.dve.value())
            dve.tensor_tensor(diag, diag, self.tmp, ALU.add).then_inc(k.dve.count(), 1)
            dve.wait_ge(k.dve.sem, k.dve.value())
            for t in range(NTT):
                n = h * NTT + t
                if t < LTT:
                    decay = self.F[:, 640 - P * t:640 - P * t + T]
                else:
                    c = t - LTT
                    decay = self.dc[:, 0, :]
                    dve.wait_ge(k.sig("decayed_ready").sem, self.s_tak + n)
                    dve.tensor_tensor(decay, self.F[:, 896 - P * c:896 - P * c + T],
                                      self.F[:, P - P * c:P - P * c + T], ALU.add).then_inc(k.dve.count(), 1)
                    dve.wait_ge(k.dve.sem, k.dve.value())
                dve.wait_ge(k.sig("scores_ready").sem, self.s_rdy + n + 1)
                if h >= 2:
                    dve.wait_ge(k.sig("heads_ready").sem, self.o_rdy + 2 * (h - 1))
                dve.scalar_tensor_tensor(out=self.s[:, h % 2, t, :], in0=k.ps[:, n % 4, :], scalar=float(P) ** -0.5,
                                         in1=decay, op0=ALU.mult, op1=ALU.mult).then_inc(k.sig("decayed_ready").sem, 1)

    def tensor(self, pe):
        k = self.k

        def scores(h):
            for t in range(NTT):
                n = h * NTT + t
                if n >= 4:
                    pe.wait_ge(k.sig("decayed_ready").sem, self.s_tak + n - 3)
                pe.matmul(k.ps[:, n % 4, :], lhsT=self.QK[:, 4 + h, t * P:(t + 1) * P], rhs=self.QK[:, h, 0:T],
                          start=True, stop=True).then_inc(k.sig("scores_ready").sem, 1)

        def out(h):
            for v in range(2):
                if h >= 2:
                    pe.wait_ge(k.sig("heads_taken").sem, self.o_tak + 2 * (h - 2) + v + 1)
                for t in range(NTT):
                    pe.wait_ge(k.sig("decayed_ready").sem, self.s_tak + h * NTT + t + 1)
                    mm = pe.matmul(k.ps[:, 4 + (2 * h + v) % 4, :],
                                   lhsT=self.V[:, t, h * 256 + v * P:h * 256 + (v + 1) * P],
                                   rhs=self.s[:, h % 2, t, :], start=t == 0, stop=t == NTT - 1)
                mm.then_inc(k.sig("heads_ready").sem, 1)

        scores(0)
        for h in range(4):
            if h < 3:
                scores(h + 1)
            out(h)


class GroupNorm(Stage):

    def __init__(self, k, view, groups, per, gain, off, center=False, after=1.0):
        self.k, self.view, self.groups, self.per, self.gain = k, view, groups, per, gain
        self.center, self.after = center, after
        self.sq = k.at(off, 2, per, T)
        self.sd = k.at(off + 2 * per * T, 2, T)
        self.rs = k.at(off + 2 * per * T + 2 * T, 2, T)
        n = groups
        self.mean = k.sig("mean_ready").take(n if center else 0)
        self.cent = k.sig("centred").take(n if center else 0)
        self.sq_b = k.sig("square_ready").take(n)
        self.ss_b = k.sig("sum_ready").take(n)
        self.sd_b = k.sig("root_ready").take(n)
        self.nrm = k.sig("normed").take(n)

    def tensor(self, pe):
        k, per = self.k, self.per

        def mean(g):
            if g >= 2:
                pe.wait_ge(k.sig("centred").sem, self.cent + g - 1)
            for t in range(per):
                mm = pe.matmul(k.ps[:, g % 2, :], lhsT=k.c("ones"), rhs=self.view[:, g * per + t, 0:T],
                               start=t == 0, stop=t == per - 1)
            mm.then_inc(k.sig("mean_ready").sem, 1)

        def square(g):
            pe.wait_ge(k.sig("square_ready").sem, self.sq_b + g + 1)
            if g >= 2:
                pe.wait_ge(k.sig("root_ready").sem, self.sd_b + g - 1)
            for t in range(per):
                mm = pe.matmul(k.ps[:, 2 + g % 2, :], lhsT=k.c("ones"), rhs=self.sq[:, g % 2, t, :],
                               start=t == 0, stop=t == per - 1)
            mm.then_inc(k.sig("sum_ready").sem, 1)

        for g in range(self.groups + 1):
            if g < self.groups and self.center:
                mean(g)
            if g >= 1:
                square(g - 1)

    def scalar(self, act):
        k, per = self.k, self.per
        for g in range(self.groups + 1):
            if g < self.groups:
                if self.center:
                    act.wait_ge(k.sig("centred").sem, self.cent + g + 1)
                if g >= 2:
                    act.wait_ge(k.sig("sum_ready").sem, self.ss_b + g - 1)
                for t in range(per):
                    a = act.activation(self.sq[:, g % 2, t, :], self.view[:, g * per + t, 0:T], ACT.Square)
                a.then_inc(k.sig("square_ready").sem, 1)
            if g >= 1:
                act.wait_ge(k.sig("sum_ready").sem, self.ss_b + g)
                if g >= 3:
                    act.wait_ge(k.sig("normed").sem, self.nrm + g - 2)
                act.activation(self.sd[:, (g - 1) % 2, :], k.ps[:, 2 + (g - 1) % 2, :], ACT.Sqrt, bias=EPS,
                               scale=1.0 / (per * P)).then_inc(k.sig("root_ready").sem, 1)

    def vector(self, dve):
        k, per = self.k, self.per
        for g in range(self.groups + 1):
            if g < self.groups and self.center:
                dve.wait_ge(k.sig("mean_ready").sem, self.mean + g + 1)
                for t in range(per):
                    x = self.view[:, g * per + t, 0:T]
                    a = dve.scalar_tensor_tensor(out=x, in0=k.ps[:, g % 2, :], scalar=-1.0 / (per * P), in1=x,
                                                 op0=ALU.mult, op1=ALU.add)
                a.then_inc(k.sig("centred").sem, 1)
            if g >= 1:
                b = (g - 1) % 2
                dve.wait_ge(k.sig("root_ready").sem, self.sd_b + g)
                dve.reciprocal(self.rs[:, b, :], self.sd[:, b, :]).then_inc(k.dve.count(), 1)
                dve.wait_ge(k.dve.sem, k.dve.value())
                if self.after != 1.0:
                    dve.tensor_scalar(self.rs[:, b, :], self.rs[:, b, :], self.after, None, ALU.mult).then_inc(k.dve.count(), 1)
                    dve.wait_ge(k.dve.sem, k.dve.value())
                for t in range(per):
                    x = self.view[:, (g - 1) * per + t, 0:T]
                    a = dve.scalar_tensor_tensor(out=x, in0=x, scalar=self.gain((g - 1) * per + t),
                                                 in1=self.rs[:, b, :], op0=ALU.mult, op1=ALU.mult)
                a.then_inc(k.sig("normed").sem, 1)


class GatedLinear(Stage):

    def __init__(self, k, w, n_tiles, x, dst, func, off, add=None, t0=0):
        self.k, self.w, self.n, self.x, self.dst, self.func, self.t0, self.add = k, w, n_tiles, x, dst, func, t0, add
        self.u0 = k.units(n_tiles)
        k.sig("unit_used").take(n_tiles)
        self.taken = k.sig("out_taken").take(n_tiles)
        self.conv = k.sig("conv_done").take(n_tiles)
        self.buf = k.at(off, 2, T)

    def sync(self, sp):
        ring_loads(self.k, sp, lambda i, j, c: self.w[i + j + self.t0, :, 0:c], self.u0, self.n)

    def tensor(self, pe):
        k = self.k

        def unit(i, j):
            u = self.u0 + j
            pe.wait_ge(k.slot[u % SLOTS], slot_count(u, i))
            pe.wait_ge(k.sig("out_taken").sem, self.taken + j - 1 + i * 8)
            for c in range(KD):
                mm = pe.matmul(k.ps[:, j % 2, :], lhsT=k.ring[:, u % SLOTS, c * P:(c + 1) * P],
                               rhs=k.H[:, c, 0:T], start=c == 0, stop=c == KD - 1)
            mm.then_inc(k.sig("unit_used").sem, 1)

        run_body(pe, self.n, 8, unit)

    def scalar(self, act):
        k = self.k

        def unit(i, j):
            act.wait_ge(k.sig("unit_used").sem, self.u0 + j + 1 + i * 8)
            act.wait_ge(k.sig("conv_done").sem, self.conv + j - 1 + i * 8)
            act.activation(self.buf[:, j % 2, :], k.ps[:, j % 2, :], self.func).then_inc(k.sig("out_taken").sem, 1)

        run_body(act, self.n, 8, unit)

    def vector(self, dve):
        k = self.k

        def unit(i, j):
            dve.wait_ge(k.sig("out_taken").sem, self.taken + j + 1 + i * 8)
            a = dve.tensor_tensor(self.dst[:, i * 8 + j, :], self.buf[:, j % 2, :], self.x[:, i * 8 + j, :], ALU.mult)
            if self.add is not None:
                a.then_inc(k.dve.count(), 1)
                dve.wait_ge(k.dve.sem, k.dve.value())
                a = dve.tensor_tensor(self.dst[:, i * 8 + j, :], self.dst[:, i * 8 + j, :],
                                      self.add[:, i * 8 + j, :], ALU.add)
            a.then_inc(k.sig("conv_done").sem, 1)

        run_body(dve, self.n, 8, unit, k.dve, 8 if self.add is not None else 0)


class DiffAttention(Stage):

    def __init__(self, k, Q, K, V, O, y_rows, off):
        self.k, self.Q, self.K, self.V, self.O, self.y_rows = k, Q, K, V, O, y_rows
        self.zero = k.at(off + 6 * N + 72, D)
        self.cleared = k.sig("zeros_made").take(1)
        self.zeros = k.sig("zeros_stored").take(16 * (MAXB - MINB) // 8)
        self.p = k.at(off, 2, 2, N)
        self.pt = k.at(off + 4 * N, 2, N)
        self.st = k.at(off + 6 * N, 8, 8)
        self.lam = k.at(off + 6 * N + 64, 8)
        self.its = [(h, q) for h in range(8) for q in range(LTT)]
        n = len(self.its)
        self.lam_b = k.sig("lambda_steps").take(3)
        self.s_rdy = k.sig("scores_ready").take(2 * n)
        self.m_rdy = k.sig("max_ready").take(2 * n)
        self.e_rdy = k.sig("exp_ready").take(2 * n)
        self.p_rdy = k.sig("probs_ready").take(n)
        self.t_rdy = k.sig("turned_ready").take(n)
        self.t_tak = k.sig("turned_taken").take(n)
        self.o_rdy = k.sig("heads_ready").take(n)
        self.o_tak = k.sig("heads_taken").take(n)

    def gpsimd(self, pool):
        k = self.k
        pool.memset(self.zero, 0.0).then_inc(k.sig("zeros_made").sem, 1)
        pool.wait_ge(k.sig("zeros_made").sem, self.cleared + 1)
        for b in range(MINB, MAXB, 8):
            pool.dma_start(self.y_rows[b * P:(b + 8) * P].rearrange("(b p) d -> p b d", p=P),
                           self.zero.unsqueeze(1).to_broadcast([P, 8, D])).then_inc(k.sig("zeros_stored").sem, 16)
        pool.wait_ge(k.sig("zeros_stored").sem, self.zeros + 16 * (MAXB - MINB) // 8)

    def tensor(self, pe):
        k, n = self.k, len(self.its)
        pe.wait_ge(k.sig("lambda_steps").sem, self.lam_b + 1)
        pe.matmul(k.ps[:, 7, 0:2], lhsT=k.c("ones"), rhs=self.lam[:, 0:2], start=True, stop=True)\
            .then_inc(k.sig("lambda_steps").sem, 1)

        def scores(i, c):
            if i >= n:
                return
            h, q = self.its[i]
            if i >= 1:
                pe.wait_ge(k.sig("exp_ready").sem, self.e_rdy + 2 * (i - 1) + c + 1)
            for half in range(2):
                mm = pe.matmul(k.ps[:, 2 * c + half, 0:384], lhsT=self.Q[c * 64:c * 64 + 64, h, q * P:(q + 1) * P],
                               rhs=self.K[c * 64:c * 64 + 64, h, half * 384:(half + 1) * 384],
                               start=True, stop=True)
            mm.then_inc(k.sig("scores_ready").sem, 1)

        def turn(i):
            pe.wait_ge(k.sig("probs_ready").sem, self.p_rdy + i + 1)
            if i >= 1:
                pe.wait_ge(k.sig("turned_taken").sem, self.t_tak + i)
            for t in range(NTT):
                mm = pe.transpose(k.ps[:, 4 + t // 4, (t % 4) * P:(t % 4 + 1) * P],
                                  self.p[:, i % 2, 0, t * P:(t + 1) * P], k.c("ident"))
            mm.then_inc(k.sig("turned_ready").sem, 1)

        def out(i):
            h, q = self.its[i]
            pe.wait_ge(k.sig("turned_taken").sem, self.t_tak + i + 1)
            if i >= 2:
                pe.wait_ge(k.sig("heads_taken").sem, self.o_tak + i - 1)
            elif i == 1:
                pe.wait_ge(k.sig("lambda_steps").sem, self.lam_b + 3)
            for t in range(NTT):
                mm = pe.matmul(k.ps[:, 6 + i % 2, 0:P], lhsT=self.V[:, t, h * P:(h + 1) * P],
                               rhs=self.pt[:, i % 2, t * P:(t + 1) * P], start=t == 0, stop=t == NTT - 1)
            mm.then_inc(k.sig("heads_ready").sem, 1)

        scores(0, 0)
        for i in range(n + 2):
            scores(i, 1)
            if i >= 2:
                out(i - 2)
            scores(i + 1, 0)
            if 1 <= i <= n:
                turn(i - 1)

    def vector(self, dve):
        k, n = self.k, len(self.its)
        lam = self.lam
        v = k.vec("lam")
        dve.tensor_tensor(lam[:, 0:2], v[:, 0:4:2], v[:, 1:4:2], ALU.mult).then_inc(k.sig("lambda_steps").sem, 1)
        dve.wait_ge(k.sig("lambda_steps").sem, self.lam_b + 3)
        dve.tensor_tensor(lam[:, 4:5], lam[:, 3:4], lam[:, 2:3], ALU.subtract).then_inc(k.dve.count(), 1)
        dve.wait_ge(k.dve.sem, k.dve.value())
        dve.tensor_scalar(lam[:, 5:6], lam[:, 4:5], -LAM_INIT, None, ALU.add).then_inc(k.dve.count(), 1)
        dve.wait_ge(k.dve.sem, k.dve.value())

        def scores(i):
            for c in range(2):
                st = self.st[:, i % 8, :]
                dve.wait_ge(k.sig("scores_ready").sem, self.s_rdy + 2 * i + c + 1)
                dve.tensor_reduce(st[:, 6 + c:7 + c], k.ps[:, 2 * c:2 * c + 2, 0:384], AX.XY, ALU.max,
                                  negate=True).then_inc(k.dve.count(), 1)
                dve.wait_ge(k.dve.sem, k.dve.value())
                dve.tensor_scalar(st[:, c:c + 1], st[:, 6 + c:7 + c], 0.125, None, ALU.mult)\
                    .then_inc(k.sig("max_ready").sem, 1)

        def turn(i):
            st, p = self.st[:, i % 8, :], self.p[:, i % 2]
            dve.wait_ge(k.sig("exp_ready").sem, self.e_rdy + 2 * i + 2)
            dve.reciprocal(st[:, 4:6], st[:, 2:4]).then_inc(k.dve.count(), 1)
            dve.wait_ge(k.dve.sem, k.dve.value())
            dve.tensor_scalar(p[:, 1, :], p[:, 1, :], st[:, 5:6], lam[:, 5:6], ALU.mult, ALU.mult).then_inc(k.dve.count(), 1)
            dve.wait_ge(k.dve.sem, k.dve.value())
            dve.scalar_tensor_tensor(out=p[:, 0, :], in0=p[:, 0, :], scalar=st[:, 4:5], in1=p[:, 1, :],
                                     op0=ALU.mult, op1=ALU.add).then_inc(k.sig("probs_ready").sem, 1)

        for i in range(n + 1):
            if i < n:
                scores(i)
            if i >= 1:
                turn(i - 1)

    def scalar(self, act):
        k, n = self.k, len(self.its)
        act.wait_ge(k.sig("lambda_steps").sem, self.lam_b + 2)
        act.activation(self.lam[:, 2:4], k.ps[:, 7, 0:2], ACT.Exp).then_inc(k.sig("lambda_steps").sem, 1)

        def scores(i):
            st = self.st[:, i % 8, :]
            for c in range(2):
                act.wait_ge(k.sig("max_ready").sem, self.m_rdy + 2 * i + c + 1)
                if i >= 2:
                    act.wait_ge(k.sig("turned_ready").sem, self.t_rdy + i - 1)
                act.activation(self.p[:, i % 2, c, :].rearrange("p (a b) -> p a b", a=2),
                               k.ps[:, 2 * c:2 * c + 2, 0:384], ACT.Exp, bias=st[:, c:c + 1], scale=0.125,
                               accum_out=st[:, 2 + c:3 + c]).then_inc(k.sig("exp_ready").sem, 1)

        def turn(i):
            act.wait_ge(k.sig("turned_ready").sem, self.t_rdy + i + 1)
            if i >= 2:
                act.wait_ge(k.sig("heads_ready").sem, self.o_rdy + i - 1)
            act.copy(self.pt[:, i % 2, 0:T], k.ps[:, 4, :])
            act.copy(self.pt[:, i % 2, T:N], k.ps[:, 5, 0:L]).then_inc(k.sig("turned_taken").sem, 1)

        def out(i):
            h, q = self.its[i]
            act.wait_ge(k.sig("heads_ready").sem, self.o_rdy + i + 1)
            act.copy(self.O[:, h, q * P:(q + 1) * P], k.ps[:, 6 + i % 2, 0:P]).then_inc(k.sig("heads_taken").sem, 1)

        for i in range(n + 2):
            if i < n:
                scores(i)
            if 1 <= i <= n:
                turn(i - 1)
            if i >= 2:
                out(i - 2)


class StepSizes(Stage):

    def __init__(self, k, w, dt, A, nA, AT, off):
        self.k, self.w, self.dt, self.A, self.nA, self.AT = k, w, dt, A, nA, AT
        self.u0 = k.units(8)
        k.sig("unit_used").take(8)
        self.x, self.e, self.s, self.s2, self.r, self.dta, self.ndta = (
            k.at(off + 192 * j, NTT, 32) for j in range(7))
        self.ea = k.at(off + 192 * 7, 32)
        self.steps = k.sig("dt_steps").take(8)

    def sync(self, sp):
        ring_loads(self.k, sp, lambda i, j, c: self.w[0, :, 0:c], self.u0, 8, lambda j: 256)

    def tensor(self, pe):
        k = self.k
        u, st = self.u0, k.sig("dt_steps")
        for j in range(8):
            pe.wait_ge(k.slot[(u + j) % SLOTS], slot_count(u + j))
        for t in range(NTT):
            for c in range(KD):
                mm = pe.matmul(k.ps[:, 0, t * 32:(t + 1) * 32], lhsT=k.H[:, c, t * P:(t + 1) * P],
                               rhs=k.ring[:, u % SLOTS, c * 32:(c + 1) * 32], start=c == 0, stop=c == KD - 1)
        mm.then_inc(k.sig("unit_used").sem, 8)
        pe.wait_ge(st.sem, self.steps + 3)

        def total(t, d, parts):
            o = k.ps[:, 1, t * 32 + d * 16:t * 32 + (d + 1) * 16]
            for n, (m, x, tt) in enumerate(parts):
                mm = pe.matmul(o, lhsT=k.c(m), rhs=x[:, tt, d * 16:(d + 1) * 16], start=n == 0, stop=n == len(parts) - 1)
            return mm

        for t in range(LTT):
            total(t, 0, [("ge", self.dta, t)] + [("ones", self.dta, a) for a in range(t)])
            total(t, 1, [("lt", self.ndta, t)] + [("ones", self.ndta, a) for a in range(t)])
        for t in range(LTT, NTT):
            total(t, 0, [("gt", self.ndta, t)] + [("ones", self.ndta, a) for a in range(t + 1, NTT)])
            mm = total(t, 1, [("lt", self.ndta, t)] + [("ones", self.ndta, a) for a in range(t)])
        mm.then_inc(st.sem, 1)
        pe.wait_ge(st.sem, self.steps + 5)
        for t in range(LTT):
            mm = pe.transpose(k.ps[0:32, 2, t * P:(t + 1) * P], self.A[:, t, :], k.c("ident"))
        mm.then_inc(st.sem, 1)

    def scalar(self, act):
        k, st = self.k, self.k.sig("dt_steps")
        act.wait_ge(st.sem, self.steps + 1)
        act.activation(self.ea, k.vec("a_log"), ACT.Exp)
        act.activation(self.e, self.e, ACT.Exp, scale=-1.0).then_inc(st.sem, 1)

    def vector(self, dve):
        k, st = self.k, self.k.sig("dt_steps")
        x, e, s, s2, r = self.x, self.e, self.s, self.s2, self.r
        over = lambda v: v.unsqueeze(1).to_broadcast([P, NTT, 32])
        dve.wait_ge(k.sig("unit_used").sem, self.u0 + 8)
        dve.tensor_tensor(x, k.ps[:, 0, 0:192].rearrange("p (a b) -> p a b", a=NTT),
                          over(k.vec("dt_bias")), ALU.add).then_inc(k.dve.count(), 1)
        dve.wait_ge(k.dve.sem, k.dve.value())
        dve.tensor_scalar(r, x, -1.0, None, ALU.mult).then_inc(k.dve.count(), 1)
        dve.wait_ge(k.dve.sem, k.dve.value())
        dve.tensor_tensor(e, x, r, ALU.max).then_inc(st.sem, 1)
        dve.wait_ge(st.sem, self.steps + 2)
        dve.tensor_scalar(r, e, 2.0, None, ALU.add).then_inc(k.dve.count(), 1)
        dve.wait_ge(k.dve.sem, k.dve.value())
        dve.reciprocal(r, r).then_inc(k.dve.count(), 1)
        dve.wait_ge(k.dve.sem, k.dve.value())
        dve.tensor_tensor(s, e, r, ALU.mult).then_inc(k.dve.count(), 1)
        dve.wait_ge(k.dve.sem, k.dve.value())
        dve.tensor_tensor(s2, s, s, ALU.mult).then_inc(k.dve.count(), 1)
        dve.wait_ge(k.dve.sem, k.dve.value())
        dve.tensor_scalar(r, s2, 1.0 / 15, 1.0 / 13, ALU.mult, ALU.add).then_inc(k.dve.count(), 1)
        dve.wait_ge(k.dve.sem, k.dve.value())
        for n in (11, 9, 7, 5, 3, 1):
            dve.tensor_tensor(r, r, s2, ALU.mult).then_inc(k.dve.count(), 1)
            dve.wait_ge(k.dve.sem, k.dve.value())
            dve.tensor_scalar(r, r, 1.0 / n, None, ALU.add).then_inc(k.dve.count(), 1)
            dve.wait_ge(k.dve.sem, k.dve.value())
        dve.tensor_tensor(r, r, s, ALU.mult).then_inc(k.dve.count(), 1)
        dve.wait_ge(k.dve.sem, k.dve.value())
        dve.tensor_scalar(r, r, 2.0, None, ALU.mult).then_inc(k.dve.count(), 1)
        dve.wait_ge(k.dve.sem, k.dve.value())
        dve.scalar_tensor_tensor(out=self.dt, in0=x, scalar=0.0, in1=r, op0=ALU.max, op1=ALU.add).then_inc(k.dve.count(), 1)
        dve.wait_ge(k.dve.sem, k.dve.value())
        dve.tensor_tensor(self.ndta, self.dt, over(self.ea), ALU.mult).then_inc(k.dve.count(), 1)
        dve.wait_ge(k.dve.sem, k.dve.value())
        dve.tensor_scalar(self.dta, self.ndta, -1.0, None, ALU.mult).then_inc(st.sem, 1)
        dve.wait_ge(st.sem, self.steps + 4)
        a = k.ps[:, 1, 0:192].rearrange("p (a b) -> p a b", a=NTT)
        dve.tensor_scalar(self.nA, a, -1.0, None, ALU.mult)
        dve.tensor_copy(self.A, a).then_inc(st.sem, 1)
        dve.wait_ge(st.sem, self.steps + 6)
        dve.tensor_copy(self.AT[0:32, :], k.ps[0:32, 2, :])


class Scan(Stage):

    def __init__(self, k, g, bufs, Y, dt, nA, AT, off):
        self.k, self.g, self.Y, self.dt, self.nA, self.AT = k, g, Y, dt, nA, AT
        self.B, self.C, self.xs = bufs[0], bufs[1], bufs[2:4]
        self.xt = k.at(off, NTT, 256)
        self.cb = k.at(off + 1536, NTT, T)
        self.M = k.at(off + 4608, NTT, T)
        self.E = k.at(off + 7680, 4, 1024)
        self.dg = k.at(off + 11776, 2, LTT, 2 * P)
        n = 4 * NTT
        self.pre = k.sig("turned_ready").take(3 + NTT)
        self.pre_t = k.sig("turned_taken").take(3 + NTT)
        self.abc = k.sig("sums_spread").take(4)
        self.cap = k.sig("capped").take(4)
        self.e_rdy = k.sig("exp_ready").take(n)
        self.m_rdy = k.sig("decayed_ready").take(n)
        self.y_tak = k.sig("heads_taken").take(2)
        self.y_rdy = k.sig("heads_ready").take(n)

    def tensor(self, pe):
        k = self.k
        for b in range(3):
            for t in (2 * b, 2 * b + 1):
                for c in range(2):
                    mm = pe.transpose(k.ps[:, b, (t % 2) * 256 + c * P:(t % 2) * 256 + (c + 1) * P],
                                      self.xs[c][:, t * P:(t + 1) * P], k.c("ident"))
            mm.then_inc(k.sig("turned_ready").sem, 1)
        for t in range(NTT):
            if t >= 1:
                pe.wait_ge(k.sig("turned_taken").sem, self.pre_t + (t if t < 4 else t))
            pe.matmul(k.ps[:, (3 + t) % 4, :], lhsT=self.B[:, t * P:(t + 1) * P], rhs=self.C[:, 0:T],
                      start=True, stop=True).then_inc(k.sig("turned_ready").sem, 1)

        def spread(r):
            if r >= 1:
                pe.wait_ge(k.sig("exp_ready").sem, self.e_rdy + r * NTT)
            for d in range(2):
                col = d * 16 + self.g * 4 + r
                mm = pe.matmul(k.ps[:, 4 + d, :], lhsT=k.c("ident")[0:32, col:col + 1].to_broadcast([32, P]),
                               rhs=self.AT[0:32, :], start=True, stop=True)
            mm.then_inc(k.sig("sums_spread").sem, 1)

        def out(r):
            half = (r % 2) * 64
            for t in range(NTT):
                n = r * NTT + t
                pe.wait_ge(k.sig("decayed_ready").sem, self.m_rdy + n + 1)
                pe.matmul(k.ps[half:half + 64, 6 + r // 2, :], lhsT=self.xt[:, t, r * 64:(r + 1) * 64],
                          rhs=self.M[:, t, :], start=t == 0, stop=t == NTT - 1)\
                    .then_inc(k.sig("heads_ready").sem, 1)
                if t == 3 and r < 3:
                    spread(r + 1)

        spread(0)
        for r in range(4):
            out(r)

    def scalar(self, act):
        k = self.k
        for b in range(3):
            act.wait_ge(k.sig("turned_ready").sem, self.pre + b + 1)
            act.copy(self.xt[:, 2 * b:2 * b + 2, :], k.ps[:, b, :].rearrange("p (a b) -> p a b", a=2))\
                .then_inc(k.sig("turned_taken").sem, 1)
        for t in range(NTT):
            act.wait_ge(k.sig("turned_ready").sem, self.pre + 3 + t + 1)
            act.copy(self.cb[:, t, :], k.ps[:, (3 + t) % 4, :]).then_inc(k.sig("turned_taken").sem, 1)
        for r in range(4):
            f, b = self.g * 4 + r, 16 + self.g * 4 + r
            act.wait_ge(k.sig("capped").sem, self.cap + r + 1)
            act.activation(self.dg[:, r % 2], self.dg[:, r % 2], ACT.Exp)
            for t in range(NTT):
                n = r * NTT + t
                E = self.E[:, n % 4, :]
                if n >= 4:
                    act.wait_ge(k.sig("decayed_ready").sem, self.m_rdy + n - 3)
                bf, bb = self.nA[:, t, f:f + 1], self.nA[:, t, b:b + 1]
                if t < LTT:
                    if t < LTT - 1:
                        a = act.activation(E[:, (t + 1) * P:T], k.ps[:, 4, (t + 1) * P:T], ACT.Exp, bias=bf)
                    if t > 0:
                        a = act.activation(E[:, 0:t * P], k.ps[:, 5, 0:t * P], ACT.Exp, bias=bb)
                else:
                    act.activation(E[:, 0:T], k.ps[:, 4, :], ACT.Exp, bias=bf)
                    a = act.activation(E[:, T:2 * T], k.ps[:, 5, :], ACT.Exp, bias=bb)
                a.then_inc(k.sig("exp_ready").sem, 1)

    def vector(self, dve):
        k = self.k

        def cap(r):
            dve.wait_ge(k.sig("sums_spread").sem, self.abc + r + 1)
            for t in range(LTT):
                for d, m in ((0, "negf"), (1, "negb")):
                    col = d * 16 + self.g * 4 + r
                    a = dve.scalar_tensor_tensor(out=self.dg[:, r % 2, t, d * P:(d + 1) * P],
                                                 in0=k.ps[:, 4 + d, t * P:(t + 1) * P], scalar=self.nA[:, t, col:col + 1],
                                                 in1=k.c(m), op0=ALU.add, op1=ALU.min)
            a.then_inc(k.sig("capped").sem, 1)

        cap(0)
        dve.wait_ge(k.sig("turned_taken").sem, self.pre_t + 3 + NTT)
        for r in range(4):
            f, b = self.g * 4 + r, 16 + self.g * 4 + r
            for t in range(NTT):
                if t == 5 and r < 3:
                    cap(r + 1)
                n = r * NTT + t
                E, M, cb = self.E[:, n % 4, :], self.M[:, t, :], self.cb[:, t, :]
                df, db = self.dt[:, t, f:f + 1], self.dt[:, t, b:b + 1]
                dve.wait_ge(k.sig("exp_ready").sem, self.e_rdy + n + 1)
                if r >= 1:
                    dve.wait_ge(k.sig("heads_ready").sem, self.y_rdy + n - NTT + 1)
                if t < LTT:
                    o = t * P
                    dg = self.dg[:, r % 2, t]
                    e0, e1, span = dg[:, 0:P], dg[:, P:2 * P], slice(o, o + P)
                    if t < LTT - 1:
                        dve.scalar_tensor_tensor(out=M[:, o + P:T], in0=E[:, o + P:T], scalar=df, in1=cb[:, o + P:T],
                                                 op0=ALU.mult, op1=ALU.mult)
                else:
                    e0, e1, span = E[:, 0:T], E[:, T:2 * T], slice(0, T)
                dve.tensor_scalar(e0, e0, df, None, ALU.mult).then_inc(k.dve.count(), 1)
                if 0 < t < LTT:
                    dve.scalar_tensor_tensor(out=M[:, 0:o], in0=E[:, 0:o], scalar=db, in1=cb[:, 0:o],
                                             op0=ALU.mult, op1=ALU.mult)
                dve.wait_ge(k.dve.sem, k.dve.value())
                dve.scalar_tensor_tensor(out=e0, in0=e1, scalar=db, in1=e0, op0=ALU.mult, op1=ALU.add).then_inc(k.dve.count(), 1)
                dve.wait_ge(k.dve.sem, k.dve.value())
                dve.tensor_tensor(M[:, span], e0, cb[:, span], ALU.mult).then_inc(k.sig("decayed_ready").sem, 1)
            if r % 2 == 1:
                dve.wait_ge(k.sig("heads_ready").sem, self.y_rdy + (r + 1) * NTT)
                c = 2 * self.g + r // 2
                dve.scalar_tensor_tensor(out=self.Y[:, c, :], in0=self.xs[r // 2][:, 0:T],
                                         scalar=k.vec("d_skip", c, c + 1), in1=k.ps[:, 6 + r // 2, :],
                                         op0=ALU.mult, op1=ALU.add)


class Router(Stage):

    def __init__(self, k, w, shared, h_rows, m):
        self.k, self.w, self.shared, self.h_rows, self.m = k, w, shared, h_rows, m
        self.u0 = k.units(8)
        self.us = k.units(6)
        k.sig("unit_used").take(14)
        off = m.WG0
        self.sc, self.sel, self.ms, self.mr, self.wt = (k.at(off + 256 * j, LTT, NE) for j in range(5))
        self.cmp, self.cm2 = k.at(off + 1280, LTT, 8, 8), k.at(off + 1536, LTT, 8, 8)
        self.m8 = k.at(off + 1792, LTT, 8, 8)
        self.gs, self.gm, self.v8 = (k.at(off + 2048 + 32 * j, LTT, 8) for j in range(3))
        self.sm, self.rs = k.at(off + 2144, LTT), k.at(off + 2148, LTT)
        off += 2152
        self.ch, self.place = k.at(off, LTT, NE), k.at(off + 256, LTT, NE)
        self.bounds, self.cum = k.at(off + 512, 2 * NE), k.at(off + 640, 2 * NE)
        self.ends = k.at(off + 768, MAXB)
        self.eb = k.at(off + 864, MAXB)
        self.nb, self.nc, self.endc = (k.at(off + 960 + j, 1) for j in range(3))
        self.a8, self.b8, self.r8 = (k.at(off + 964 + 32 * j, LTT, 8) for j in range(3))
        self.eq = m.y.rearrange("p a (b c) -> p (a b) c", c=8 * NE).rearrange("p a (b c) -> p a b c", c=NE)
        self.iota = k.at(off + 1060, P + LTT)
        off += 1060 + P + LTT
        self.rhot, self.bhot = k.at(off, LTT * 8, P), k.at(off + 4096, LTT * 8, MAXB)
        assert off + 4096 + LTT * 8 * MAXB <= m.end
        self.pe_s = k.sig("route_product").take(4)
        self.dve_s = k.sig("route_step").take(5)
        self.got = k.sig("iota_loaded").take(16)
        self.turned = k.sig("rows_turned").take(8)
        self.rows_taken = k.sig("rows_taken").take(8)
        self.rows_stored = k.sig("rows_stored").take(16)
        self.sh_taken = k.sig("shared_taken").take(4)
        self.sh_hid = k.sig("shared_hidden").take(1)
        self.sh_down = k.sig("shared_down").take(6)
        self.sh_acc = k.sig("shared_acc").take(8)

    def sync(self, sp):
        k = self.k
        ring_loads(k, sp, lambda i, j, c: self.w[0, :, 0:c], self.u0, 8, lambda j: 512)
        ring_loads(k, sp, lambda i, j, c: self.shared[i + j, :, 0:c], self.us, 6)

    def tensor(self, pe):
        k, m = self.k, self.m
        for j in range(8):
            pe.wait_ge(k.slot[(self.u0 + j) % SLOTS], slot_count(self.u0 + j))
        for t in range(LTT):
            for c in range(KD):
                mm = pe.matmul(k.ps[:, 0, t * NE:(t + 1) * NE], lhsT=k.H[:, c, t * P:(t + 1) * P],
                               rhs=k.ring[:, self.u0 % SLOTS, c * NE:(c + 1) * NE], start=c == 0, stop=c == KD - 1)
        mm.then_inc(k.sig("unit_used").sem, 8)
        for n in range(8):
            t, half = n // 2, n % 2
            if n >= 2:
                pe.wait_ge(k.sig("rows_taken").sem, self.rows_taken + n - 1)
            for c in range(4):
                mm = pe.transpose(k.ps[:, 6 + half, c * P:(c + 1) * P], k.H[:, 4 * half + c, t * P:(t + 1) * P],
                                  k.c("ident"))
            mm.then_inc(k.sig("rows_turned").sem, 1)
        for f in range(2):
            for h in range(2):
                u = self.us + 2 * f + h
                pe.wait_ge(k.slot[u % SLOTS], slot_count(u))
                for c in range(KD):
                    mm = pe.matmul(k.ps[:, 2 + 2 * f + h, :], lhsT=k.ring[:, u % SLOTS, c * P:(c + 1) * P],
                                   rhs=k.H[:, c, 0:T], start=c == 0, stop=c == KD - 1)
                mm.then_inc(k.sig("unit_used").sem, 1)
        pe.wait_ge(k.sig("route_step").sem, self.dve_s + 1)
        for t in range(LTT):
            for s in range(t + 1):
                pe.matmul(k.ps[:, 0, t * NE:(t + 1) * NE], lhsT=k.c("lt" if s == t else "ones"), rhs=self.ch[:, s, :],
                          start=s == 0, stop=s == t)
        for s in range(LTT):
            mm = pe.matmul(k.ps[0:NE, 0, 256:257], lhsT=self.ch[:, s, :], rhs=k.c("ones")[:, 0:1],
                           start=s == 0, stop=s == LTT - 1)
        mm.then_inc(k.sig("route_product").sem, 1)
        pe.wait_ge(k.sig("route_step").sem, self.dve_s + 2)
        pe.matmul(k.ps[:, 1, 0:2 * NE], lhsT=k.c("ones")[0:NE, :], rhs=self.bounds[0:NE, :], start=True, stop=True)
        pe.matmul(k.ps[0:NE, 1, 128:129], lhsT=k.c("ge")[0:NE, 0:NE], rhs=self.nb[0:NE, :], start=True, stop=True)\
            .then_inc(k.sig("route_product").sem, 1)
        pe.wait_ge(k.sig("route_step").sem, self.dve_s + 3)
        pe.matmul(k.ps[:, 1, 0:MAXB], lhsT=k.c("ones")[0:NE, :], rhs=self.ends[0:NE, :], start=True, stop=True)\
            .then_inc(k.sig("route_product").sem, 1)
        pe.wait_ge(k.sig("shared_hidden").sem, self.sh_hid + 1)
        for n in range(8):
            half, t = n // 4, n % 4
            u = self.us + 4 + half
            if t == 0:
                pe.wait_ge(k.slot[u % SLOTS], slot_count(u))
            if n >= 4:
                pe.wait_ge(k.sig("shared_acc").sem, self.sh_acc + n - 3)
            for f in range(2):
                o = (t * 2 + f) * P
                mm = pe.matmul(k.ps[:, 2 + t, :], lhsT=k.ring[:, u % SLOTS, o:o + P], rhs=m.s_hid[:, f, :],
                               start=f == 0, stop=f == 1)
            mm.then_inc(k.sig("shared_down" if t < 3 else "unit_used").sem, 1)
        pe.wait_ge(k.sig("route_step").sem, self.dve_s + 5)
        for n in range(LTT * 8):
            mm = pe.matmul(k.ps[:, 0, 0:MAXB], lhsT=self.rhot[:, n, :], rhs=self.bhot[:, n, :],
                           start=n == 0, stop=n == LTT * 8 - 1)
        mm.then_inc(k.sig("route_product").sem, 1)

    def scalar(self, act):
        k, m = self.k, self.m
        act.wait_ge(k.sig("unit_used").sem, self.u0 + 8)
        act.activation(self.sc, k.ps[:, 0, 0:256].rearrange("p (a b) -> p a b", a=LTT), ACT.Sigmoid)\
            .then_inc(k.sig("scores_made").sem, 1)
        for n in range(8):
            act.wait_ge(k.sig("rows_turned").sem, self.turned + n + 1)
            act.copy(m.h_tok[:, n // 2, (n % 2) * T:(n % 2 + 1) * T], k.ps[:, 6 + n % 2, :])\
                .then_inc(k.sig("rows_taken").sem, 1)
        for f in range(2):
            act.wait_ge(k.sig("unit_used").sem, self.us + 2 * f + 2)
            act.activation(m.s_sg[:, f, :], k.ps[:, 2 + 2 * f, :], ACT.Silu).then_inc(k.sig("shared_taken").sem, 1)
            act.copy(m.s_up[:, f, :], k.ps[:, 3 + 2 * f, :]).then_inc(k.sig("shared_taken").sem, 1)
        for n in range(8):
            half, t = n // 4, n % 4
            if t < 3:
                act.wait_ge(k.sig("shared_down").sem, self.sh_down + 3 * half + t + 1)
            else:
                act.wait_ge(k.sig("unit_used").sem, self.us + 5 + half)
            act.copy(m.acc[:, n, :], k.ps[:, 2 + t, :]).then_inc(k.sig("shared_acc").sem, 1)

    def gpsimd(self, pool):
        k, m = self.k, self.m
        pool.dma_start(self.iota, m.iota).then_inc(k.sig("iota_loaded").sem, 16)
        pool.wait_ge(k.sig("rows_taken").sem, self.rows_taken + 8)
        pool.dma_start(self.h_rows.rearrange("(a p) d -> p a d", p=P), m.h_tok)\
            .then_inc(k.sig("rows_stored").sem, 16)
        pool.wait_ge(k.sig("shared_taken").sem, self.sh_taken + 4)
        for f in range(2):
            pool.tensor_tensor(m.s_hid[:, f, :], m.s_sg[:, f, :], m.s_up[:, f, :], ALU.mult)\
                .then_inc(k.sig("shared_halves").sem, 1)
        pool.wait_ge(k.sig("shared_halves").sem, 2)
        pool.memset(m.done, 0.0).then_inc(k.sig("shared_hidden").sem, 1)
        pool.wait_ge(k.sig("rows_stored").sem, self.rows_stored + 16)

    def vector(self, dve):
        k, m = self.k, self.m
        dve.wait_ge(k.sig("scores_made").sem, 1)
        dve.tensor_tensor(self.sel, self.sc, k.vec("rbias").unsqueeze(1).to_broadcast([P, LTT, NE]), ALU.add)\
            .then_inc(k.dve.count(), 1)
        dve.wait_ge(k.dve.sem, k.dve.value())
        for t in range(LTT):
            for g in range(8):
                dve.max(self.m8[:, t, g, :], self.sel[:, t, g * 8:(g + 1) * 8]).then_inc(k.dve.count(), 1)
        dve.wait_ge(k.dve.sem, k.dve.value())
        dve.tensor_tensor(self.gs, self.m8[:, :, :, 0], self.m8[:, :, :, 1], ALU.add).then_inc(k.dve.count(), 1)
        dve.wait_ge(k.dve.sem, k.dve.value())
        for t in range(LTT):
            mine = self.gs[:, t, :].unsqueeze(2).to_broadcast([P, 8, 8])
            other = self.gs[:, t, :].unsqueeze(1).to_broadcast([P, 8, 8])
            dve.tensor_tensor(self.cmp[:, t], other, mine, ALU.is_gt)
            dve.tensor_tensor(self.cm2[:, t], other, mine, ALU.is_equal).then_inc(k.dve.count(), 1)
        dve.wait_ge(k.dve.sem, k.dve.value())
        bef = k.vec("before").rearrange("p (a b) -> p a b", a=8)
        for t in range(LTT):
            dve.tensor_tensor(self.cm2[:, t], self.cm2[:, t], bef, ALU.mult).then_inc(k.dve.count(), 1)
        dve.wait_ge(k.dve.sem, k.dve.value())
        dve.tensor_tensor(self.cmp, self.cmp, self.cm2, ALU.add).then_inc(k.dve.count(), 1)
        dve.wait_ge(k.dve.sem, k.dve.value())
        dve.tensor_reduce(self.gm, self.cmp, AX.X, ALU.add).then_inc(k.dve.count(), 1)
        dve.wait_ge(k.dve.sem, k.dve.value())
        dve.tensor_scalar(self.gm, self.gm, 3.5, NEG, ALU.is_gt, ALU.mult).then_inc(k.dve.count(), 1)
        dve.wait_ge(k.dve.sem, k.dve.value())
        for t in range(LTT):
            dve.tensor_tensor(self.ms[:, t].rearrange("p (a b) -> p a b", a=8),
                              self.sel[:, t].rearrange("p (a b) -> p a b", a=8),
                              self.gm[:, t].unsqueeze(2).to_broadcast([P, 8, 8]), ALU.add).then_inc(k.dve.count(), 1)
        dve.wait_ge(k.dve.sem, k.dve.value())
        for t in range(LTT):
            dve.max(self.v8[:, t], self.ms[:, t]).then_inc(k.dve.count(), 1)
        dve.wait_ge(k.dve.sem, k.dve.value())
        for t in range(LTT):
            dve.match_replace(out=self.mr[:, t], in_to_replace=self.v8[:, t], in_values=self.ms[:, t],
                              imm_value=-BIG).then_inc(k.dve.count(), 1)
        dve.wait_ge(k.dve.sem, k.dve.value())
        dve.tensor_scalar(self.ch, self.mr, -2e38, None, ALU.is_lt).then_inc(k.sig("route_step").sem, 1)
        dve.wait_ge(k.sig("route_step").sem, self.dve_s + 1)
        dve.tensor_tensor(self.wt, self.ch, self.sc, ALU.mult).then_inc(k.dve.count(), 1)
        dve.wait_ge(k.dve.sem, k.dve.value())
        dve.tensor_reduce(self.sm, self.wt, AX.X, ALU.add).then_inc(k.dve.count(), 1)
        dve.wait_ge(k.dve.sem, k.dve.value())
        dve.reciprocal(self.rs, self.sm).then_inc(k.dve.count(), 1)
        dve.wait_ge(k.dve.sem, k.dve.value())
        for t in range(LTT):
            dve.tensor_scalar(self.wt[:, t], self.wt[:, t], self.rs[:, t:t + 1], 2.5, ALU.mult, ALU.mult)
        nc, nb = self.nc[0:NE, :], self.nb[0:NE, :]
        dve.wait_ge(k.sig("route_product").sem, self.pe_s + 1)
        dve.tensor_copy(nc, k.ps[0:NE, 0, 256:257]).then_inc(k.dve.count(), 1)
        dve.wait_ge(k.dve.sem, k.dve.value())
        dve.tensor_scalar(nb, nc, 0.5, None, ALU.is_gt).then_inc(k.dve.count(), 1)
        for b in range(1, LTT):
            dve.wait_ge(k.dve.sem, k.dve.value())
            dve.scalar_tensor_tensor(out=nb, in0=nc, scalar=P * b + 0.5, in1=nb, op0=ALU.is_gt, op1=ALU.add)\
                .then_inc(k.dve.count(), 1)
        dve.wait_ge(k.dve.sem, k.dve.value())
        dve.tensor_scalar(self.bounds[0:NE, 0:NE], k.c("ge")[0:NE, 0:NE], nb, None, ALU.mult)\
            .then_inc(k.dve.count(), 1)
        dve.wait_ge(k.dve.sem, k.dve.value())
        dve.tensor_scalar(self.bounds[0:NE, NE:2 * NE], k.c("lt")[0:NE, 0:NE], nb, None, ALU.mult)\
            .then_inc(k.sig("route_step").sem, 1)
        dve.wait_ge(k.sig("iota_loaded").sem, self.got + 16)
        dve.wait_ge(k.sig("route_product").sem, self.pe_s + 2)
        dve.tensor_copy(self.endc[0:NE, :], k.ps[0:NE, 1, 128:129]).then_inc(k.dve.count(), 1)
        dve.tensor_copy(self.cum, k.ps[:, 1, 0:2 * NE]).then_inc(k.dve.count(), 1)
        dve.wait_ge(k.dve.sem, k.dve.value())
        dve.tensor_scalar(self.ends[0:NE, :], self.iota[0:NE, 0:MAXB], self.endc[0:NE, :], None, ALU.is_ge)\
            .then_inc(k.sig("route_step").sem, 1)
        for t in range(LTT):
            dve.scalar_tensor_tensor(out=self.place[:, t], in0=self.cum[:, NE:2 * NE], scalar=float(P),
                                     in1=k.ps[:, 0, t * NE:(t + 1) * NE], op0=ALU.mult, op1=ALU.add)\
                .then_inc(k.dve.count(), 1)
        dve.wait_ge(k.dve.sem, k.dve.value())
        dve.scalar_tensor_tensor(out=self.place, in0=self.place, scalar=1.0, in1=self.ch, op0=ALU.add, op1=ALU.mult)\
            .then_inc(k.dve.count(), 1)
        dve.wait_ge(k.dve.sem, k.dve.value())
        for t in range(LTT):
            dve.max(self.v8[:, t], self.place[:, t]).then_inc(k.dve.count(), 1)
        dve.wait_ge(k.dve.sem, k.dve.value())
        dve.tensor_scalar(self.a8, self.v8, -1.0, None, ALU.add).then_inc(k.dve.count(), 1)
        dve.wait_ge(k.dve.sem, k.dve.value())
        dve.tensor_copy(m.places, self.a8)
        dve.tensor_scalar(self.b8, self.a8, 1.0 / P, -63.5 / P, ALU.mult, ALU.add).then_inc(k.dve.count(), 1)
        for v in (12582912.0, -12582912.0):
            dve.wait_ge(k.dve.sem, k.dve.value())
            dve.tensor_scalar(self.b8, self.b8, v, None, ALU.add).then_inc(k.dve.count(), 1)
        dve.wait_ge(k.dve.sem, k.dve.value())
        dve.scalar_tensor_tensor(out=self.r8, in0=self.b8, scalar=-float(P), in1=self.a8, op0=ALU.mult, op1=ALU.add)\
            .then_inc(k.dve.count(), 1)
        dve.wait_ge(k.dve.sem, k.dve.value())
        dve.wait_ge(k.sig("route_product").sem, self.pe_s + 3)
        dve.tensor_scalar(self.eb, k.ps[:, 1, 0:MAXB], NE - 1.0, None, ALU.min).then_inc(k.dve.count(), 1)
        dve.tensor_scalar(self.ends, k.ps[:, 1, 0:MAXB], NE - 0.5, None, ALU.is_lt).then_inc(k.dve.count(), 1)
        dve.wait_ge(k.dve.sem, k.dve.value())
        dve.tensor_copy(m.expert, self.eb[0:1, :])
        dve.tensor_reduce(self.nc, self.ends[:, 0:MAXB:2], AX.X, ALU.add).then_inc(k.dve.count(), 1)
        dve.wait_ge(k.dve.sem, k.dve.value())
        dve.tensor_copy(m.pairs, self.nc[0:1, :]).then_inc(k.sig("route_step").sem, 1)
        for t in range(LTT):
            for j in range(8):
                n = t * 8 + j
                dve.tensor_scalar(self.rhot[:, n, :], self.iota[:, 0:P], self.r8[:, t, j:j + 1], None, ALU.is_equal)
                a = dve.tensor_scalar(self.bhot[:, n, :], self.iota[:, 0:MAXB], self.b8[:, t, j:j + 1],
                                      self.iota[:, P + t:P + t + 1], ALU.is_equal, ALU.mult)
        a.then_inc(k.sig("route_step").sem, 1)
        for t in range(LTT):
            dve.tensor_tensor(self.eq[:, t], self.place[:, t].unsqueeze(1).to_broadcast([P, 8, NE]),
                              self.v8[:, t].unsqueeze(2).to_broadcast([P, 8, NE]), ALU.is_equal)\
                .then_inc(k.dve.count(), 1)
        dve.wait_ge(k.dve.sem, k.dve.value())
        for t in range(LTT):
            dve.tensor_tensor(self.eq[:, t], self.eq[:, t], self.wt[:, t].unsqueeze(1).to_broadcast([P, 8, NE]),
                              ALU.mult).then_inc(k.dve.count(), 1)
        dve.wait_ge(k.dve.sem, k.dve.value())
        for t in range(LTT):
            dve.tensor_reduce(m.w8[:, t], self.eq[:, t], AX.X, ALU.add)
        dve.wait_ge(k.sig("route_product").sem, self.pe_s + 4)
        dve.tensor_copy(m.list, k.ps[:, 0, 0:MAXB]).then_inc(k.sig("plan_ready").sem, 1)


class MoeMemory:

    def __init__(self, k, iota, off):
        self.iota = iota
        self.acc = k.at(off, KD, T)
        off += KD * T
        self.places, self.w8 = k.at(off, LTT * 8).bitcast(U32), k.at(off + 32, LTT, 8)
        self.list, self.col = k.at(off + 64, MAXB).bitcast(U32), k.at(off + 160, 2).bitcast(U32)
        self.done = k.at(off + 162, 1)
        self.expert = k.at(off + 164, MAXB)[0:1, :].bitcast(I32)
        self.pairs = k.at(off + 260, 1)[0:1, :].bitcast(I32)
        off += 264
        self.s_sg, self.s_up, self.s_hid = (k.at(off + 1024 * j, 2, T) for j in range(3))
        off += 3072
        self.h_tok = k.at(off, LTT, D)
        self.x_rows, self.xT = k.at(off, 2, D), k.at(off + 2048, 2, KD, P)
        off += 4096
        self.sg, self.hid, self.hT = (k.at(off + 512 * j, 2, 256) for j in range(3))
        off += 1536
        self.y = k.at(off, 2, D)
        off += 2048
        self.WG0 = off
        self.WG, self.WD = k.at(off, 2, KD, 512), k.at(off + 8192, 2, 2, D)
        self.G = k.at(off, 8, D)
        self.y_tok = k.at(off + 8192, 2, D)
        self.end = off + 12288


class Experts(Stage):

    def __init__(self, k, w_gu, w_down, h_rows, y_rows, m):
        self.k, self.w_gu, self.w_down, self.h_rows, self.y_rows, self.m = k, w_gu, w_down, h_rows, y_rows, m
        self.plan = k.sig("plan_ready").take(1)

    def blocks(self, eng, step):
        pairs = eng.value_load(self.m.pairs, min_val=MINB // 2, max_val=MAXB // 2)
        step(0, 0, 0)
        with eng.Fori(0, pairs - 1) as i:
            step(i, 1, 1)
            step(i, 0, 2)
        step(pairs - 1, 1, 1)

    def sync(self, sp):
        k, m = self.k, self.m
        sp.wait_ge(k.sig("plan_ready").sem, self.plan + 1)

        def load(i, p, b):
            e = sp.value_load(m.expert[:, bass.ds(i * 2 + b, 1)], min_val=0, max_val=NE - 1)
            sp.wait_ge(k.sig("gate_up_made").sem, i * 2 + b - 1 + PRIME)
            for half in range(2):
                sp.dma_start(m.WG[:, p, 4 * half:4 * half + 4, :], self.w_gu[bass.ds(e, 1), :, 4 * half:4 * half + 4, :]
                             .rearrange("a p c f -> p (a c) f")).then_inc(k.sig(f"gate_weights{p}").sem, 16)
            sp.wait_ge(k.sig("down_made").sem, i * 2 + b - 1 + PRIME)
            sp.dma_start(m.WD[:, p], self.w_down[bass.ds(e, 1)].rearrange("a p c f -> p (a c) f"))\
                .then_inc(k.sig(f"down_weights{p}").sem, 16)

        self.blocks(sp, load)

    def gpsimd(self, pool):
        k, m = self.k, self.m

        def gather(i, p, b):
            pool.wait_ge(k.sig("x_turned").sem, i * 2 + b - 1 + PRIME)
            pool.tensor_copy(m.col[:, p:p + 1], m.list[:, bass.ds(i * 2 + b, 1)])\
                .then_inc(k.sig("column_copied").sem, 1)
            pool.wait_ge(k.sig("column_copied").sem, i * 2 + b + 1)
            pool.tensor_tensor(k.small[:, 34 + p:35 + p], m.w8[:, 0, 0:1], m.w8[:, 0, 0:1], ALU.add)
            pool.indirect_dma_start(m.x_rows[:, p, :], None, self.h_rows,
                                    bass.IndirectOffsetOnAxis(ap=m.col[:, p:p + 1], axis=0))\
                .then_inc(k.sig(f"rows_gathered{p}").sem, 16)

        self.blocks(pool, gather)

    def tensor(self, pe):
        k, m = self.k, self.m

        def turn_x(i, p, b):
            pe.wait_ge(k.sig(f"rows_gathered{p}").sem, i * 16 + 16 * (b // 2 + 1))
            pe.wait_ge(k.sig("x_taken").sem, i * 4 + 2 * b + PRIME)
            for c in range(KD):
                mm = pe.transpose(k.ps[:, 2 + c // 4, (c % 4) * P:(c % 4 + 1) * P], m.x_rows[:, p, c * P:(c + 1) * P],
                                  k.c("ident"))
            mm.then_inc(k.sig("x_turned").sem, 1)

        def gate_up(i, p, b):
            pe.wait_ge(k.sig("x_taken").sem, i * 4 + 2 * b + 2 + PRIME)
            pe.wait_ge(k.sig(f"gate_weights{p}").sem, i * 32 + 32 * (b // 2 + 1))
            pe.wait_ge(k.sig("h_made").sem, i * 2 + b - 1 + PRIME)
            for c in range(KD):
                mm = pe.matmul(k.ps[:, p, :], lhsT=m.xT[:, p, c, :], rhs=m.WG[:, p, c, :],
                               start=c == 0, stop=c == KD - 1)
            mm.then_inc(k.sig("gate_up_made").sem, 1)

        def down(i, p, b):
            pe.wait_ge(k.sig("hT_taken").sem, i * 2 + b + 1 + PRIME)
            pe.wait_ge(k.sig(f"down_weights{p}").sem, i * 16 + 16 * (b // 2 + 1))
            pe.wait_ge(k.sig("y_taken0").sem, i * 2 + b + PRIME)
            pe.wait_ge(k.sig("y_taken1").sem, i * 2 + b + PRIME)
            for half in range(2):
                for f in range(2):
                    mm = pe.matmul(k.ps[:, 4 + half, :], lhsT=m.hT[:, p, f * P:(f + 1) * P],
                                   rhs=m.WD[:, p, f, half * T:(half + 1) * T], start=f == 0, stop=f == 1)
            mm.then_inc(k.sig("down_made").sem, 1)

        def turn_h(i, p, b):
            pe.wait_ge(k.sig("h_made").sem, i * 2 + b + 1 + PRIME)
            pe.wait_ge(k.sig("hT_taken").sem, i * 2 + b + PRIME)
            for f in range(2):
                mm = pe.transpose(k.ps[:, 6, f * P:(f + 1) * P], m.hid[:, p, f * P:(f + 1) * P], k.c("ident"))
            mm.then_inc(k.sig("h_turned").sem, 1)

        def step(i, p, b, first=False, last=False):
            gate_up(i, p, b)
            if not last:
                turn_x(i, 1 - p, b + 1)
            if not first:
                down(i, 1 - p, b - 1)
            turn_h(i, p, b)
            if last:
                down(i, p, b)

        turn_x(0, 0, 0)
        pairs = pe.value_load(m.pairs, min_val=MINB // 2, max_val=MAXB // 2)
        step(0, 0, 0, first=True)
        with pe.Fori(0, pairs - 1) as i:
            step(i, 1, 1)
            step(i, 0, 2)
        step(pairs - 1, 1, 1, last=True)

    def scalar(self, act):
        k, m = self.k, self.m

        def silu(i, p, b):
            act.wait_ge(k.sig("gate_up_made").sem, i * 2 + b + 1 + PRIME)
            act.wait_ge(k.sig("h_made").sem, i * 2 + b - 1 + PRIME)
            act.activation(m.sg[:, p, :], k.ps[:, p, 0:256], ACT.Silu).then_inc(k.sig("silu_made").sem, 1)

        def take_x(i, p, b):
            act.wait_ge(k.sig("x_turned").sem, i * 2 + b + 1 + PRIME)
            act.wait_ge(k.sig("gate_up_made").sem, i * 2 + b - 1 + PRIME)
            for h in range(2):
                act.copy(m.xT[:, p, 4 * h:4 * h + 4, :].rearrange("p a b -> p (a b)"), k.ps[:, 2 + h, :])\
                    .then_inc(k.sig("x_taken").sem, 1)

        def take_y(i, p, b):
            act.wait_ge(k.sig("down_made").sem, i * 2 + b + 1 + PRIME)
            act.wait_ge(k.sig(f"y_stored{p}").sem, i * 16 + 16 * (b // 2 + 1))
            act.copy(m.y[:, p, 0:T], k.ps[:, 4, :]).then_inc(k.sig("y_taken0").sem, 1)
            act.wait_ge(k.sig("y_taken0").sem, i * 2 + b + 1 + PRIME)
            act.wait_ge(k.sig("y_taken1").sem, i * 2 + b + 1 + PRIME)
            act.dma_start(self.y_rows[bass.ds((i * 2 + b) * P, P), :], m.y[:, p, :])\
                .then_inc(k.sig(f"y_stored{p}").sem, 16)

        take_x(0, 0, 0)
        pairs = act.value_load(m.pairs, min_val=MINB // 2, max_val=MAXB // 2)
        silu(0, 0, 0)
        take_x(0, 1, 1)
        with act.Fori(0, pairs - 1) as i:
            for p, b in ((1, 1), (0, 2)):
                silu(i, p, b)
                take_x(i, 1 - p, b + 1)
                take_y(i, 1 - p, b - 1)
        silu(pairs - 1, 1, 1)
        take_y(pairs - 1, 0, 0)
        take_y(pairs - 1, 1, 1)
        for p in range(2):
            act.wait_ge(k.sig(f"y_stored{p}").sem, pairs * 16 + 16)
            act.copy(k.small[:, 32 + p:33 + p], m.w8[:, 0, 0:1])

    def vector(self, dve):
        k, m = self.k, self.m
        for n, name in enumerate(MOE_PRIMED):
            dve.memset(k.small[:, 16 + n:17 + n], 0.0).then_inc(k.sig(name).sem, PRIME)
        for p in range(2):
            dve.memset(k.small[:, 30 + p:31 + p], 0.0).then_inc(k.sig(f"y_stored{p}").sem, 16)

        def make_h(i, p, b):
            dve.wait_ge(k.sig("silu_made").sem, i * 2 + b + 1 + PRIME)
            dve.wait_ge(k.sig("h_turned").sem, i * 2 + b - 1 + PRIME)
            dve.tensor_tensor(m.hid[:, p, :], k.ps[:, p, 256:512], m.sg[:, p, :], ALU.mult)\
                .then_inc(k.sig("h_made").sem, 1)

        def take_y(i, p, b):
            dve.wait_ge(k.sig("down_made").sem, i * 2 + b + 1 + PRIME)
            dve.wait_ge(k.sig(f"y_stored{p}").sem, i * 16 + 16 * (b // 2 + 1))
            dve.tensor_copy(m.y[:, p, T:2 * T], k.ps[:, 5, :]).then_inc(k.sig("y_taken1").sem, 1)

        def take_h(i, p, b):
            dve.wait_ge(k.sig("h_turned").sem, i * 2 + b + 1 + PRIME)
            dve.wait_ge(k.sig("down_made").sem, i * 2 + b - 1 + PRIME)
            dve.tensor_copy(m.hT[:, p, :], k.ps[:, 6, 0:256]).then_inc(k.sig("hT_taken").sem, 1)

        pairs = dve.value_load(m.pairs, min_val=MINB // 2, max_val=MAXB // 2)
        make_h(0, 0, 0)
        take_h(0, 0, 0)
        with dve.Fori(0, pairs - 1) as i:
            for p, b in ((1, 1), (0, 2)):
                make_h(i, p, b)
                take_y(i, 1 - p, b - 1)
                take_h(i, p, b)
        make_h(pairs - 1, 1, 1)
        take_y(pairs - 1, 0, 0)
        take_h(pairs - 1, 1, 1)
        take_y(pairs - 1, 1, 1)


class Combine(Stage):

    def __init__(self, k, y_rows, m):
        self.k, self.y_rows, self.m = k, y_rows, m
        self.g_rdy = [k.sig(f"y_gathered{b}").take(16 * LTT) for b in range(8)]
        self.w_rdy = k.sig("row_weighted").take(LTT * 8)
        self.y_trn = k.sig("y_turned").take(2 * LTT)
        self.a_rdy = k.sig("acc_added").take(2 * LTT)

    def gpsimd(self, pool):
        k, m = self.k, self.m
        for n in range(LTT * 8):
            if n >= 8:
                pool.wait_ge(k.sig("row_weighted").sem, self.w_rdy + n - 7)
            pool.indirect_dma_start(m.G[:, n % 8, :], None, self.y_rows,
                                    bass.IndirectOffsetOnAxis(ap=m.places[:, n:n + 1], axis=0))\
                .then_inc(k.sig(f"y_gathered{n % 8}").sem, 16)

    def vector(self, dve):
        k, m = self.k, self.m

        def add(t):
            for h in range(2):
                dve.wait_ge(k.sig("y_turned").sem, self.y_trn + 2 * t + h + 1)
                a = m.acc[:, 4 * h:4 * h + 4, t * P:(t + 1) * P]
                dve.tensor_tensor(a, k.ps[:, 2 * (t % 2) + h, :].rearrange("p (a b) -> p a b", a=4), a, ALU.add)\
                    .then_inc(k.sig("acc_added").sem, 1)

        for t in range(LTT):
            y = m.y_tok[:, t % 2, :]
            for j in range(8):
                n = t * 8 + j
                dve.wait_ge(k.sig(f"y_gathered{j}").sem, self.g_rdy[j] + 16 * (t + 1))
                w = m.w8[:, t, j:j + 1]
                if j == 0:
                    if t >= 2:
                        dve.wait_ge(k.sig("y_turned").sem, self.y_trn + 2 * (t - 1))
                    dve.tensor_scalar(y, m.G[:, j, :], w, None, ALU.mult).then_inc(k.sig("row_weighted").sem, 1)
                else:
                    dve.wait_ge(k.sig("row_weighted").sem, self.w_rdy + n)
                    dve.scalar_tensor_tensor(out=y, in0=m.G[:, j, :], scalar=w, in1=y, op0=ALU.mult, op1=ALU.add)\
                        .then_inc(k.sig("row_weighted").sem, 1)
            if t >= 1:
                add(t - 1)
        add(LTT - 1)

    def tensor(self, pe):
        k, m = self.k, self.m
        for t in range(LTT):
            pe.wait_ge(k.sig("row_weighted").sem, self.w_rdy + 8 * (t + 1))
            for h in range(2):
                if t >= 2:
                    pe.wait_ge(k.sig("acc_added").sem, self.a_rdy + 2 * (t - 2) + h + 1)
                for c in range(4):
                    mm = pe.transpose(k.ps[:, 2 * (t % 2) + h, c * P:(c + 1) * P],
                                      m.y_tok[:, t % 2, (4 * h + c) * P:(4 * h + c + 1) * P], k.c("ident"))
                mm.then_inc(k.sig("y_turned").sem, 1)


class LoadContext(Stage):

    def __init__(self, k, dram):
        self.k, self.dram = k, dram
        self.got = k.sig("context_loaded").take(16)

    def gpsimd(self, pool):
        k = self.k
        pool.dma_start(k.X[:, :, T:N], self.dram["ctx2T"]).then_inc(k.sig("context_loaded").sem, 16)
        pool.wait_ge(k.sig("context_loaded").sem, self.got + 16)


def plan(k, d):
    F = k.free
    st = [Load(k, d)]
    add = st.append
    add(Mods(k, 0, d["ada0"], "c0"))
    add(Norm(k, k.X, 0, 1, 0, k.H))
    QK, V, U, G = k.at(F, 8, N), k.at(F + 6144, NTT, 512), k.at(F + 9216, 4, N), k.at(F + 12288, NTT, 512)
    add(Linear(k, d["hyb_qku"], 8, k.H, QK))
    add(Linear(k, d["hyb_qku"], 4, k.H, U, func=ACT.Gelu_apprx_tanh, t0=8))
    add(TokLinear(k, d["hyb_vg"], 1, V))
    add(TokLinear(k, d["hyb_vg"], 1, G, func=ACT.Gelu_apprx_tanh, t0=4))
    add(SpatialGate(k, d, G, U, F + 15360))
    add(Neighbourhood(k, d, QK, V, F + 15360))
    Yo = k.at(F, KD, N)
    add(Linear(k, d["hyb_out"], 8, k.H, Yo))
    add(Norm(k, Yo, 0, 2, scratch=F + 6144))
    add(Norm(k, k.X, 0, 4, 3, k.H))
    hid = k.at(F, FT, N)
    add(ConvLinear(k, d["ffn_in0"], 2 * FT, hid, "cw0", "cb0", F + FT * N))
    add(Linear(k, d["ffn_out0"], 8, hid, k.H, kt=FT))
    add(Norm(k, k.H, 0, 5))
    add(Mods(k, 1, d["ada1"], "c0"))
    add(Norm(k, k.X, 1, 1, 0, k.H))
    O = k.at(F, 16, T)
    for half in range(2):
        q, QK, V = F + 8192, k.at(F + 8192, 8, N), k.at(F + 8192 + 6144, NTT, 1024)
        add(Linear(k, d["ret_qk"], 8, k.H, QK, t0=8 * half))
        add(Rope(k, d, QK, range(8), "rot64", "cos_r", F + 20480))
        add(TokLinear(k, d["ret_v"], 2, V, t0=8 * half))
        add(Retention(k, d, QK, V, O, 4 * half, F + 20480))
    add(GroupNorm(k, O, 8, 2, lambda t: k.vec("gn_g", t, t + 1), F + 8192, center=True))
    add(GatedLinear(k, d["ret_g"], 16, O, O, ACT.Silu, F + 8192))
    Yo = k.at(F + 8192, KD, N)
    add(Linear(k, d["ret_out"], 8, O, Yo, kt=16, spans=(LAT,)))
    add(Norm(k, Yo, 1, 2, spans=(LAT,), scratch=F + 8192 + 6144))
    add(Norm(k, k.X, 1, 4, 3, k.H, spans=(LAT,)))
    add(ConvLinear(k, d["ffn_in1"], 2 * FT, hid, "cw1", "cb1", F + FT * N, spans=(LAT,)))
    add(Linear(k, d["ffn_out1"], 8, hid, k.H, kt=FT, spans=(LAT,)))
    add(Norm(k, k.H, 1, 5, spans=(LAT,)))
    add(LoadContext(k, d))
    add(Mods(k, 2, d["ada2"], "c2"))
    add(Norm(k, k.X, 2, 1, 0, k.H))
    O, Y = k.at(F, KD, T), k.at(F + 4096, KD, T)
    Q, K, V = k.at(F + 4096, KD, T), k.at(F + 8192, KD, N), k.at(F + 14336, NTT, 1024)
    add(Linear(k, d["dif_qk"], 8, k.H, Q, spans=(LAT,)))
    add(Linear(k, d["dif_qk"], 8, k.H, K, t0=8))
    add(Rope(k, d, Q, range(8), "rot32", "cos_d", F + 20480))
    add(Rope(k, d, K, range(8), "rot32", "cos_d", F + 20480))
    add(TokLinear(k, d["dif_v"], 2, V))
    add(DiffAttention(k, Q, K, V, O, d["y_rows"], F + 20480))
    add(GroupNorm(k, O, 8, 1, lambda t: k.vec("subln"), F + 8192, after=1.0 - LAM_INIT))
    dt, A, nA, AT = k.at(F + 8192, NTT, 32), k.at(F + 8384, NTT, 32), k.at(F + 8576, NTT, 32), k.at(F + 8768, T)
    add(StepSizes(k, d["w_dt"], dt, A, nA, AT, F + 9280))
    bufs = [k.at(F + 9280 + N * j, N) for j in range(4)]
    for g in range(4):
        add(ConvLinear(k, d["xbc"], 4, bufs, "scw", "scb", F + 9280 + 4 * N, pair=False, t0=4 * g))
        add(Scan(k, g, bufs, Y, dt, nA, AT, F + 9280 + 4 * N))
    add(GatedLinear(k, d["z"], 8, Y, Y, ACT.Silu, F + 8192))
    add(GroupNorm(k, Y, 4, 2, lambda t: k.vec("ssd_norm", t, t + 1), F + 8192))
    YA, YS = k.at(F + 8192, KD, T), k.at(F + 12288, KD, T)
    add(Linear(k, d["w_ba"], 8, O, YA, spans=(LAT,)))
    add(GatedLinear(k, d["gates"], 8, YA, YA, ACT.Sigmoid, F + 16384))
    add(Linear(k, d["w_bs"], 8, Y, YS, spans=(LAT,)))
    add(GatedLinear(k, d["gates"], 8, YS, YS, ACT.Sigmoid, F + 16384, add=YA, t0=8))
    Yo = k.at(F, KD, T)
    add(Linear(k, d["w_out2"], 8, YS, Yo, spans=(LAT,)))
    add(Norm(k, Yo, 2, 2, spans=(LAT,), scratch=F + 16384))
    add(Norm(k, k.X, 2, 4, 3, k.H, spans=(LAT,)))
    m = MoeMemory(k, d["consts"][:, BCON["iota"][0]:BCON["iota"][0] + P + LTT], F)
    add(Router(k, d["w_router"], d["w_shared"], d["h_rows"], m))
    add(Experts(k, d["w_gate_up"], d["w_down"], d["h_rows"], d["y_rows"], m))
    add(Combine(k, d["y_rows"], m))
    acc = m.acc
    add(Norm(k, acc, 2, 5, spans=(LAT,), scratch=F + 4096))
    return st


def build(nc, d, out, upto=None, dump=None):
    with ExitStack() as ctx:
        k = Core(nc, ctx)
        stages = plan(k, d)
        if upto is not None:
            stages = stages[:upto]
        met = ctx.enter_context(nc.semaphore("stage_met"))
        stored = ctx.enter_context(nc.semaphore("output_stored"))
        own = ctx.enter_context(nc.semaphore("vector_own"))
        block = ctx.enter_context(nc.Block(no_gpsimd_drain=True))

        def run(eng, part):
            for n, s in enumerate(stages):
                part(s, eng)
                eng.drain().then_inc(met, 1)
                eng.wait_ge(met, 4 * (n + 1))

        @block.sync
        def _(sp):
            for s in stages:
                s.sync(sp)
            sp.wait_ge(met, 4 * len(stages))
            src = k.X[:, :, 0:T] if dump is None else dump(k)
            sp.dma_start(out, src).then_inc(stored, 16)
            sp.wait_ge(stored, 16)

        @block.tensor
        def _(pe):
            run(pe, lambda s, e: s.tensor(e))

        @block.vector
        def _(dve):
            k.dve = Chain(own)
            run(dve, lambda s, e: s.vector(e))

        @block.scalar
        def _(act):
            run(act, lambda s, e: s.scalar(e))

        @block.gpsimd
        def _(pool):
            run(pool, lambda s, e: s.gpsimd(e))



def cols(v):
    v = np.asarray(v).reshape(-1, P)
    return v.T


def tiles(w):
    K, n = w.shape
    return np.ascontiguousarray(w.reshape(K // P, P, n // P, P).transpose(2, 1, 0, 3)).reshape(n // P, P, K)


def feature_major(x):
    return np.ascontiguousarray(x.T.reshape(KD, P, -1).transpose(1, 0, 2))


def constants():
    c = np.zeros((P, NCONALL), np.float32)
    r, j = np.arange(P)[:, None], np.arange(P)[None, :]

    def put(name, v):
        o, w = (CON.get(name) or BCON.get(name))
        c[:, o:o + w] = v

    put("ident", r == j)
    put("ones", 1.0)
    put("ge", j >= r)
    put("le", j <= r)
    put("lt", r < j)
    put("gt", r > j)
    put("negf", np.where(j >= r, 0.0, NEG))
    put("negb", np.where(j <= r, 0.0, NEG))
    for name, half in (("rot64", 64), ("rot32", 32)):
        m = np.zeros((P, P), np.float32)
        for o in range(P):
            if o % (2 * half) < half:
                m[o + half, o] = -1.0
            else:
                m[o - half, o] = 1.0
        put(name, m)
    q = np.arange(P) % GRID_W
    c0 = np.clip(q - 8, 0, GRID_W - 16)
    kc = np.arange(GRID_W)
    put("namask", np.where((kc[None] >= c0[:, None]) & (kc[None] < c0[:, None] + 16), 0.0, NEG))
    put("iota", np.concatenate([np.broadcast_to(j, (P, P)), r + P * np.arange(LTT)[None, :]], 1))
    put("absd", np.abs(np.arange(1408)[None, :] - 640 - r))
    t = np.arange(T)
    row, col = (t // GRID_W).astype(np.float32), (t % GRID_W).astype(np.float32)
    for tag, nf, base, dim in (("r", 32, 10000.0, 128), ("d", 16, 10000.0, 64)):
        inv = (np.float32(base) ** (-np.arange(nf, dtype=np.float32) / np.float32(nf))).astype(np.float32)
        ang = np.concatenate([row[:, None] * inv, col[:, None] * inv], -1).astype(np.float32)
        full = np.tile(ang, (1, P // (dim // 2))).T
        put(f"cos_{tag}", np.cos(full))
        put(f"sin_{tag}", np.sin(full))
    return c


def lay_out(a):
    f = np.float32
    a = {n: np.asarray(v) for n, v in a.items()}
    rep = lambda v: np.broadcast_to(np.asarray(v).reshape(1, -1), (P, np.asarray(v).size))
    vecs = np.zeros((P, NVEC), f)

    def put(name, v):
        o, w = VEC[name]
        vecs[:, o:o + w] = v

    pair = lambda x, y: np.stack([cols(x), cols(y)], -1).reshape(P, 16)
    put("c0", pair(a["c"][0], a["c_ctx"]))
    put("c2", pair(a["c_2"][0], a["c_ctx_2"]))
    put("ada_b0", cols(a["ada_b"][0]))
    put("ada_b1", cols(a["ada_b"][1]))
    put("ada_b2", cols(a["b_ada_2"][0]))
    put("norm0", cols(a["norm_g"][0].reshape(-1)))
    put("norm1", cols(a["norm_g"][1].reshape(-1)))
    put("norm2", np.concatenate([cols(a[n + "_2"][0]) for n in ("g_pre_mix", "g_post_mix", "g_pre_ffn", "g_post_ffn")], 1))
    gu = np.arange(2 * FT).reshape(2, FT).T.reshape(-1)
    for l in range(2):
        put(f"cw{l}", np.concatenate([cols(a["ffn_conv_w"][l][t])[:, gu] for t in range(3)], 1))
        put(f"cb{l}", cols(a["ffn_conv_b"][l])[:, gu])
    put("gn_g", cols(a["ret_gn_g"][0]))
    put("subln", cols(a["g_attn_subln_2"][0]))
    put("ssd_norm", cols(a["g_ssd_norm_2"][0]))
    put("d_skip", cols(np.repeat(a["d_skip_2"][0], 64)))
    order = np.array([[8 + g, 12 + g, 2 * g, 2 * g + 1] for g in range(4)]).reshape(-1)
    put("scw", np.concatenate([cols(a["conv_w_2"][0][t])[:, order] for t in range(3)], 1))
    put("scb", cols(a["conv_b_2"][0])[:, order])
    put("lgd", rep(a["ret_log_decay"][0]))
    put("dt_bias", rep(a["dt_bias_2"][0]))
    put("a_log", rep(a["a_log_2"][0]))
    put("rbias", rep(a["router_bias_2"][0]))
    for n, name in enumerate(("lam_q1_2", "lam_k1_2", "lam_q2_2", "lam_k2_2")):
        vecs[0:64, VEC["lam"][0] + n] = a[name][0]
    put("before", rep((np.arange(8)[None, :] < np.arange(8)[:, None]).astype(f)))

    d = {"vecs": vecs, "consts": constants(), "xT": feature_major(a["x"][0]), "ctxT": feature_major(a["ctx"][0]),
         "ctx2T": feature_major(a["ctx_2"][0])}
    moving = lambda w: np.ascontiguousarray(w.reshape(4, 2, P, 12, T).transpose(3, 0, 2, 1, 4)).reshape(48, P, UC)
    d["ada0"], d["ada1"], d["ada2"] = moving(a["ada_w"][0]), moving(a["ada_w"][1]), moving(a["w_ada_2"][0])
    w = a["hyb_w_in"][0]
    d["hyb_qku"] = tiles(np.concatenate([w[:, 0:1024], w[:, 1536:2048]], 1))
    d["hyb_vg"] = tiles(np.concatenate([w[:, 1024:1536], w[:, 2048:2560]], 1))
    rpb = np.zeros((8, 15, 127), f)
    rpb[:, :, 48:79] = a["na_rpb"][0]
    col = np.arange(GRID_W)
    d["rpb"] = np.ascontiguousarray(rpb[:, :, 63 - col[:, None] + col[None, :]].transpose(0, 2, 1, 3))
    d["sgu_w"] = np.ascontiguousarray(a["sgu_w"][0].transpose(2, 0, 1))
    b = a["sgu_b"][0].reshape(4, 2, P).transpose(1, 0, 2)
    d["sgu_b"] = np.ascontiguousarray(np.repeat(b, 64, axis=0))
    d["hyb_out"] = tiles(a["hyb_w_out"][0])
    for l in range(2):
        d[f"ffn_in{l}"] = tiles(a["ffn_w_in"][l])[gu]
        d[f"ffn_out{l}"] = tiles(a["ffn_w_out"][l])
    w = a["ret_w_in"][0]
    q, kk = tiles(w[:, 0:1024]), tiles(w[:, 1024:2048])
    d["ret_qk"] = np.concatenate([q[0:4], kk[0:4], q[4:8], kk[4:8]])
    d["ret_v"], d["ret_g"] = tiles(w[:, 2048:4096]), tiles(w[:, 4096:6144])
    halves = lambda t: np.ascontiguousarray(t.reshape(t.shape[0], P, 2, UC).transpose(0, 2, 1, 3)).reshape(-1, P, UC)
    d["ret_out"] = halves(tiles(a["ret_w_out"][0]))
    w = a["w_in_2"][0]
    d["dif_qk"], d["dif_v"], d["z"] = tiles(w[:, 0:2048]), tiles(w[:, 2048:3072]), tiles(w[:, 3072:4096])
    d["xbc"] = tiles(w[:, 4096:6144])[order]
    d["w_dt"] = np.ascontiguousarray(w[:, 6144:6176].reshape(KD, P, 32).transpose(1, 0, 2)).reshape(1, P, 256)
    d["gates"] = tiles(w[:, 6176:8224])
    d["w_ba"], d["w_bs"], d["w_out2"] = (tiles(a[n + "_2"][0]) for n in ("w_branch_attn", "w_branch_ssd", "w_out"))
    d["w_router"] = np.ascontiguousarray(a["w_router_2"][0].reshape(KD, P, NE).transpose(1, 0, 2)).reshape(1, P, 512)
    d["w_gate_up"] = np.ascontiguousarray(np.concatenate([a["w_e_gate_2"][0], a["w_e_up_2"][0]], 2)
                                          .reshape(NE, KD, P, 512).transpose(0, 2, 1, 3))
    d["w_down"] = np.ascontiguousarray(a["w_e_down_2"][0].reshape(NE, 2, P, D).transpose(0, 2, 1, 3))
    gu = np.stack([tiles(a["w_sh_gate_2"][0]), tiles(a["w_sh_up_2"][0])], 1).reshape(4, P, UC)
    down = a["w_sh_down_2"][0].reshape(2, P, 2, 4, P).transpose(2, 1, 3, 0, 4).reshape(2, P, UC)
    d["w_shared"] = np.concatenate([gu, down])
    return d


def kernel(**inputs):
    import concourse.bacc as bacc
    from concourse.bass_utils import run_bass_kernel_spmd

    nc = bacc.Bacc("TRN2", target_bir_lowering=False, num_devices=1)
    d = lay_out(inputs)
    dram = {n: nc.dram_tensor(n, v.shape, F32, kind="ExternalInput").ap() for n, v in d.items()}
    for n, shape in INTERNAL.items():
        dram[n] = nc.dram_tensor(n, shape, F32, kind="Internal").ap()
    out = nc.dram_tensor("out", [P, KD, T], F32, kind="ExternalOutput").ap()
    build(nc, dram, out)
    r = run_bass_kernel_spmd(nc, [d], core_ids=[0])
    y = np.asarray(r.results[0]["out"])
    return np.ascontiguousarray(y.transpose(2, 1, 0)).reshape(1, T, D)
```
